# Optimizing a Trainium2 kernel written in Bass

```python
import jax, jax.numpy as jnp
from jax import lax
import numpy as np

D_MODEL = 1024
BATCH = 1
SEQ = 512
DEPTH = 1

D_MIX = D_MODEL
D_RET = D_MIX // 2
D_POOL = D_MIX - D_RET
RET_HEADS = 8
RET_HEAD_DIM = D_RET // RET_HEADS
RET_CHUNK = 128
ROPE_BASE = 10000.0
POOL_WINDOWS = (2, 4, 8, 16)
POOL_GROUPS = len(POOL_WINDOWS)
POOL_GROUP_DIM = D_POOL // POOL_GROUPS
D_IN_PROJ = 4 * D_RET + D_POOL
N_EXPERTS = 32
TOP_K = 4
D_EXPERT = D_MODEL
SWIGLU_LIMIT = 7.0
SWIGLU_ALPHA = 1.702
PLE_DIM = 256
NORM_EPS = 1e-5
GN_EPS = 1e-5


def rms_norm(x, g):
    xf = x.astype(jnp.float32)
    y = xf * lax.rsqrt(jnp.mean(xf * xf, axis=-1, keepdims=True) + NORM_EPS)
    return (y * g.astype(jnp.float32)).astype(x.dtype)

def rope(x, positions):
    half = x.shape[-1] // 2
    inv_freq = ROPE_BASE ** (-jnp.arange(half, dtype=jnp.float32) / half)
    ang = positions.astype(jnp.float32)[..., None] * inv_freq
    cos = jnp.cos(ang)[:, :, None, :]
    sin = jnp.sin(ang)[:, :, None, :]
    xf = x.astype(jnp.float32)
    x1, x2 = xf[..., :half], xf[..., half:]
    out = jnp.concatenate([x1 * cos - x2 * sin, x2 * cos + x1 * sin], axis=-1)
    return out.astype(x.dtype)

def retention(q, k, v, gn_w):
    B, S, H, d = q.shape
    C = RET_CHUNK
    N = S // C
    log_gamma = jnp.log1p(-jnp.power(2.0, -5.0 - jnp.arange(H, dtype=jnp.float32)))
    qc = q.reshape(B, N, C, H, d)
    kc = (k * (d ** -0.5)).reshape(B, N, C, H, d)
    vc = v.reshape(B, N, C, H, d)
    idx = jnp.arange(C, dtype=jnp.float32)
    rel = idx[:, None] - idx[None, :]
    causal = rel >= 0
    decay = jnp.where(causal[None], jnp.exp(jnp.where(causal, rel, 0.0)[None] * log_gamma[:, None, None]), 0.0)
    scores = jnp.einsum('bnchd,bnmhd->bnhcm', qc, kc) * decay
    intra = jnp.einsum('bnhcm,bnmhd->bnchd', scores, vc)
    zeta = jnp.exp((C - 1 - idx)[None, :] * log_gamma[:, None])
    kv = jnp.einsum('bnmhd,hm,bnmhe->bnhde', kc, zeta, vc)
    chunk_decay = jnp.exp(C * log_gamma)[:, None, None]

    def step(state, kv_i):
        return chunk_decay * state + kv_i, state

    init = jnp.zeros((B, H, d, d), dtype=kv.dtype)
    _, states = lax.scan(step, init, jnp.moveaxis(kv, 1, 0))
    states = jnp.moveaxis(states, 0, 1)
    xi = jnp.exp((idx + 1.0)[None, :] * log_gamma[:, None])
    cross = jnp.einsum('bnchd,bnhde,hc->bnche', qc, states, xi)
    y = (intra + cross).reshape(B, S, H, d).astype(jnp.float32)
    mu = jnp.mean(y, axis=-1, keepdims=True)
    var = jnp.mean(jnp.square(y - mu), axis=-1, keepdims=True)
    y = (y - mu) * lax.rsqrt(var + GN_EPS)
    y = y.reshape(B, S, H * d) * gn_w.astype(jnp.float32)
    return y.astype(q.dtype)

def pool_mixer(u, w_pool, pool_scale):
    B, S, _ = u.shape
    ug = u.reshape(B, S, POOL_GROUPS, POOL_GROUP_DIM).astype(jnp.float32)
    P = jnp.pad(jnp.cumsum(ug, axis=1), ((0, 0), (1, 0), (0, 0), (0, 0)))
    t = jnp.arange(S, dtype=jnp.float32)
    outs = []
    for gi, w in enumerate(POOL_WINDOWS):
        Pg = P[:, :, gi]
        lag = jnp.pad(Pg, ((0, 0), (w, 0), (0, 0)))[:, :S + 1]
        window_sum = Pg[:, 1:] - lag[:, 1:]
        count = jnp.minimum(t + 1.0, float(w))
        outs.append(window_sum / count[None, :, None] - ug[:, :, gi])
    pooled = jnp.stack(outs, axis=2).astype(u.dtype)
    mixed = jnp.einsum('bsgc,gcd->bsgd', pooled, w_pool)
    return mixed.reshape(B, S, D_POOL) * pool_scale

def moe(hn, router_w, router_b, w_gu, b_gu, w_down, b_down):
    B, S, D = hn.shape
    xt = hn.reshape(-1, D)
    logits = xt.astype(jnp.float32) @ router_w.astype(jnp.float32) + router_b.astype(jnp.float32)
    top_vals, top_idx = lax.top_k(logits, TOP_K)
    gates = jax.nn.softmax(top_vals, axis=-1)
    flat_e = top_idx.reshape(-1)
    order = jnp.argsort(flat_e)
    sorted_e = flat_e[order]
    tok = order // TOP_K
    xs = xt[tok]
    group_sizes = jnp.bincount(flat_e, length=N_EXPERTS).astype(jnp.int32)
    gu = lax.ragged_dot(xs, w_gu, group_sizes) + b_gu[sorted_e]
    gate = jnp.minimum(gu[:, ::2], SWIGLU_LIMIT)
    up = jnp.clip(gu[:, 1::2], -SWIGLU_LIMIT, SWIGLU_LIMIT)
    act = (up + 1.0) * (gate * jax.nn.sigmoid(SWIGLU_ALPHA * gate))
    y = lax.ragged_dot(act.astype(w_down.dtype), w_down, group_sizes) + b_down[sorted_e]
    y = y * gates.reshape(-1)[order][:, None].astype(y.dtype)
    out = jnp.zeros_like(xt).at[tok].add(y.astype(xt.dtype))
    return out.reshape(B, S, D)

def first_inputs(seed: int = 0) -> dict:
    key = jax.random.key(seed)
    ks = jax.random.split(key, 24)
    f32 = jnp.float32
    L = DEPTH

    def nrm(k, shape, scale):
        return jax.random.normal(k, shape, dtype=f32) * scale

    offsets = jax.random.randint(ks[2], (BATCH, 1), 0, 1024, dtype=jnp.int32)
    positions = (jnp.arange(SEQ, dtype=jnp.int32)[None, :] + offsets).astype(jnp.int32)
    return {
        "x": nrm(ks[0], (BATCH, SEQ, D_MODEL), 1.0),
        "p": nrm(ks[1], (DEPTH, BATCH, SEQ, PLE_DIM), 1.0),
        "positions": positions,
        "w_in": nrm(ks[3], (L, D_MODEL, D_IN_PROJ), D_MODEL ** -0.5),
        "w_out": nrm(ks[4], (L, D_MIX, D_MODEL), D_MIX ** -0.5),
        "ret_gn_w": 1.0 + nrm(ks[5], (L, D_RET), 0.02),
        "pool_w": nrm(ks[6], (L, POOL_GROUPS, POOL_GROUP_DIM, POOL_GROUP_DIM), POOL_GROUP_DIM ** -0.5),
        "pool_scale": 1.0 + nrm(ks[7], (L, D_POOL), 0.02),
        "norm_mix_w": 1.0 + nrm(ks[8], (L, D_MODEL), 0.02),
        "norm_moe_w": 1.0 + nrm(ks[9], (L, D_MODEL), 0.02),
        "router_w": nrm(ks[10], (L, D_MODEL, N_EXPERTS), D_MODEL ** -0.5),
        "router_b": nrm(ks[11], (L, N_EXPERTS), 0.01),
        "expert_w_gate_up": nrm(ks[12], (L, N_EXPERTS, D_MODEL, 2 * D_EXPERT), D_MODEL ** -0.5),
        "expert_b_gate_up": nrm(ks[13], (L, N_EXPERTS, 2 * D_EXPERT), 0.02),
        "expert_w_down": nrm(ks[14], (L, N_EXPERTS, D_EXPERT, D_MODEL), D_EXPERT ** -0.5),
        "expert_b_down": nrm(ks[15], (L, N_EXPERTS, D_MODEL), 0.02),
        "norm_ple_w": 1.0 + nrm(ks[16], (L, D_MODEL), 0.02),
        "ple_gate_w": nrm(ks[17], (L, D_MODEL, D_MODEL), D_MODEL ** -0.5),
        "ple_proj_w": nrm(ks[18], (L, PLE_DIM, D_MODEL), PLE_DIM ** -0.5),
        "final_norm_w": 1.0 + nrm(ks[19], (D_MODEL,), 0.02),
    }

def first_block(x, p, positions, w_in, w_out, ret_gn_w, pool_w, pool_scale, norm_mix_w,
              norm_moe_w, router_w, router_b, expert_w_gate_up, expert_b_gate_up,
              expert_w_down, expert_b_down, norm_ple_w, ple_gate_w, ple_proj_w, final_norm_w):
    B, S, _ = x.shape
    h = x
    for l in range(DEPTH):
        hn = rms_norm(h, norm_mix_w[l])
        proj = hn @ w_in[l]
        q = proj[..., 0 * D_RET:1 * D_RET].reshape(B, S, RET_HEADS, RET_HEAD_DIM)
        k = proj[..., 1 * D_RET:2 * D_RET].reshape(B, S, RET_HEADS, RET_HEAD_DIM)
        v = proj[..., 2 * D_RET:3 * D_RET].reshape(B, S, RET_HEADS, RET_HEAD_DIM)
        g = proj[..., 3 * D_RET:4 * D_RET]
        u = proj[..., 4 * D_RET:]
        q = rope(q, positions)
        k = rope(k, positions)
        ret = jax.nn.silu(g) * retention(q, k, v, ret_gn_w[l])
        pool = pool_mixer(u, pool_w[l], pool_scale[l])
        h = h + jnp.concatenate([ret, pool], axis=-1) @ w_out[l]
        h = h + moe(rms_norm(h, norm_moe_w[l]), router_w[l], router_b[l],
                    expert_w_gate_up[l], expert_b_gate_up[l], expert_w_down[l], expert_b_down[l])
        gate = jax.nn.sigmoid(rms_norm(h, norm_ple_w[l]) @ ple_gate_w[l])
        h = h + gate * (p[l] @ ple_proj_w[l])
    return rms_norm(h, final_norm_w)


CHUNK = 64
ROPE_THETA = 10000.0
RMS_EPS = 1e-6
NEG_INF = -1e30

A_HEADS = 8
A_HEAD_DIM = 64
A_WIDTH = A_HEADS * A_HEAD_DIM
IDX_HEADS = 8
IDX_DIM = 64
IDX_ROPE_DIM = 32
TOPK_MAX = 256
SPARSE_Q_BLOCK = 32

B_HEADS = 8
B_NOPE_DIM = 64
B_ROPE_DIM = 32
B_QK_DIM = B_NOPE_DIM + B_ROPE_DIM
B_V_DIM = 64
B_WIDTH = B_HEADS * B_V_DIM
Q_LORA = 384
KV_LORA = 256
DENSE_Q_BLOCK = 128

D_MIX_2 = A_WIDTH + B_WIDTH
IN_SPLITS = (A_WIDTH, A_WIDTH, A_WIDTH, A_WIDTH, IDX_HEADS * IDX_DIM, IDX_DIM, IDX_HEADS,
             Q_LORA, KV_LORA, B_ROPE_DIM, B_WIDTH)
D_IN = 4 * A_WIDTH + IDX_HEADS * IDX_DIM + IDX_DIM + IDX_HEADS + Q_LORA + KV_LORA + B_ROPE_DIM + B_WIDTH


def rms_norm_2(x, g):
    xf = x.astype(jnp.float32)
    y = xf * lax.rsqrt(jnp.mean(xf * xf, axis=-1, keepdims=True) + RMS_EPS)
    return (y * g.astype(jnp.float32)).astype(x.dtype)

def rope_2(x, pos):
    d = x.shape[-1]
    half = d // 2
    freqs = jnp.power(ROPE_THETA, -jnp.arange(half, dtype=jnp.float32) * 2.0 / d)
    ang = pos.astype(jnp.float32)[:, None] * freqs[None, :]
    cos = jnp.cos(ang)[None, :, None, :]
    sin = jnp.sin(ang)[None, :, None, :]
    xf = x.astype(jnp.float32)
    x1, x2 = xf[..., :half], xf[..., half:]
    return jnp.concatenate([x1 * cos - x2 * sin, x2 * cos + x1 * sin], axis=-1).astype(x.dtype)

def chunk_limit(pos):
    return (pos // CHUNK + 1) * CHUNK

def indexer_sparse_attention(q, k, v, q_idx, k_idx, w_idx, pos):
    B, S, H, dh = q.shape
    topk = min(TOPK_MAX, S // 4)
    nblk = S // SPARSE_Q_BLOCK
    key_pos = jnp.arange(S, dtype=jnp.int32)
    idx_scale = (IDX_DIM * IDX_HEADS) ** -0.5
    att_scale = dh ** -0.5

    def to_blocks(a):
        return jnp.moveaxis(a.reshape(B, nblk, SPARSE_Q_BLOCK, *a.shape[2:]), 1, 0)

    def block(args):
        qb, qib, wb, pb = args
        limit = chunk_limit(pb)
        rel = jax.nn.relu(jnp.einsum('bqhd,bsd->bqhs', qib, k_idx).astype(jnp.float32))
        score = jnp.einsum('bqhs,bqh->bqs', rel, wb.astype(jnp.float32)) * idx_scale
        admissible = key_pos[None, :] < limit[:, None]
        score = jnp.where(admissible[None], score, NEG_INF)
        _, sel = lax.top_k(score, topk)
        valid = sel < limit[None, :, None]
        k_sel = jax.vmap(lambda kb, ib: kb[ib])(k, sel)
        v_sel = jax.vmap(lambda vb, ib: vb[ib])(v, sel)
        logits = jnp.einsum('bqhd,bqkhd->bhqk', qb, k_sel).astype(jnp.float32) * att_scale
        logits = jnp.where(valid[:, None], logits, NEG_INF)
        p = jax.nn.softmax(logits, axis=-1).astype(v.dtype)
        return jnp.einsum('bhqk,bqkhd->bqhd', p, v_sel)

    out = lax.map(block, (to_blocks(q), to_blocks(q_idx), to_blocks(w_idx),
                          pos.reshape(nblk, SPARSE_Q_BLOCK)))
    return jnp.moveaxis(out, 0, 1).reshape(B, S, H, dh)

def chunk_causal_attention(q, k, v, pos):
    B, S, H, dq = q.shape
    dv = v.shape[-1]
    nblk = S // DENSE_Q_BLOCK
    scale = dq ** -0.5

    def block(args):
        qb, pb = args
        logits = jnp.einsum('bqhd,bshd->bhqs', qb, k).astype(jnp.float32) * scale
        mask = pos[None, :] < chunk_limit(pb)[:, None]
        logits = jnp.where(mask[None, None], logits, NEG_INF)
        p = jax.nn.softmax(logits, axis=-1).astype(v.dtype)
        return jnp.einsum('bhqs,bshd->bqhd', p, v)

    qbl = jnp.moveaxis(q.reshape(B, nblk, DENSE_Q_BLOCK, H, dq), 1, 0)
    out = lax.map(block, (qbl, pos.reshape(nblk, DENSE_Q_BLOCK)))
    return jnp.moveaxis(out, 0, 1).reshape(B, S, H, dv)

def second_inputs(seed: int = 0) -> dict:
    key = jax.random.key(seed)
    ks = jax.random.split(key, 12)
    f32 = jnp.float32

    def gain(k, n):
        return 1.0 + 0.02 * jax.random.normal(k, (DEPTH, n), f32)

    x = jax.random.normal(ks[0], (BATCH, SEQ, D_MODEL), f32)
    norm_gain = gain(ks[1], D_MODEL)
    w_in = jax.random.normal(ks[2], (DEPTH, D_MODEL, D_IN), f32) * D_MODEL ** -0.5
    a_q_norm = gain(ks[3], A_HEAD_DIM)
    a_k_norm = gain(ks[4], A_HEAD_DIM)
    b_q_latent_norm = gain(ks[5], Q_LORA)
    b_kv_latent_norm = gain(ks[6], KV_LORA)
    w_uq = jax.random.normal(ks[7], (DEPTH, Q_LORA, B_HEADS * B_QK_DIM), f32) * Q_LORA ** -0.5
    w_ukv = jax.random.normal(ks[8], (DEPTH, KV_LORA, B_HEADS * (B_NOPE_DIM + B_V_DIM)), f32) * KV_LORA ** -0.5
    b_q_norm = gain(ks[9], B_QK_DIM)
    b_k_norm = gain(ks[10], B_QK_DIM)
    w_out = jax.random.normal(ks[11], (DEPTH, D_MIX_2, D_MODEL), f32) * D_MIX_2 ** -0.5
    return {"x": x, "norm_gain": norm_gain, "w_in": w_in, "a_q_norm": a_q_norm,
            "a_k_norm": a_k_norm, "b_q_latent_norm": b_q_latent_norm,
            "b_kv_latent_norm": b_kv_latent_norm, "w_uq": w_uq, "w_ukv": w_ukv,
            "b_q_norm": b_q_norm, "b_k_norm": b_k_norm, "w_out": w_out}

def second_block(x, norm_gain, w_in, a_q_norm, a_k_norm, b_q_latent_norm, b_kv_latent_norm,
              w_uq, w_ukv, b_q_norm, b_k_norm, w_out):
    B, S, _ = x.shape
    pos = jnp.arange(S, dtype=jnp.int32)
    offsets = [int(o) for o in np.cumsum(IN_SPLITS)[:-1]]
    h = x
    for l in range(DEPTH):
        xn = rms_norm_2(h, norm_gain[l])
        proj = xn @ w_in[l]
        (q_a, k_a, v_a, g_a, q_i, k_i, w_i,
         c_q, c_kv, k_rope, g_b) = jnp.split(proj, offsets, axis=-1)

        q_a = rope_2(rms_norm_2(q_a.reshape(B, S, A_HEADS, A_HEAD_DIM), a_q_norm[l]), pos)
        k_a = rope_2(rms_norm_2(k_a.reshape(B, S, A_HEADS, A_HEAD_DIM), a_k_norm[l]), pos)
        v_a = v_a.reshape(B, S, A_HEADS, A_HEAD_DIM)
        q_i = q_i.reshape(B, S, IDX_HEADS, IDX_DIM)
        q_i = jnp.concatenate([rope_2(q_i[..., :IDX_ROPE_DIM], pos), q_i[..., IDX_ROPE_DIM:]], axis=-1)
        k_i = k_i[:, :, None, :]
        k_i = jnp.concatenate([rope_2(k_i[..., :IDX_ROPE_DIM], pos), k_i[..., IDX_ROPE_DIM:]], axis=-1)[:, :, 0, :]
        o_a = indexer_sparse_attention(q_a, k_a, v_a, q_i, k_i, w_i, pos)

        q_b = (rms_norm_2(c_q, b_q_latent_norm[l]) @ w_uq[l]).reshape(B, S, B_HEADS, B_QK_DIM)
        kv = (rms_norm_2(c_kv, b_kv_latent_norm[l]) @ w_ukv[l]).reshape(B, S, B_HEADS, B_NOPE_DIM + B_V_DIM)
        k_nope, v_b = kv[..., :B_NOPE_DIM], kv[..., B_NOPE_DIM:]
        k_rope_h = jnp.broadcast_to(k_rope[:, :, None, :], (B, S, B_HEADS, B_ROPE_DIM))
        k_b = jnp.concatenate([k_nope, k_rope_h], axis=-1)
        q_b = rms_norm_2(q_b, b_q_norm[l])
        k_b = rms_norm_2(k_b, b_k_norm[l])
        q_b = jnp.concatenate([q_b[..., :B_NOPE_DIM], rope_2(q_b[..., B_NOPE_DIM:], pos)], axis=-1)
        k_b = jnp.concatenate([k_b[..., :B_NOPE_DIM], rope_2(k_b[..., B_NOPE_DIM:], pos)], axis=-1)
        o_b = chunk_causal_attention(q_b, k_b, v_b, pos)

        mixed = jnp.concatenate([o_a.reshape(B, S, A_WIDTH) * jax.nn.silu(g_a),
                                 o_b.reshape(B, S, B_WIDTH) * jax.nn.silu(g_b)], axis=-1)
        h = h + mixed @ w_out[l]
    return h


def setup_inputs(seed=0):
    out = dict(first_inputs(seed))
    for name, value in second_inputs(seed + 1).items():
        if name != "x":
            out[name + "_2"] = value
    return out


def reference(
    x, p, positions, w_in, w_out, ret_gn_w, pool_w, pool_scale, norm_mix_w, norm_moe_w,
    router_w, router_b, expert_w_gate_up, expert_b_gate_up, expert_w_down, expert_b_down,
    norm_ple_w, ple_gate_w, ple_proj_w, final_norm_w, norm_gain_2, w_in_2, a_q_norm_2,
    a_k_norm_2, b_q_latent_norm_2, b_kv_latent_norm_2, w_uq_2, w_ukv_2, b_q_norm_2, b_k_norm_2,
    w_out_2,
):
    x = first_block(
        x, p, positions, w_in, w_out, ret_gn_w, pool_w, pool_scale, norm_mix_w, norm_moe_w,
        router_w, router_b, expert_w_gate_up, expert_b_gate_up, expert_w_down, expert_b_down,
        norm_ple_w, ple_gate_w, ple_proj_w, final_norm_w,
    )
    return second_block(
        x, norm_gain_2, w_in_2, a_q_norm_2, a_k_norm_2, b_q_latent_norm_2, b_kv_latent_norm_2,
        w_uq_2, w_ukv_2, b_q_norm_2, b_k_norm_2, w_out_2,
    )


_drawn_inputs = setup_inputs


def setup_inputs(seed=0):
    import zlib

    import numpy as np

    out = dict(_drawn_inputs(seed))
    spreads = {}
    factors = {'expert_b_gate_up': 5.548,
     'expert_b_down': 6.203,
     'norm_ple_w': 8.0,
     'norm_gain_2': 6.672,
     'a_q_norm_2': 8.0,
     'a_k_norm_2': 8.0,
     'b_q_latent_norm_2': 8.0,
     'b_kv_latent_norm_2': 8.0,
     'b_q_norm_2': 8.0,
     'b_k_norm_2': 8.0}
    for name, (base, spread) in spreads.items():
        noise = np.random.default_rng([zlib.crc32(name.encode()), seed]).standard_normal(out[name].shape)
        drawn = base * np.exp(spread * noise) if base else spread * noise
        out[name] = __import__('jax').numpy.asarray(drawn.astype(out[name].dtype))
    for name, factor in factors.items():
        out[name] = (out[name] * factor).astype(out[name].dtype)
    return out
```

```python
from contextlib import ExitStack

import numpy as np

import concourse.bass as bass
from concourse import mybir

F32 = mybir.dt.float32
BF16 = mybir.dt.bfloat16
I32 = mybir.dt.int32
U32 = mybir.dt.uint32
ALU = mybir.AluOpType
ACT = mybir.ActivationFunctionType
X = mybir.AxisListType.X
ds = bass.ds

P = 128
S, D = 512, 1024
NT = S // P
KD = D // P
HEADS, DH = 8, 64
D_RET = HEADS * DH
WINDOWS = (2, 4, 8, 16)
PAD = max(WINDOWS)
E, TOPK = 32, 4
D_E = 1024
LIMIT, ALPHA = 7.0, 1.702
PLE = 256
NITEM = 48
EPS1, EPS2 = 1e-5, 1e-6
NEG = -1e30
TAKEN = -3e38
KEEP = 128
Q_LORA, KV_LORA = 384, 256
DQ_B, D_ROPE_B = 96, 32
HALF_A, HALF_I = DH // 2, 16
C_QA, C_KA, C_VA, C_GA, C_QI = 0, 512, 1024, 1536, 2048
C_KI, C_WI, C_CQ, C_CKV, C_KR, C_GB = 2560, 2624, 2632, 3016, 3272, 3304
D_IN2 = 3816
NCH2 = -(-D_IN2 // 512)
TWO_PI = 2 * np.pi
PI_A = 6.28125
PI_B = float(np.float32(np.floor((TWO_PI - PI_A) * 2 ** 21) / 2 ** 21))
PI_C = float(np.float32(TWO_PI - PI_A - PI_B))
ROUND = 12582912.0


class Cols:

    def __init__(self, **widths):
        self.at, self.n = {}, 0
        for name, w in widths.items():
            self.at[name] = (self.n, self.n + w)
            self.n += w


CONST = Cols(ident=P, causal=S, ustrict=P, ones=P, chunkbias=S, cos_a=NT * HALF_A, sin_a=NT * HALF_A,
             cos_i=NT * HALF_I, sin_i=NT * HALF_I, gq=NT * HEADS, gk=NT * HEADS, invw=4 * PAD,
             invfreq=HALF_A, iota32=E, iota48=NITEM, pmod=1, tok=NT)
SMALL = Cols(g_mix=KD, gn_w=4, pool_scale=4, g_ple=KD, gain2=KD, bq_lat=3, bkv_lat=2, router_b=E,
             aq=DH, ak=DH, bq=DQ_B, bk=DQ_B)


def shape_constants():
    c = {}
    p = np.arange(P)
    tok = np.arange(NT)[None, :] * P + p[:, None]
    c["ident"] = np.eye(P)
    c["causal"] = np.concatenate([(p[None, :] >= p[:, None]), np.ones((P, S - P))], 1)
    c["ustrict"] = p[:, None] < p[None, :]
    c["ones"] = np.ones((P, P))
    last = np.where((p[:, None] < 64) & (p[None, :] >= 64), NEG, 0.0)
    c["chunkbias"] = np.concatenate([np.zeros((P, S - P)), last], 1)
    f32 = np.float32
    for name, half in (("a", HALF_A), ("i", HALF_I)):
        freq = np.power(f32(10000.0), -np.arange(half, dtype=f32) * f32(2.0) / f32(2 * half)).astype(f32)
        ang = (tok[:, :, None].astype(f32) * freq[None, None, :]).astype(f32).astype(np.float64)
        c["cos_" + name], c["sin_" + name] = np.cos(ang), np.sin(ang)
    lg = np.log1p(-np.power(2.0, -5.0 - np.arange(HEADS)))
    c["gq"] = np.exp(tok[:, :, None] * lg)
    c["gk"] = np.exp(-tok[:, :, None] * lg) * DH ** -0.5
    c["invw"] = np.broadcast_to(np.stack([1.0 / np.minimum(np.arange(PAD) + 1.0, w) for w in WINDOWS])[None],
                                (P, 4, PAD))
    c["invfreq"] = np.broadcast_to(np.power(f32(10000.0), -np.arange(HALF_A, dtype=f32) / f32(HALF_A))[None],
                                   (P, HALF_A))
    c["iota32"] = np.broadcast_to(np.arange(E)[None], (P, E))
    c["iota48"] = np.broadcast_to(np.arange(NITEM)[None], (P, NITEM))
    c["pmod"] = (p % E)[:, None]
    c["tok"] = tok
    return np.concatenate([np.asarray(c[k], np.float64).reshape(P, -1) for k in CONST.at], 1).astype(np.float32)


def build_program(nc, d):
    ctx = ExitStack()
    with ctx:
        def sb(name, shape, dt=F32):
            return ctx.enter_context(nc.sbuf_tensor("sb_" + name, shape, dt))

        def sem(name):
            return ctx.enter_context(nc.semaphore(name))

        def dram(name, shape, dt=F32):
            return nc.dram_tensor("scratch_" + name, shape, dt, kind="Internal").ap()

        ring = sb("ring", [P, 12 * 2048])
        wbuf = sb("wbuf", [P, 2, KD * 512])
        h = sb("h", [P, NT, D])
        xcols = sb("xcols", [P, KD * S])
        xrows = sb("xrows", [P, NT * D])
        scr = sb("scr", [P, 3072])
        cst = sb("cst", [P, CONST.n])
        sml = sb("sml", [P, SMALL.n])
        grow = sb("grow", [P, D])
        rw = sb("rw", [P, KD, E])
        st = sb("st", [P, 512])
        bank = [ctx.enter_context(nc.psum_tensor(f"bank{i}", [P, 512], F32)) for i in range(8)]

        C = {k: cst[:, a:b] for k, (a, b) in CONST.at.items()}
        M = {k: sml[:, a:b] for k, (a, b) in SMALL.at.items()}
        ident = C["ident"]
        xc = xcols[:, :].rearrange("p (k s) -> p k s", k=KD)
        xr = xrows[:, :].rearrange("p (t n) -> p t n", t=NT)

        taken = [0]

        def stat(n, dt=F32):
            a = taken[0]
            taken[0] += n
            assert taken[0] <= 512
            v = st[:, a:a + n]
            return v if dt == F32 else v.bitcast(dt)

        sumsq = stat(NT)
        rstd = stat(NT)
        posf = stat(NT)
        posi = stat(NT, I32)
        mu = stat(HEADS * NT)
        var = stat(HEADS * NT)
        gates = stat(16)
        gsum = stat(NT)
        negv0 = stat(NT)
        slot_u = stat(16, U32)
        place_u = stat(16, U32)
        tok_i = stat(NT, I32)
        item_e = stat(NITEM)
        item_ei = stat(NITEM, I32)
        n_items = stat(1, I32)
        idx_cur = stat(1, I32)
        idx_all = stat(NITEM, I32)
        nmax = stat(4)
        rs_all = stat(16)
        minus_half = stat(HEADS * NT)
        wi_s = stat(NT * HEADS)
        top8 = stat(NT * 8)
        idx8 = stat(NT * 8, U32)

        proj = ring[:, 0:8192].rearrange("p (t n) -> p t n", t=NT)
        tmp4 = ring[:, 8192:12288].rearrange("p (b n) -> p b n", b=4)
        qkT = ring[:, 12288:16384].rearrange("p (w a s) -> p w a s", w=2, a=4)
        scT = ring[:, 16384:20480].rearrange("p (b j s) -> p b j s", b=2, j=NT)
        uT = ring[:, 20480:22592].rearrange("p (g s) -> p g s", g=4)
        win = [ring[:, 22592 + i * 528:22592 + (i + 1) * 528] for i in range(2)]
        poolw = ring[:, 23648:24160].rearrange("p (g n) -> p g n", g=4)
        cos1 = scr[:, 0:128].rearrange("p (t f) -> p t f", t=NT)
        sin1 = scr[:, 128:256].rearrange("p (t f) -> p t f", t=NT)
        ang = scr[:, 256:384]
        turns = scr[:, 384:512]
        ctmp = scr[:, 512:640]
        yzero = scr[:, 1024:1024 + D]

        onehot = scr[:, 0:512].rearrange("p (a e) -> p a e", e=E)
        prod = scr[:, 512:1024].rearrange("p (a e) -> p a e", e=E)
        cmp48 = scr[:, 1024:1024 + NITEM * E].rearrange("p (i e) -> p i e", e=E)
        route = scr[:, 2560:3072]
        logits = route[:, 0:128].rearrange("p (t e) -> p t e", e=E)
        member = route[:, 128:256].rearrange("p (t e) -> p t e", e=E)
        gdense = route[:, 256:384].rearrange("p (t e) -> p t e", e=E)
        nblk, incl, base = route[:, 384:416], route[:, 416:448], route[:, 448:480]
        more = route[:, 480:512]
        gT = xrows[0:E, 0:S]
        bdown = wbuf[0:E, 0, 3072:4096]
        braw = wbuf[0:E, 0, 0:2048]
        bparts = wbuf[0:96, 0, 2048:3072].bitcast(BF16)
        bpart2 = scr[0:E, 0:1024].bitcast(BF16)
        bpart3 = scr[0:E, 1024:2048].bitcast(BF16)
        gu_w = [ring[:, c * 2048:(c + 1) * 2048] for c in range(8)]
        dn_w = [ring[:, 16384 + c * 2048:16384 + (c + 1) * 2048].rearrange("p (j n) -> p j n", j=2) for c in range(4)]
        xg, gate_s, up_s, sig_s = (xrows[:, i * 1024:(i + 1) * 1024] for i in range(4))
        xgT, act_s, actT, y_s = (xcols[:, i * 1024:(i + 1) * 1024] for i in range(4))
        xgT, actT = (a.rearrange("p (k n) -> p k n", k=KD) for a in (xgT, actT))
        sel_e = scr[0:96, 2048:2112].bitcast(BF16)

        ygat = ring[:, 0:16384].rearrange("p (a n) -> p a n", a=16)
        p_rows = ring[:, 16384:17408].rearrange("p (t n) -> p t n", t=NT)
        p_cols = ring[:, 17408:18432].rearrange("p (k s) -> p k s", k=2)
        plew = ring[:, 18432:20480].rearrange("p (k n) -> p k n", k=2)
        sig2 = ring[:, 20480:24576].rearrange("p (b n) -> p b n", b=8)

        pr2 = ring[:, 0:NT * D_IN2].rearrange("p (t n) -> p t n", t=NT)
        o2 = NT * D_IN2
        qkaT = ring[:, o2:o2 + 4096].rearrange("p (w a s) -> p w a s", w=2, a=4)
        qiT = ring[:, o2 + 4096:o2 + 6144].rearrange("p (a s) -> p a s", a=4)
        kiT = ring[:, o2 + 6144:o2 + 6656]
        selbias = ring[:, o2 + 6656:o2 + 8704].rearrange("p (t s) -> p t s", t=NT)
        ki2 = ring[:, o2 + 8704:o2 + 8704 + 512].rearrange("p (t n) -> p t n", t=NT)
        rot = xrows[:, :].rearrange("p (b n) -> p b n", b=4)
        lat_cols = xcols[:, 0:5 * S].rearrange("p (k s) -> p k s", k=5)
        qrow = xcols[:, 5 * S:5 * S + 768]
        krow = xcols[:, 5 * S + 768:5 * S + 1536]
        kbT = xrows[:, :].rearrange("p (a s) -> p a s", a=HEADS)
        sS = [scr[:, i * 512:(i + 1) * 512] for i in range(2)]
        sP = [scr[:, 1024 + i * 512:1024 + (i + 1) * 512] for i in range(2)]
        sPT = [scr[:, 2048 + i * 512:2048 + (i + 1) * 512].rearrange("p (j n) -> p j n", j=NT) for i in range(2)]

        def qbT(hd):
            return pr2[:, hd, C_KA:C_KA + S] if hd < 4 else qiT[:, hd - 4, :]

        xn_dram = dram("rows", [S, D])
        place_dram = dram("place", [P * NITEM, 1], I32)
        y_dram = dram("y", [NITEM * P, D])

        yzero_st = sem("yzero_st")
        sums_rdy = sem("sums_rdy")
        rstd_rdy = sem("rstd_rdy")
        cst_ld = sem("cst_ld")
        x_ld = sem("x_ld")
        small_ld = sem("small_ld")
        poolw_ld = sem("poolw_ld")
        trig_in = sem("trig_in")
        trig_out = sem("trig_out")
        silu_sig = sem("silu_sig")
        proj_done = sem("proj_done")
        proj_ev = sem("proj_ev")
        gate_ev = sem("gate_ev")
        rope_done = sem("rope_done")
        qkT_done = sem("qkT_done")
        qkT_ev = sem("qkT_ev")
        pad_zero = sem("pad_zero")
        pooled = sem("pooled")
        mixg_done = sem("mixg_done")
        mixg_ev = sem("mixg_ev")
        sc_done = sem("sc_done")
        sc_ev = sem("sc_ev")
        y1_done = sem("y1_done")
        ret_rows = sem("ret_rows")
        retT_done = sem("retT_done")
        wo_done = sem("wo_done")
        wo_ev = sem("wo_ev")
        rows_st = sem("rows_st")
        lg_done = sem("lg_done")
        gexp_in = sem("gexp_in")
        gexp = sem("gexp")
        member_rdy = sem("member_rdy")
        gd_rdy = sem("gd_rdy")
        rank_done = sem("rank_done")
        gT_done = sem("gT_done")
        gT_ev = sem("gT_ev")
        bd_ld = sem("bd_ld")
        bd_done = sem("bd_done")
        bd_ev = sem("bd_ev")
        braw_ld = sem("braw_ld")
        bsplit = sem("bsplit")
        bp_ld = sem("bp_ld")
        place_rdy = sem("place_rdy")
        place_zero = sem("place_zero")
        zero_st = sem("zero_st")
        place_st = sem("place_st")
        idx_ld = sem("idx_ld")
        item_rdy = sem("item_rdy")
        gu_used = sem("gu_used")
        dn_used = sem("dn_used")
        xg_ld = sem("xg_ld")
        xgT_done = sem("xgT_done")
        xgT_ev = sem("xgT_ev")
        gu_done = sem("gu_done")
        gu_ev = sem("gu_ev")
        g_rdy = sem("g_rdy")
        sig_rdy = sem("sig_rdy")
        act_rdy = sem("act_rdy")
        actT_done = sem("actT_done")
        actT_ev = sem("actT_ev")
        y_free = sem("y_free")
        y_st = sem("y_st")
        sel_rdy = sem("sel_rdy")
        combined = sem("combined")
        p_ld = sem("p_ld")
        plew_ld = sem("plew_ld")
        pT_done = sem("pT_done")
        pT_ev = sem("pT_ev")
        plg_done = sem("plg_done")
        plp_done = sem("plp_done")
        plg_sig = sem("plg_sig")
        ple_ev = sem("ple_ev")
        final_rdy = sem("final_rdy")
        pr2_done = sem("pr2_done")
        qa_rdy = sem("qa_rdy")
        qkaT_done = sem("qkaT_done")
        ix_done = sem("ix_done")
        ix_relu = sem("ix_relu")
        ix_acc = sem("ix_acc")
        lat_rdy = sem("lat_rdy")
        latT_done = sem("latT_done")
        qb_done = sem("qb_done")
        qb_ev = sem("qb_ev")
        kv_done = sem("kv_done")
        k_ev = sem("k_ev")
        qb_rdy = sem("qb_rdy")
        qbT_done = sem("qbT_done")
        at_done = sem("at_done")
        at_s = sem("at_s")
        at_exp = sem("at_exp")
        pT2_done = sem("pT2_done")
        pT2_ev = sem("pT2_ev")
        pv_done = sem("pv_done")
        o_ev = sem("o_ev")
        gsig2 = sem("gsig2")
        mixed = sem("mixed")
        mxT_done = sem("mxT_done")
        out_done = sem("out_done")
        out_rdy = sem("out_rdy")
        out_st = sem("out_st")
        grow_ld = sem("grow_ld")
        grow2_ld = sem("grow2_ld")
        rw_ld = sem("rw_ld")
        norm_sq = sem("norm_sq")
        norm_rows = sem("norm_rows")
        norm_T = sem("norm_T")
        w_ld = [sem(f"w_ld{i}") for i in range(2)]
        retT_ev = [sem(f"retT_ev{i}") for i in range(2)]
        pr2_ev = [sem(f"pr2_ev{i}") for i in range(2)]
        qkaT_ev = [sem(f"qkaT_ev{i}") for i in range(2)]
        lat_ev = [sem(f"lat_ev{i}") for i in range(2)]
        qbT_ev = [sem(f"qbT_ev{i}") for i in range(2)]
        mxT_ev = [sem(f"mxT_ev{i}") for i in range(2)]
        yg_ld = [sem(f"yg_ld{i}") for i in range(4)]
        gu_ld = [sem(f"gu_ld{i}") for i in range(8)]
        dn_ld = [sem(f"dn_ld{i}") for i in range(4)]
        norm_cols = [sem(f"norm_cols{i}") for i in range(2)]
        NORM = {"mix": 0, "moe": 1, "ple": 2, "two": 3}
        SQ = {"mix": 0, "moe": 1, "ple": 2, "fin": 3, "two": 4}

        block = ctx.enter_context(nc.Block())

        def in_cols(ap, n, w=512):
            return ap[:, n * 512:n * 512 + w].rearrange("(k p) n -> p k n", p=P)

        IN_ORDER = (0, 1, 4, 2, 3)
        chunks = [(in_cols(d["w_in"], n), 8, 512) for n in IN_ORDER]
        chunks += [(in_cols(d["w_out"], n), 8, 512) for n in range(2)]
        L_PLE = len(chunks)
        chunks += [(in_cols(d["ple_gate_w"], n), 8, 512) for n in range(2)]
        L_IN2 = len(chunks)
        for n in range(NCH2):
            w = min(512, D_IN2 - n * 512)
            chunks.append((in_cols(d["w_in_2"], n, w), 8, w))
        L_UQ = len(chunks)
        chunks.append((d["w_uq_2"].rearrange("(k p) n -> p k n", p=P), 3, HEADS * DQ_B))
        chunks.append((d["w_ukv_2"].rearrange("(k p) n -> p k n", p=P), 2, D))
        L_OUT2 = len(chunks)
        chunks += [(in_cols(d["w_out_2"], n), 8, 512) for n in range(2)]

        def chunk_used(L):
            if L < 5:
                return proj_done, 4 * (L + 1)
            if L < L_PLE:
                return wo_done, 4 * (L - 4)
            if L < L_IN2:
                return plp_done, 4 * (L - L_PLE + 1)
            if L < L_UQ:
                return pr2_done, 4 * (L - L_IN2 + 1)
            return (qb_done if L == L_UQ else kv_done), NT

        def wview(L):
            _, k, w = chunks[L]
            return wbuf[:, L % 2, 0:k * w].rearrange("p (k n) -> p k n", k=k)

        @block.sync
        def _(sp):
            def load_chunk(L):
                if L >= 2:
                    used, n = chunk_used(L - 2)
                    sp.wait_ge(used, n)
                sp.dma_start(wview(L), chunks[L][0]).then_inc(w_ld[L % 2], 16)

            for L in range(L_PLE):
                load_chunk(L)
            sp.wait_ge(wo_done, 2 * NT)
            sp.dma_start(braw, d["expert_b_gate_up"]).then_inc(braw_ld, 16)
            sp.dma_start(bdown, d["expert_b_down"]).then_inc(bd_ld, 16)
            load_chunk(L_PLE)

            def load_gu(e, c, rows):
                sp.dma_start(gu_w[c], d["expert_w_gate_up"][ds(e, 1), c * P:(c + 1) * P, :].rearrange("o p n -> p (o n)")
                             ).then_inc(gu_ld[c], 16)

            def load_dn(e, c):
                sp.dma_start(dn_w[c], d["expert_w_down"][ds(e, 1), c * 256:(c + 1) * 256, :]
                             .rearrange("o (j p) n -> p (o j) n", p=P)).then_inc(dn_ld[c], 16)

            sp.wait_ge(wo_ev, 8)
            for c in range(8):
                load_gu(0, c, None)
            for c in range(4):
                load_dn(0, c)
            sp.wait_ge(item_rdy, 1)
            n_it = sp.value_load(n_items[0:1, 0:1], min_val=E, max_val=NITEM - 1)
            with sp.Fori(1, n_it) as i:
                e = sp.value_load(item_ei[0:1, ds(i, 1)], min_val=0, max_val=E - 1)
                for c in range(8):
                    sp.wait_ge(gu_used, 8 * i + (c - 7))
                    load_gu(e, c, None)
                for c in range(4):
                    sp.wait_ge(dn_used, 4 * i + (c - 3))
                    load_dn(e, c)
            sp.wait_ge(combined, 1)
            load_chunk(L_PLE + 1)
            for L in range(L_IN2, len(chunks)):
                load_chunk(L)

        @block.tensor
        def _(pe):
            def norm_to_cols(n, src):
                pe.wait_ge(norm_rows, NT * (NORM[n] + 1))
                for k in range(KD):
                    b = bank[4 + k % 4]
                    if k >= 4:
                        pe.wait_ge(norm_cols[k % 2], 4 * NORM[n] + (k - 4) // 2 + 1)
                    for t in range(NT):
                        mm = pe.transpose(b[:, t * P:(t + 1) * P], src[:, t, k * P:(k + 1) * P], ident)
                    mm.then_inc(norm_T, 1)

            def cols_ready(n):
                pe.wait_ge(norm_cols[0], 4 * (NORM[n] + 1))
                pe.wait_ge(norm_cols[1], 4 * (NORM[n] + 1))

            def chunk_ready(L):
                pe.wait_ge(w_ld[L % 2], 16 * (L // 2 + 1))

            def dense_rows(L, lhs, t, b, cols=None):
                wv = wview(L)
                k_n, w = wv.shape[1], wv.shape[2]
                a, z = cols or (0, w)
                for k in range(k_n):
                    mm = pe.matmul(b[:, 0:z - a], lhs[:, k, t * P:(t + 1) * P], wv[:, k, a:z],
                                   start=(k == 0), stop=(k == k_n - 1))
                return mm

            pe.wait_ge(cst_ld, 16)
            norm_to_cols("mix", xr)
            cols_ready("mix")
            for j, n in enumerate(IN_ORDER):
                chunk_ready(j)
                for t in range(NT):
                    g = 4 * j + t
                    if g >= 4:
                        pe.wait_ge(proj_ev, g - 3)
                    b = bank[g % 4]
                    if n < 4:
                        mm = dense_rows(j, xc, t, b)
                    else:
                        wv = wview(j)
                        for k in range(KD):
                            mm = pe.matmul(b[:, :], wv[:, k, t * P:(t + 1) * P], xc[:, k, :],
                                           start=(k == 0), stop=(k == KD - 1))
                    mm.then_inc(proj_done, 1)
            pe.wait_ge(poolw_ld, 16)
            for g in range(4):
                pe.wait_ge(pooled, g + 1)
                pe.matmul(bank[4 + g][:, :], poolw[:, g, :], uT[:, g, PAD:], start=True, stop=True
                          ).then_inc(mixg_done, 1)
            pe.wait_ge(gate_ev, 4)
            for w in range(2):
                pe.wait_ge(rope_done, w + 1)
                for a in range(4):
                    if w == 1:
                        pe.wait_ge(qkT_ev, a + 1)
                    for t in range(NT):
                        mm = pe.transpose(bank[a][:, t * P:(t + 1) * P], proj[:, t, w * D_RET + a * P:w * D_RET + (a + 1) * P], ident)
                    mm.then_inc(qkT_done, 1)
            pe.wait_ge(mixg_ev, 4)

            def scores(hd):
                a, lo = hd // 2, 64 * (hd % 2)
                for j in range(NT):
                    n = 4 * hd + j
                    if n >= 4:
                        pe.wait_ge(sc_ev, n - 3)
                    pe.matmul(bank[j][:, 0:S - j * P], qkT[lo:lo + 64, 1, a, j * P:(j + 1) * P],
                              qkT[lo:lo + 64, 0, a, j * P:S], start=True, stop=True).then_inc(sc_done, 1)

            def values(hd):
                pe.wait_ge(sc_ev, 4 * hd + 4)
                for i in range(NT):
                    for j in range(i + 1):
                        mm = pe.matmul(bank[4 + i][:, hd * DH:(hd + 1) * DH], scT[:, hd % 2, j, i * P:(i + 1) * P],
                                       proj[:, j, 2 * D_RET + hd * DH:2 * D_RET + (hd + 1) * DH],
                                       start=(j == 0), stop=(j == i))
                return mm

            pe.wait_ge(qkT_ev, 8)
            for hd in range(HEADS):
                scores(hd)
                if hd:
                    values(hd - 1)
            values(HEADS - 1).then_inc(y1_done, 1)
            pe.wait_ge(sc_ev, 32)
            for k in range(4):
                for t in range(NT):
                    pe.wait_ge(ret_rows, t + 1)
                    mm = pe.transpose(bank[k][:, t * P:(t + 1) * P], xr[:, t, 512 + k * P:512 + (k + 1) * P], ident)
                mm.then_inc(retT_done, 1)
            pe.wait_ge(retT_ev[0], 2)
            pe.wait_ge(retT_ev[1], 2)
            for n in range(2):
                chunk_ready(5 + n)
                for t in range(NT):
                    if n:
                        pe.wait_ge(wo_ev, t + 1)
                    dense_rows(5 + n, xc, t, bank[t]).then_inc(wo_done, 1)

            norm_to_cols("moe", xr)
            cols_ready("moe")
            pe.wait_ge(rw_ld, 16)
            pe.wait_ge(wo_ev, 8)
            for t in range(NT):
                for k in range(KD):
                    mm = pe.matmul(bank[0][:, t * E:(t + 1) * E], xc[:, k, t * P:(t + 1) * P], rw[:, k, :],
                                   start=(k == 0), stop=(k == KD - 1))
            mm.then_inc(lg_done, 1)
            pe.wait_ge(member_rdy, 1)
            for t in range(NT):
                for j in range(t + 1):
                    pe.matmul(bank[1][:, t * E:(t + 1) * E], C["ustrict"] if j == t else C["ones"], member[:, j, :],
                              start=(j == 0), stop=(j == t))
            for j in range(NT):
                mm = pe.matmul(bank[2][:, 0:E], C["ones"], member[:, j, :], start=(j == 0), stop=(j == NT - 1))
            mm.then_inc(rank_done, 1)
            pe.wait_ge(gd_rdy, 1)
            for t in range(NT):
                mm = pe.transpose(bank[3][0:E, t * P:(t + 1) * P], gdense[:, t, :], ident)
            mm.then_inc(gT_done, 1)
            pe.wait_ge(gT_ev, 1)
            pe.wait_ge(bd_ld, 16)
            for n in range(2):
                for t in range(NT):
                    if n:
                        pe.wait_ge(bd_ev, t + 1)
                    pe.matmul(bank[4 + t][:, :], gT[:, t * P:(t + 1) * P], bdown[:, n * 512:(n + 1) * 512],
                              start=True, stop=True).then_inc(bd_done, 1)

            def item_T(i):
                pe.wait_ge(xg_ld, 16 * i + 16)
                for k in range(KD):
                    mm = pe.transpose(bank[6 + k // 4][:, k % 4 * P:(k % 4 + 1) * P], xg[:, k * P:(k + 1) * P], ident)
                mm.then_inc(xgT_done, 1)

            def act_T(i):
                pe.wait_ge(act_rdy, i + 1)
                for k in range(KD):
                    mm = pe.transpose(bank[6 + k // 4][:, k % 4 * P:(k % 4 + 1) * P], act_s[:, k * P:(k + 1) * P], ident)
                mm.then_inc(actT_done, 1)

            def gate_up(i, mid=None):
                pe.wait_ge(xgT_ev, i + 1)
                for c in range(KD):
                    pe.wait_ge(gu_ld[c], 16 * i + 16)
                    for n in range(4):
                        mm = pe.matmul(bank[n][:, :], xgT[:, c, :], gu_w[c][:, n * 512:(n + 1) * 512],
                                       start=(c == 0), stop=False)
                    mm.then_inc(gu_used, 1)
                    if c == 3 and mid:
                        mid()
                pe.wait_ge(sel_rdy, i + 1)
                for n in range(4):
                    mm = pe.matmul(bank[n][:, :], sel_e, bparts[:, n * 512:(n + 1) * 512], start=False, stop=True)
                mm.then_inc(gu_done, 1)

            def down(i):
                pe.wait_ge(actT_ev, i + 1)
                pe.wait_ge(y_free, i + 1)
                for c in range(4):
                    pe.wait_ge(dn_ld[c], 16 * i + 16)
                    for j in range(2):
                        for n in range(2):
                            mm = pe.matmul(bank[4 + n][:, :], actT[:, 2 * c + j, :], dn_w[c][:, j, n * 512:(n + 1) * 512],
                                           start=(c == 0 and j == 0), stop=(c == 3 and j == 1))
                    mm.then_inc(dn_used, 1)

            pe.wait_ge(bd_ev, 8)
            pe.wait_ge(place_rdy, 1)
            n_it = pe.value_load(n_items[0:1, 0:1], min_val=E, max_val=NITEM - 1)
            item_T(0)
            pe.wait_ge(bp_ld, 32)
            pe.wait_ge(bsplit, 3)
            gate_up(0)
            item_T(1)
            with pe.Fori(1, n_it) as i:
                pe.wait_ge(gu_ev, i)
                gate_up(i, lambda: act_T(i - 1))
                pe.wait_ge(actT_ev, i)
                item_T(i + 1)
                down(i - 1)
            pe.wait_ge(xgT_ev, n_it + 1)
            act_T(n_it - 1)
            down(n_it - 1)

            pe.wait_ge(p_ld, 16)
            pe.wait_ge(gu_ev, n_it)
            for k in range(2):
                for t in range(NT):
                    mm = pe.transpose(bank[k][:, t * P:(t + 1) * P], p_rows[:, t, k * P:(k + 1) * P], ident)
                mm.then_inc(pT_done, 1)
            pe.wait_ge(y_free, n_it + 1)
            pe.wait_ge(xgT_ev, n_it + 1)
            norm_to_cols("ple", xr)
            cols_ready("ple")
            pe.wait_ge(pT_ev, 2)
            pe.wait_ge(plew_ld, 16)
            for n in range(2):
                chunk_ready(L_PLE + n)
                for t in range(NT):
                    g = 4 * n + t
                    if g >= 2:
                        pe.wait_ge(ple_ev, g - 1)
                    dense_rows(L_PLE + n, xc, t, bank[2 * (g % 2)]).then_inc(plg_done, 1)
                    for k in range(2):
                        mm = pe.matmul(bank[2 * (g % 2) + 1][:, :], p_cols[:, k, t * P:(t + 1) * P],
                                       plew[:, k, n * 512:(n + 1) * 512], start=(k == 0), stop=(k == 1))
                    mm.then_inc(plp_done, 1)

            norm_to_cols("two", xr)
            cols_ready("two")
            pe.wait_ge(ple_ev, 8)
            for n in range(NCH2):
                chunk_ready(L_IN2 + n)
                for t in range(NT):
                    g = 4 * n + t
                    if g >= 4:
                        pe.wait_ge(pr2_ev[g % 2], (g - 4) // 2 + 1)
                    dense_rows(L_IN2 + n, xc, t, bank[g % 4]).then_inc(pr2_done, 1)
            pe.wait_ge(pr2_ev[0], 16)
            pe.wait_ge(pr2_ev[1], 16)

            def cols2(n):
                if n < 8:
                    return lambda t: pr2[:, t, n * P:(n + 1) * P]
                if n < 12:
                    return lambda t: pr2[:, t, C_QI + (n - 8) * P:C_QI + (n - 7) * P]
                return lambda t: ki2[:, t, :]

            for n in range(13):
                if n in (0, 4, 8):
                    pe.wait_ge(qa_rdy, n // 4 + 1)
                if n >= 4:
                    pe.wait_ge(qkaT_ev[n % 2], (n - 4) // 2 + 1)
                f = cols2(n)
                for t in range(NT):
                    mm = pe.transpose(bank[n % 4][:, t * P:(t + 1) * P], f(t), ident)
                mm.then_inc(qkaT_done, 1)
            pe.wait_ge(qkaT_ev[0], 7)
            pe.wait_ge(qkaT_ev[1], 6)
            for u in range(3 * HEADS):
                t, hd = 1 + u // HEADS, u % HEADS
                lo = 64 * (hd % 2)
                if u >= 4:
                    pe.wait_ge(ix_relu, u - 3)
                pe.matmul(bank[4 + u % 4][:, 0:P * (t + 1)], qiT[lo:lo + 64, hd // 2, t * P:(t + 1) * P],
                          kiT[lo:lo + 64, 0:P * (t + 1)], start=True, stop=True).then_inc(ix_done, 1)
            for k in range(5):
                if k == 0:
                    pe.wait_ge(lat_rdy, 2)
                if k >= 4:
                    pe.wait_ge(lat_ev[0], 1)
                for t in range(NT):
                    mm = pe.transpose(bank[k % 4][:, t * P:(t + 1) * P], pr2[:, t, C_CQ + k * P:C_CQ + (k + 1) * P], ident)
                mm.then_inc(latT_done, 1)
            pe.wait_ge(lat_ev[0], 3)
            pe.wait_ge(lat_ev[1], 2)
            chunk_ready(L_UQ)
            chunk_ready(L_UQ + 1)
            pe.wait_ge(ix_relu, 24)
            for t in range(NT):
                if t:
                    pe.wait_ge(qb_ev, t)
                    pe.wait_ge(k_ev, t)
                dense_rows(L_UQ, lat_cols, t, bank[0], (0, 512))
                dense_rows(L_UQ, lat_cols, t, bank[1], (512, 768)).then_inc(qb_done, 1)
                dense_rows(L_UQ + 1, lat_cols[:, 3:5, :], t, bank[2], (0, 512))
                dense_rows(L_UQ + 1, lat_cols[:, 3:5, :], t, bank[3], (512, 1024)).then_inc(kv_done, 1)
                for w in range(2):
                    pe.wait_ge(qb_rdy, 2 * t + w + 1)
                    row = (qrow, krow)[w]
                    for half in range(2):
                        n = 4 * t + 2 * w + half
                        if n >= 4:
                            pe.wait_ge(qbT_ev[n % 2], (n - 4) // 2 + 1)
                        b = bank[4 + n % 4]
                        for a in range(4):
                            hd = 4 * half + a
                            mm = pe.transpose(b[0:DQ_B, a * P:(a + 1) * P], row[:, hd * DQ_B:(hd + 1) * DQ_B], ident)
                        mm.then_inc(qbT_done, 1)
            pe.wait_ge(qbT_ev[0], 8)
            pe.wait_ge(qbT_ev[1], 8)
            pe.wait_ge(qb_ev, NT)
            pe.wait_ge(k_ev, NT)

            def unit(u):
                att, t, hd = u // 32, u // 8 % 4, u % 8
                return att, t, hd, P * (t + 1)

            def at_scores(u):
                att, t, hd, w = unit(u)
                if u >= 2:
                    pe.wait_ge(at_s, u - 1)
                if att == 0:
                    lo = 64 * (hd % 2)
                    q = qkaT[lo:lo + 64, 0, hd // 2, t * P:(t + 1) * P]
                    k = qkaT[lo:lo + 64, 1, hd // 2, 0:w]
                else:
                    q, k = qbT(hd)[0:DQ_B, t * P:(t + 1) * P], kbT[0:DQ_B, hd, 0:w]
                pe.matmul(bank[u % 2][:, 0:w], q, k, start=True, stop=True).then_inc(at_done, 1)

            def at_T(u):
                att, t, hd, w = unit(u)
                pe.wait_ge(at_exp, u + 1)
                if u >= 2:
                    pe.wait_ge(pT2_ev, u - 1)
                for j in range(t + 1):
                    mm = pe.transpose(bank[2 + u % 2][:, j * P:(j + 1) * P], sP[u % 2][:, j * P:(j + 1) * P], ident)
                mm.then_inc(pT2_done, 1)

            def at_values(u):
                att, t, hd, w = unit(u)
                pe.wait_ge(pT2_ev, u + 1)
                g = u // 8
                if hd == 0 and g >= 2:
                    pe.wait_ge(o_ev, g - 1)
                for j in range(t + 1):
                    v = pr2[:, j, (C_VA, C_QI)[att] + hd * DH:(C_VA, C_QI)[att] + (hd + 1) * DH]
                    mm = pe.matmul(bank[4 + g % 2][:, hd * DH:(hd + 1) * DH], sPT[u % 2][:, j, :], v,
                                   start=(j == 0), stop=(j == t))
                mm.then_inc(pv_done, 1)

            for u in range(64 + 2):
                if u < 64:
                    at_scores(u)
                if 1 <= u <= 64:
                    at_T(u - 1)
                if u >= 2:
                    at_values(u - 2)
            pe.wait_ge(mixed, 8)
            for k in range(KD):
                if k >= 4:
                    pe.wait_ge(mxT_ev[k % 2], (k - 4) // 2 + 1)
                for t in range(NT):
                    c = C_QA + k * P if k < 4 else C_CQ + (k - 4) * P
                    mm = pe.transpose(bank[k % 4][:, t * P:(t + 1) * P], pr2[:, t, c:c + P], ident)
                mm.then_inc(mxT_done, 1)
            pe.wait_ge(mxT_ev[0], 4)
            pe.wait_ge(mxT_ev[1], 4)
            for n in range(2):
                chunk_ready(L_OUT2 + n)
                for t in range(NT):
                    dense_rows(L_OUT2 + n, xc, t, bank[4 * (n == 0) + t]).then_inc(out_done, 1)

        @block.scalar
        def _(act):
            def copy(out, in_, scale=1.0):
                return nc.scalar.activation(out, in_, ACT.Copy, scale=scale)

            def squares(n):
                for t in range(NT):
                    ins = nc.scalar.activation(xr[:, t, :], h[:, t, :], ACT.Square, accum_out=sumsq[:, t:t + 1])
                    ins.then_inc(norm_sq, 1)

            def cols_evac(n, gain):
                for k in range(0, KD, 2):
                    act.wait_ge(norm_T, KD * NORM[n] + k + 1)
                    copy(xc[:, k, :], bank[4 + k % 4][:, :], gain[:, k:k + 1] if gain is not None else 1.0
                         ).then_inc(norm_cols[0], 1)

            act.dma_start(h[:, :, :], d["x"].rearrange("(t p) n -> p t n", p=P)).then_inc(x_ld, 16)
            act.dma_start(cst[:, :], d["constants"]).then_inc(cst_ld, 16)
            act.dma_start(sml[:, :], d["small"]).then_inc(small_ld, 16)
            act.dma_start(posi, d["positions"]).then_inc(small_ld, 16)
            act.dma_start(poolw, d["pool_w"].rearrange("g c n -> c g n")).then_inc(poolw_ld, 16)
            act.dma_start(rw[:, :, :], d["router_w"].rearrange("(k p) e -> p k e", p=P)).then_inc(rw_ld, 16)
            act.dma_start(grow[:, :], d["norm_moe_w"].partition_broadcast(P)).then_inc(grow_ld, 16)
            act.wait_ge(x_ld, 16)
            squares("mix")
            act.wait_ge(trig_in, 1)
            nc.scalar.activation(sin1, ang.rearrange("p (t f) -> p t f", t=NT), ACT.Sin)
            nc.scalar.activation(cos1, ctmp.rearrange("p (t f) -> p t f", t=NT), ACT.Sin).then_inc(trig_out, 1)
            act.wait_ge(small_ld, 32)
            cols_evac("mix", M["g_mix"])
            act.wait_ge(pad_zero, 1)
            for g in range(16):
                act.wait_ge(proj_done, g + 1)
                n, t = IN_ORDER[g // 4], g % 4
                dst = uT[:, t, PAD:] if n == 4 else proj[:, t, n * 512:(n + 1) * 512]
                copy(dst, bank[g % 4][:, :]).then_inc(proj_ev, 1)
            for t in range(NT):
                act.wait_ge(proj_done, 17 + t)
                nc.scalar.activation(xr[:, t, 0:512], bank[t][:, :], ACT.Sigmoid).then_inc(silu_sig, 1)
            for g in range(4):
                act.wait_ge(mixg_done, g + 1)
                copy(xc[:, 4 + g, :], bank[4 + g][:, :], M["pool_scale"][:, g:g + 1]).then_inc(mixg_ev, 1)
            for n in range(8):
                act.wait_ge(qkT_done, n + 1)
                copy(qkT[:, n // 4, n % 4, :], bank[n % 4][:, :]).then_inc(qkT_ev, 1)
            for k in (0, 2):
                act.wait_ge(retT_done, k + 1)
                copy(xc[:, k, :], bank[k][:, :], M["gn_w"][:, k:k + 1]).then_inc(retT_ev[0], 1)

            act.wait_ge(wo_ev, 8)
            squares("moe")
            act.wait_ge(norm_rows, 2 * NT)
            act.dma_start(xn_dram.rearrange("(t p) n -> p t n", p=P), xr).then_inc(rows_st, 16)
            cols_evac("moe", None)
            act.wait_ge(gexp_in, 1)
            for t in range(NT):
                ins = nc.scalar.activation(gates[:, t * 4:(t + 1) * 4], top8[:, t * 8:t * 8 + 4], ACT.Exp,
                                           bias=negv0[:, t:t + 1], accum_out=gsum[:, t:t + 1])
            act.drain().then_inc(gexp, 1)
            act.wait_ge(gT_done, 1)
            act.wait_ge(rows_st, 16)
            copy(gT, bank[3][0:E, :]).then_inc(gT_ev, 1)
            act.wait_ge(bsplit, 3)
            act.dma_start(bparts[32:64, :], bpart2).then_inc(bp_ld, 16)
            act.dma_start(bparts[64:96, :], bpart3).then_inc(bp_ld, 16)

            def copy_T(i, done, ev, dst):
                act.wait_ge(done, i + 1)
                copy(dst[:, 0:4, :], bank[6][:, :].rearrange("p (k n) -> p k n", k=4))
                copy(dst[:, 4:8, :], bank[7][:, :].rearrange("p (k n) -> p k n", k=4))
                act.drain().then_inc(ev, 1)

            def sigmoid(i):
                act.wait_ge(g_rdy, i + 1)
                nc.scalar.activation(sig_s, gate_s, ACT.Sigmoid, scale=ALPHA).then_inc(sig_rdy, 1)

            def store_y(i):
                act.wait_ge(dn_used, 4 * i + 4)
                copy(y_s[:, 0:512], bank[4][:, :])
                copy(y_s[:, 512:1024], bank[5][:, :])
                act.drain().then_inc(y_free, 1)
                act.dma_start(y_dram[ds(i * P, P), :], y_s).then_inc(y_st, 16)

            act.nop().then_inc(y_free, 1)
            act.wait_ge(item_rdy, 1)
            n_it = act.value_load(n_items[0:1, 0:1], min_val=E, max_val=NITEM - 1)
            copy_T(0, xgT_done, xgT_ev, xgT)
            copy_T(1, xgT_done, xgT_ev, xgT)
            sigmoid(0)
            with act.Fori(1, n_it) as i:
                copy_T(i - 1, actT_done, actT_ev, actT)
                copy_T(i + 1, xgT_done, xgT_ev, xgT)
                sigmoid(i)
                store_y(i - 1)
                act.wait_ge(y_st, 16 * i)
            copy_T(n_it - 1, actT_done, actT_ev, actT)
            store_y(n_it - 1)

            act.dma_start(grow[:, :], d["final_norm_w"].partition_broadcast(P)).then_inc(grow2_ld, 16)
            act.wait_ge(dn_used, 4 * n_it)
            act.wait_ge(y_st, 16 * n_it)
            act.dma_start(p_rows, d["p"].rearrange("(t p) n -> p t n", p=P)).then_inc(p_ld, 16)
            act.dma_start(plew, d["ple_proj_w"].rearrange("(k p) n -> p k n", p=P)).then_inc(plew_ld, 16)
            for k in range(2):
                act.wait_ge(pT_done, k + 1)
                copy(p_cols[:, k, :], bank[k][:, :]).then_inc(pT_ev, 1)
            act.wait_ge(combined, 1)
            squares("ple")
            cols_evac("ple", M["g_ple"])
            for g in range(8):
                act.wait_ge(plg_done, g + 1)
                nc.scalar.activation(sig2[:, g, :], bank[2 * (g % 2)][:, :], ACT.Sigmoid).then_inc(plg_sig, 1)
            act.wait_ge(ple_ev, 8)
            squares("fin")
            act.wait_ge(final_rdy, 1)
            squares("two")
            cols_evac("two", M["gain2"])
            for g in range(0, 4 * NCH2, 2):
                act.wait_ge(pr2_done, g + 1)
                n, t = g // 4, g % 4
                w = min(512, D_IN2 - n * 512)
                copy(pr2[:, t, n * 512:n * 512 + w], bank[g % 4][:, 0:w]).then_inc(pr2_ev[0], 1)

            def dst2(n):
                return qkaT[:, n // 4, n % 4, :] if n < 8 else qiT[:, n - 8, :] if n < 12 else kiT

            for n in range(0, 13, 2):
                act.wait_ge(qkaT_done, n + 1)
                copy(dst2(n), bank[n % 4][:, :]).then_inc(qkaT_ev[0], 1)
            for u in range(24):
                t = 1 + u // HEADS
                act.wait_ge(ix_done, u + 1)
                if u >= 2:
                    act.wait_ge(ix_acc, u - 1)
                nc.scalar.activation(sP[u % 2][:, 0:P * (t + 1)], bank[4 + u % 4][:, 0:P * (t + 1)], ACT.Relu
                                     ).then_inc(ix_relu, 1)
            for k in (0, 2, 4):
                act.wait_ge(latT_done, k + 1)
                gain = M["bq_lat"][:, k:k + 1] if k < 3 else M["bkv_lat"][:, k - 3:k - 2]
                copy(lat_cols[:, k, :], bank[k % 4][:, :], gain).then_inc(lat_ev[0], 1)
            for t in range(NT):
                act.wait_ge(qb_done, t + 1)
                if t:
                    act.wait_ge(qbT_done, 4 * t - 2)
                copy(qrow[:, 0:512], bank[0][:, :])
                copy(qrow[:, 512:768], bank[1][:, 0:256]).then_inc(qb_ev, 1)
                act.wait_ge(kv_done, t + 1)
                for half in range(2):
                    src = bank[2 + half][:, :].rearrange("p (a n) -> p a n", a=4)
                    copy(pr2[:, t, C_QI + half * 256:C_QI + (half + 1) * 256].rearrange("p (a n) -> p a n", a=4),
                         src[:, :, 64:128])
                    if t and half == 0:
                        act.wait_ge(qbT_done, 4 * t)
                    ins = copy(krow[:, half * 384:(half + 1) * 384].rearrange("p (a n) -> p a n", a=4)[:, :, 0:64],
                               src[:, :, 0:64])
                ins.then_inc(k_ev, 1)
                for n in (4 * t, 4 * t + 2):
                    act.wait_ge(qbT_done, n + 1)
                    for a in range(4):
                        hd = a
                        dst = qbT(hd) if n % 4 == 0 else kbT[:, hd, :]
                        ins = copy(dst[0:DQ_B, t * P:(t + 1) * P], bank[4 + n % 4][0:DQ_B, a * P:(a + 1) * P])
                    ins.then_inc(qbT_ev[0], 1)
            def unit(u):
                t = u // 8 % 4
                return t, P * (t + 1)

            def exponentials(u):
                t, w = unit(u)
                act.wait_ge(at_s, u + 1)
                if u >= 2:
                    act.wait_ge(pT2_done, u - 1)
                nc.scalar.activation(sP[u % 2][:, 0:w], sS[u % 2][:, 0:w], ACT.Exp, bias=nmax[:, u % 4:u % 4 + 1],
                                     scale=-1.0, accum_out=rs_all[:, u % 16:u % 16 + 1]).then_inc(at_exp, 1)

            def at_copy(u):
                t, w = unit(u)
                act.wait_ge(pT2_done, u + 1)
                if u >= 2:
                    act.wait_ge(pv_done, u - 1)
                copy(sPT[u % 2][:, 0:t + 1, :], bank[2 + u % 2][:, 0:w].rearrange("p (j n) -> p j n", j=t + 1)
                     ).then_inc(pT2_ev, 1)

            for u in range(64 + 1):
                if u < 64:
                    if u % 8 == 0 and u >= 16:
                        act.wait_ge(o_ev, u // 8 - 1)
                    exponentials(u)
                if u:
                    at_copy(u - 1)
            for g in range(8):
                att, t = g // 4, g % 4
                c = (C_GA, C_GB)[att]
                act.wait_ge(o_ev, g + 1)
                nc.scalar.activation(sS[g % 2], pr2[:, t, c:c + 512], ACT.Sigmoid).then_inc(gsig2, 1)
                act.wait_ge(mixed, g + 1)
            for k in range(0, KD, 2):
                act.wait_ge(mxT_done, k + 1)
                copy(xc[:, k, :], bank[k % 4][:, :]).then_inc(mxT_ev[0], 1)
            for t in range(NT):
                act.wait_ge(out_rdy, NT + t + 1)
                act.dma_start(d["out"][t * P:(t + 1) * P, :], h[:, t, :]).then_inc(out_st, 16)
            act.wait_ge(out_st, 16 * NT)

        @block.vector
        def _(dve):
            v = nc.vector
            D_ = dve.drain

            asked = [0]

            def rsqrt_mean():
                asked[0] += 1
                dve.drain().then_inc(sums_rdy, 1)
                dve.wait_ge(rstd_rdy, asked[0])

            def norm_to_rows(n, eps, gain=None):
                dve.wait_ge(norm_sq, NT * (SQ[n] + 1))
                rsqrt_mean()
                for t in range(NT):
                    if gain is None:
                        ins = v.tensor_scalar(xr[:, t, :], h[:, t, :], rstd[:, t:t + 1], None, ALU.mult)
                    else:
                        ins = v.scalar_tensor_tensor(out=xr[:, t, :], in0=h[:, t, :], scalar=rstd[:, t:t + 1],
                                                     in1=gain, op0=ALU.mult, op1=ALU.mult)
                    ins.then_inc(norm_rows, 1)

            def cols_evac(n, gain):
                for k in range(1, KD, 2):
                    dve.wait_ge(norm_T, KD * NORM[n] + k + 1)
                    if gain is None:
                        ins = v.tensor_copy(xc[:, k, :], bank[4 + k % 4][:, :])
                    else:
                        ins = v.tensor_scalar(xc[:, k, :], bank[4 + k % 4][:, :], gain[:, k:k + 1], None, ALU.mult)
                    ins.then_inc(norm_cols[1], 1)

            def rope(x1, x2, cos, sin, t):
                v.tensor_tensor(t[0], x1, cos, ALU.mult)
                v.tensor_tensor(t[1], x2, sin, ALU.mult)
                v.tensor_tensor(t[2], x2, cos, ALU.mult)
                v.tensor_tensor(t[3], x1, sin, ALU.mult)
                D_()
                v.tensor_tensor(x1, t[0], t[1], ALU.subtract)
                return v.tensor_tensor(x2, t[2], t[3], ALU.add)

            def over(ap, axis, n):
                u = ap.unsqueeze(axis)
                shape = list(u.shape)
                shape[axis] = n
                return u.to_broadcast(shape)

            dve.wait_ge(cst_ld, 16)
            dve.wait_ge(small_ld, 32)
            v.tensor_copy(posf, posi)
            D_()
            a3 = ang.rearrange("p (t f) -> p t f", t=NT)
            v.tensor_tensor(a3, over(posf, 2, HALF_A), over(C["invfreq"], 1, NT), ALU.mult)
            D_()
            v.tensor_scalar(turns, ang, float(1 / TWO_PI), ROUND, ALU.mult, ALU.add)
            D_()
            v.tensor_scalar(turns, turns, ROUND, None, ALU.subtract)
            D_()
            for part in (PI_A, PI_B, PI_C):
                v.scalar_tensor_tensor(out=ang, in0=turns, scalar=-part, in1=ang, op0=ALU.mult, op1=ALU.add)
                D_()
            v.tensor_scalar(ang, ang, 3.1415925, -3.1415925, ALU.min, ALU.max)
            D_()
            v.scalar_tensor_tensor(out=ctmp, in0=ang, scalar=-1.0, in1=ang, op0=ALU.mult, op1=ALU.max)
            D_()
            v.tensor_scalar(ctmp, ctmp, -1.0, float(np.pi / 2), ALU.mult, ALU.add).then_inc(trig_in, 1)
            norm_to_rows("mix", EPS1)
            cols_evac("mix", M["g_mix"])
            dve.wait_ge(trig_out, 1)
            t4 = [tmp4[:, b, :].rearrange("p (t a f) -> p t a f", t=NT, a=HEADS) for b in range(4)]
            for w in range(2):
                dve.wait_ge(proj_ev, 4 * w + 4)
                x = proj[:, :, w * D_RET:(w + 1) * D_RET].rearrange("p t (a f) -> p t a f", a=HEADS)
                rope(x[:, :, :, 0:HALF_A], x[:, :, :, HALF_A:DH], over(cos1, 2, HEADS), over(sin1, 2, HEADS), t4)
                D_()
                g = C[("gq", "gk")[w]].rearrange("p (t a) -> p t a", t=NT)
                v.tensor_tensor(x, x, over(g, 3, DH), ALU.mult).then_inc(rope_done, 1)
            for t in range(NT):
                dve.wait_ge(silu_sig, t + 1)
                v.tensor_tensor(proj[:, t, 1536:2048], bank[t][:, :], xr[:, t, 0:512], ALU.mult).then_inc(gate_ev, 1)
            for n in range(32):
                j = n % 4
                dve.wait_ge(sc_done, n + 1)
                w = S - j * P
                v.tensor_tensor(scT[:, n // 4 % 2, j, j * P:S], bank[j][:, 0:w], C["causal"][:, 0:w], ALU.mult
                                ).then_inc(sc_ev, 1)
            dve.wait_ge(y1_done, 1)
            for t in range(NT):
                y = bank[4 + t][:, :].rearrange("p (a n) -> p a n", a=HEADS)
                yc = xr[:, t, 512:1024].rearrange("p (a n) -> p a n", a=HEADS)
                sq = tmp4[:, t, 0:512].rearrange("p (a n) -> p a n", a=HEADS)
                m, q = mu[:, t * 8:(t + 1) * 8], var[:, t * 8:(t + 1) * 8]
                v.tensor_reduce(m, y, X, ALU.add)
                D_()
                v.tensor_scalar(m, m, 1.0 / DH, None, ALU.mult)
                D_()
                v.tensor_tensor(yc, y, over(m, 2, DH), ALU.subtract)
                D_()
                v.tensor_tensor(sq, yc, yc, ALU.mult)
                D_()
                v.tensor_reduce(q, sq, X, ALU.add)
                D_()
                rsqrt_mean()
                v.tensor_tensor(yc, yc, over(q, 2, DH), ALU.mult)
                D_()
                v.tensor_tensor(xr[:, t, 512:1024], xr[:, t, 512:1024], proj[:, t, 1536:2048], ALU.mult
                                ).then_inc(ret_rows, 1)
            for k in (1, 3):
                dve.wait_ge(retT_done, k + 1)
                v.tensor_scalar(xc[:, k, :], bank[k][:, :], M["gn_w"][:, k:k + 1], None, ALU.mult).then_inc(retT_ev[1], 1)
            for g in range(8):
                n, t = g // 4, g % 4
                dve.wait_ge(wo_done, g + 1)
                hv = h[:, t, n * 512:(n + 1) * 512]
                v.tensor_tensor(hv, hv, bank[t][:, :], ALU.add).then_inc(wo_ev, 1)

            dve.wait_ge(grow_ld, 16)
            norm_to_rows("moe", EPS1, grow[:, :])
            cols_evac("moe", None)
            dve.wait_ge(lg_done, 1)
            v.tensor_tensor(logits, bank[0][:, 0:NT * E].rearrange("p (t e) -> p t e", e=E), over(M["router_b"], 1, NT), ALU.add)
            D_()
            for t in range(NT):
                v.max(top8[:, t * 8:(t + 1) * 8], logits[:, t, :])
                D_()
                v.max_index(idx8[:, t * 8:(t + 1) * 8], top8[:, t * 8:(t + 1) * 8], logits[:, t, :])
            D_()
            t8 = top8.rearrange("p (t a) -> p t a", a=8)
            v.tensor_scalar(negv0.unsqueeze(2), t8[:, :, 0:1], -1.0, None, ALU.mult).then_inc(gexp_in, 1)
            idxf = more[:, 0:16]
            v.tensor_copy(idxf.rearrange("p (t a) -> p t a", a=TOPK), idx8.rearrange("p (t a) -> p t a", a=8)[:, :, 0:TOPK])
            D_()
            v.tensor_tensor(onehot, over(C["iota32"], 1, 16), over(idxf, 2, E), ALU.is_equal)
            D_()
            v.tensor_reduce(member, onehot.rearrange("p (t a) e -> p t e a", t=NT), X, ALU.add).then_inc(member_rdy, 1)
            dve.wait_ge(gexp, 1)
            v.reciprocal(gsum, gsum)
            D_()
            g3 = gates.rearrange("p (t a) -> p t a", a=TOPK)
            v.tensor_tensor(g3, g3, over(gsum, 2, TOPK), ALU.mult)
            D_()
            v.tensor_tensor(prod, onehot, over(gates, 2, E), ALU.mult)
            D_()
            v.tensor_reduce(gdense, prod.rearrange("p (t a) e -> p t e a", t=NT), X, ALU.add).then_inc(gd_rdy, 1)
            dve.wait_ge(rank_done, 1)
            dve.wait_ge(yzero_st, 16)
            cnt = bank[2][:, 0:E]
            v.tensor_scalar(nblk, cnt, float(P), 1.0, ALU.is_gt, ALU.add)
            D_()
            for m in (2, 3):
                v.tensor_scalar(more, cnt, float(m * P), None, ALU.is_gt)
                D_()
                v.tensor_tensor(nblk, nblk, more, ALU.add)
                D_()
            v.tensor_tensor_scan(incl, C["ones"][:, 0:E], nblk, 0.0, ALU.mult, ALU.add)
            D_()
            v.tensor_copy(n_items, incl[:, E - 1:E])
            v.tensor_tensor(base, incl, nblk, ALU.subtract)
            v.tensor_tensor(cmp48, over(incl, 1, NITEM), over(C["iota48"], 2, E), ALU.is_le)
            D_()
            v.tensor_scalar(base, base, float(P), None, ALU.mult)
            v.tensor_reduce(item_e, cmp48, X, ALU.add)
            D_()
            v.tensor_scalar(item_e, item_e, float(E - 1), None, ALU.min)
            slot3 = logits
            v.tensor_tensor(slot3, bank[1][:, 0:NT * E].rearrange("p (t e) -> p t e", e=E), over(base, 1, NT), ALU.add)
            D_()
            v.tensor_copy(item_ei, item_e)
            v.tensor_tensor(prod.rearrange("p (t a) e -> p t a e", t=NT), onehot.rearrange("p (t a) e -> p t a e", t=NT),
                            over(slot3, 2, TOPK), ALU.mult)
            D_()
            slotf, placef = more[:, 0:16], more[:, 16:32]
            v.tensor_reduce(slotf, prod, X, ALU.add)
            v.tensor_copy(tok_i, C["tok"])
            D_()
            v.tensor_copy(slot_u, slotf)
            D_()
            v.tensor_scalar(place_u, slot_u, 7, None, ALU.logical_shift_right)
            v.tensor_scalar(idx8[:, 0:16], slot_u, P - 1, None, ALU.bitwise_and)
            D_()
            v.tensor_copy(placef, place_u)
            v.tensor_copy(slotf, idx8[:, 0:16])
            D_()
            v.scalar_tensor_tensor(out=placef, in0=slotf, scalar=float(NITEM), in1=placef, op0=ALU.mult, op1=ALU.add)
            D_()
            v.tensor_copy(place_u, placef)
            dve.drain().then_inc(place_rdy, 1)
            dve.drain().then_inc(item_rdy, 1)
            for g in range(8):
                n, t = g // 4, g % 4
                dve.wait_ge(bd_done, g + 1)
                hv = h[:, t, n * 512:(n + 1) * 512]
                v.tensor_tensor(hv, hv, bank[4 + t][:, :], ALU.add).then_inc(bd_ev, 1)
            dve.wait_ge(braw_ld, 16)
            v.tensor_copy(bparts[0:E, :], braw).then_inc(bsplit, 1)
            D_()
            for out, left in ((bpart2, bparts[0:E, :]), (bpart3, bpart2)):
                v.tensor_tensor(braw, braw, left, ALU.subtract)
                D_()
                v.tensor_copy(out, braw).then_inc(bsplit, 1)
                D_()

            def pick(i):
                v.tensor_scalar(sel_e, item_e[0:96, ds(i, 1)].to_broadcast([96, P]), C["pmod"][0:96, :], None,
                                ALU.is_equal).then_inc(sel_rdy, 1)

            def swiglu(i):
                dve.wait_ge(gu_done, i + 1)
                for n in range(4):
                    pair = bank[n][:, :].rearrange("p (n two) -> p n two", two=2)
                    v.tensor_scalar(gate_s[:, n * 256:(n + 1) * 256].unsqueeze(2), pair[:, :, 0:1], LIMIT, None, ALU.min)
                dve.drain().then_inc(g_rdy, 1)
                for n in range(4):
                    pair = bank[n][:, :].rearrange("p (n two) -> p n two", two=2)
                    v.tensor_scalar(up_s[:, n * 256:(n + 1) * 256].unsqueeze(2), pair[:, :, 1:2], LIMIT, -LIMIT, ALU.min, ALU.max)
                dve.drain().then_inc(gu_ev, 1)
                v.scalar_tensor_tensor(out=up_s, in0=up_s, scalar=1.0, in1=gate_s, op0=ALU.add, op1=ALU.mult)
                D_()
                dve.wait_ge(sig_rdy, i + 1)
                v.tensor_tensor(act_s, up_s, sig_s, ALU.mult).then_inc(act_rdy, 1)

            pick(0)
            n_it = dve.value_load(n_items[0:1, 0:1], min_val=E, max_val=NITEM - 1)
            with dve.Fori(0, n_it) as i:
                swiglu(i)
                pick(i + 1)

            for a in range(16):
                t = a // 4
                if a % 4 == 0:
                    dve.wait_ge(yg_ld[t], 16 * TOPK)
                v.scalar_tensor_tensor(out=h[:, t, :], in0=ygat[:, a, :], scalar=gates[:, a:a + 1], in1=h[:, t, :],
                                       op0=ALU.mult, op1=ALU.add)
                D_()
            dve.drain().then_inc(combined, 1)
            norm_to_rows("ple", EPS1)
            cols_evac("ple", M["g_ple"])
            for g in range(8):
                n, t = g // 4, g % 4
                hv = h[:, t, n * 512:(n + 1) * 512]
                dve.wait_ge(plg_sig, g + 1)
                dve.wait_ge(plp_done, g + 1)
                v.tensor_tensor(sig2[:, g, :], sig2[:, g, :], bank[2 * (g % 2) + 1][:, :], ALU.mult)
                D_()
                v.tensor_tensor(hv, hv, sig2[:, g, :], ALU.add).then_inc(ple_ev, 1)
            dve.wait_ge(norm_sq, NT * (SQ["fin"] + 1))
            dve.wait_ge(grow2_ld, 16)
            rsqrt_mean()
            for t in range(NT):
                v.scalar_tensor_tensor(out=h[:, t, :], in0=h[:, t, :], scalar=rstd[:, t:t + 1], in1=grow[:, :],
                                       op0=ALU.mult, op1=ALU.mult)
            dve.drain().then_inc(final_rdy, 1)
            norm_to_rows("two", EPS2)
            cols_evac("two", M["gain2"])
            for g in range(1, 4 * NCH2, 2):
                dve.wait_ge(pr2_done, g + 1)
                n, t = g // 4, g % 4
                w = min(512, D_IN2 - n * 512)
                v.tensor_copy(pr2[:, t, n * 512:n * 512 + w], bank[g % 4][:, 0:w]).then_inc(pr2_ev[1], 1)
            dve.wait_ge(pr2_ev[0], 16)
            D_()
            r4 = [rot[:, b, :].rearrange("p (t a f) -> p t a f", t=NT, a=HEADS) for b in range(4)]
            ca = C["cos_a"].rearrange("p (t f) -> p t f", t=NT)
            sa = C["sin_a"].rearrange("p (t f) -> p t f", t=NT)
            for w in range(2):
                x = pr2[:, :, w * 512:(w + 1) * 512]
                x4 = x.rearrange("p t (a f) -> p t a f", a=HEADS)
                sq = xrows[:, 0:2048].rearrange("p (t n) -> p t n", t=NT)
                v.tensor_tensor(sq, x, x, ALU.mult)
                D_()
                v.tensor_reduce(mu, xrows[:, 0:2048].rearrange("p (a f) -> p a f", f=DH), X, ALU.add)
                D_()
                rsqrt_mean()
                v.tensor_tensor(x4, x4, over(mu.rearrange("p (t a) -> p t a", t=NT), 3, DH), ALU.mult)
                D_()
                for t in range(NT):
                    v.tensor_tensor(x4[:, t], x4[:, t], over(M[("aq", "ak")[w]], 1, HEADS), ALU.mult)
                D_()
                rope(x4[:, :, :, 0:HALF_A], x4[:, :, :, HALF_A:DH], over(ca, 2, HEADS), over(sa, 2, HEADS), r4
                     ).then_inc(qa_rdy, 1)
                D_()
            ci = C["cos_i"].rearrange("p (t f) -> p t f", t=NT)
            si = C["sin_i"].rearrange("p (t f) -> p t f", t=NT)
            xi = pr2[:, :, C_QI:C_QI + 512].rearrange("p t (a f) -> p t a f", a=HEADS)
            i4 = [rot[:, b, 0:512].rearrange("p (t a f) -> p t a f", t=NT, a=HEADS) for b in range(4)]
            rope(xi[:, :, :, 0:16], xi[:, :, :, 16:32], over(ci, 2, HEADS), over(si, 2, HEADS), i4)
            D_()
            xk = pr2[:, :, C_KI:C_KI + 64]
            k4 = [rot[:, b, 0:64].rearrange("p (t f) -> p t f", t=NT) for b in range(4)]
            rope(xk[:, :, 0:16], xk[:, :, 16:32], ci, si, k4)
            D_()
            v.tensor_copy(ki2[:, :, 0:64], xk)
            v.tensor_copy(ki2[:, :, 64:128], xk)
            v.tensor_scalar(wi_s.rearrange("p (t a) -> p t a", t=NT), pr2[:, :, C_WI:C_WI + 8], float((64 * 8) ** -0.5), None, ALU.mult)
            dve.drain().then_inc(qa_rdy, 1)

            def dst2(n):
                return qkaT[:, n // 4, n % 4, :] if n < 8 else qiT[:, n - 8, :] if n < 12 else kiT

            for n in range(1, 13, 2):
                dve.wait_ge(qkaT_done, n + 1)
                v.tensor_copy(dst2(n), bank[n % 4][:, :]).then_inc(qkaT_ev[1], 1)
            for j, (c, n) in enumerate(((C_CQ, Q_LORA), (C_CKV, KV_LORA))):
                x = pr2[:, :, c:c + n]
                sq = xrows[:, 0:NT * n].rearrange("p (t n) -> p t n", t=NT)
                v.tensor_tensor(sq, x, x, ALU.mult)
                D_()
                v.tensor_reduce(mu[:, 0:NT], sq, X, ALU.add)
                D_()
                rsqrt_mean()
                v.tensor_tensor(x, x, over(mu[:, 0:NT], 2, n), ALU.mult).then_inc(lat_rdy, 1)
                D_()
            v.tensor_copy(selbias[:, 0, 0:P], C["chunkbias"][:, S - P:S])
            for u in range(24):
                t, hd = 1 + u // HEADS, u % HEADS
                w = P * (t + 1)
                acc, rel = sS[0][:, 0:w], sP[u % 2][:, 0:w]
                wcol = wi_s[:, t * 8 + hd:t * 8 + hd + 1]
                dve.wait_ge(ix_relu, u + 1)
                if hd == 0:
                    v.tensor_scalar(acc, rel, wcol, None, ALU.mult).then_inc(ix_acc, 1)
                else:
                    v.scalar_tensor_tensor(out=acc, in0=rel, scalar=wcol, in1=acc, op0=ALU.mult, op1=ALU.add
                                           ).then_inc(ix_acc, 1)
                D_()
                if hd == HEADS - 1:
                    v.tensor_tensor(acc, acc, C["chunkbias"][:, S - w:S], ALU.add)
                    D_()
                    for r in range(KEEP // 8):
                        v.max(top8[:, 0:8], acc)
                        D_()
                        v.match_replace(acc, top8[:, 0:8], acc, TAKEN)
                        D_()
                    v.tensor_scalar(selbias[:, t, 0:w], acc, TAKEN / 2, NEG, ALU.is_gt, ALU.mult)
                    D_()
            for k in (1, 3):
                dve.wait_ge(latT_done, k + 1)
                gain = M["bq_lat"][:, k:k + 1] if k < 3 else M["bkv_lat"][:, k - 3:k - 2]
                v.tensor_scalar(lat_cols[:, k, :], bank[k % 4][:, :], gain, None, ALU.mult).then_inc(lat_ev[1], 1)
            for t in range(NT):
                for w, row in enumerate((qrow, krow)):
                    r = row.rearrange("p (a n) -> p a n", a=HEADS)
                    if w == 0:
                        dve.wait_ge(qb_ev, t + 1)
                    else:
                        dve.wait_ge(k_ev, t + 1)
                        v.tensor_copy(r[:, :, 64:96], over(pr2[:, t, C_KR:C_KR + 32], 1, HEADS))
                        D_()
                    sq = scr[:, 0:768].rearrange("p (a n) -> p a n", a=HEADS)
                    v.tensor_tensor(sq, r, r, ALU.mult)
                    D_()
                    v.tensor_reduce(mu[:, 0:8], sq, X, ALU.add)
                    D_()
                    rsqrt_mean()
                    v.tensor_tensor(r, r, over(mu[:, 0:8], 2, DQ_B), ALU.mult)
                    D_()
                    v.tensor_tensor(r, r, over(M[("bq", "bk")[w]], 1, HEADS), ALU.mult)
                    D_()
                    b4 = [scr[:, 768 + b * 128:768 + (b + 1) * 128].rearrange("p (a f) -> p a f", a=HEADS) for b in range(4)]
                    rope(r[:, :, 64:80], r[:, :, 80:96], over(ci[:, t, :], 1, HEADS), over(si[:, t, :], 1, HEADS), b4
                         ).then_inc(qb_rdy, 1)
                    D_()
                for n in (4 * t + 1, 4 * t + 3):
                    dve.wait_ge(qbT_done, n + 1)
                    for a in range(4):
                        hd = 4 + a
                        dst = qbT(hd) if n % 4 == 1 else kbT[:, hd, :]
                        ins = v.tensor_copy(dst[0:DQ_B, t * P:(t + 1) * P], bank[4 + n % 4][0:DQ_B, a * P:(a + 1) * P])
                    ins.then_inc(qbT_ev[1], 1)

            def at_mask(u):
                att, t = u // 32, u // 8 % 4
                w = P * (t + 1)
                dve.wait_ge(at_done, u + 1)
                if u >= 2:
                    dve.wait_ge(at_exp, u - 1)
                bias = selbias[:, t, 0:w] if att == 0 else C["chunkbias"][:, S - w:S]
                v.tensor_tensor_reduce(sS[u % 2][:, 0:w], bank[u % 2][:, 0:w], bias, -float((DH, DQ_B)[att]) ** -0.5, 3e38,
                                       ALU.add, ALU.min, nmax[:, u % 4:u % 4 + 1])
                dve.drain().then_inc(at_s, 1)

            def at_out(g):
                att, t = g // 4, g % 4
                dve.wait_ge(pv_done, 8 * (g + 1))
                r = rs_all[:, 8 * (g % 2):8 * (g % 2) + 8]
                v.reciprocal(var[:, 0:8], r)
                D_()
                c = (C_QA, C_CQ)[att]
                v.tensor_tensor(pr2[:, t, c:c + 512].rearrange("p (a n) -> p a n", a=HEADS),
                                bank[4 + g % 2][:, :].rearrange("p (a n) -> p a n", a=HEADS),
                                over(var[:, 0:8], 2, DH), ALU.mult).then_inc(o_ev, 1)

            for u in range(64):
                at_mask(u)
                if u % 8 == 3 and u > 8:
                    at_out(u // 8 - 1)
            at_out(7)
            for g in range(8):
                att, t = g // 4, g % 4
                c, cg = (C_QA, C_CQ)[att], (C_GA, C_GB)[att]
                ov = pr2[:, t, c:c + 512]
                D_()
                v.tensor_tensor(ov, ov, pr2[:, t, cg:cg + 512], ALU.mult)
                D_()
                dve.wait_ge(gsig2, g + 1)
                v.tensor_tensor(ov, ov, sS[g % 2], ALU.mult).then_inc(mixed, 1)
            for k in range(1, KD, 2):
                dve.wait_ge(mxT_done, k + 1)
                v.tensor_copy(xc[:, k, :], bank[k % 4][:, :]).then_inc(mxT_ev[1], 1)
            for g in range(8):
                n, t = g // 4, g % 4
                hv = h[:, t, n * 512:(n + 1) * 512]
                dve.wait_ge(out_done, g + 1)
                v.tensor_tensor(hv, hv, bank[4 * (n == 0) + t][:, :], ALU.add).then_inc(out_rdy, 1)

        @block.gpsimd
        def _(pool):
            g_ = nc.gpsimd
            D_ = pool.drain
            done = [0]

            def rsqrt_mean(out, sums, n, eps):
                done[0] += 1
                pool.wait_ge(sums_rdy, done[0])
                g_.tensor_scalar(out, sums, 1.0 / n, eps, ALU.mult, ALU.add)
                D_()
                g_.tensor_tensor(out, out, minus_half[:, 0:out.shape[1]], ALU.pow).then_inc(rstd_rdy, 1)

            g_.memset(idx_all, 0).then_inc(place_zero, 1)
            pool.wait_ge(place_zero, 1)
            pool.dma_start(place_dram.rearrange("(p i) o -> p (i o)", p=P), idx_all).then_inc(zero_st, 16)
            g_.memset(minus_half, -0.5)
            g_.memset(uT[:, :, 0:PAD], 0.0)
            g_.memset(yzero, 0.0)
            g_.memset(win[0][:, 0:PAD], 0.0)
            g_.memset(win[1][:, 0:PAD], 0.0)
            D_().then_inc(pad_zero, 1)
            pool.wait_ge(pad_zero, 1)
            pool.dma_start(y_dram[E * P:, :].rearrange("(i p) n -> p i n", p=P),
                           yzero.unsqueeze(1).to_broadcast([P, NITEM - E, D])).then_inc(yzero_st, 16)
            rsqrt_mean(rstd, sumsq, D, EPS1)
            pool.wait_ge(proj_ev, 12)
            pool.wait_ge(cst_ld, 16)
            iw = C["invw"].rearrange("p (g n) -> p g n", g=4)
            for g, w in enumerate(WINDOWS):
                src, step, at = uT[:, g, :], 1, 0
                while step < w:
                    g_.tensor_tensor(win[at][:, PAD:], src[:, PAD:], src[:, PAD - step:PAD + S - step], ALU.add)
                    D_()
                    src, step, at = win[at], 2 * step, 1 - at
                mean = win[at]
                g_.tensor_scalar(mean[:, PAD:], src[:, PAD:], 1.0 / w, None, ALU.mult)
                D_()
                g_.tensor_tensor(mean[:, PAD:2 * PAD], src[:, PAD:2 * PAD], iw[:, g, :], ALU.mult)
                D_()
                g_.tensor_tensor(uT[:, g, PAD:], mean[:, PAD:], uT[:, g, PAD:], ALU.subtract).then_inc(pooled, 1)
                D_()
            for t in range(NT):
                rsqrt_mean(var[:, t * 8:(t + 1) * 8], var[:, t * 8:(t + 1) * 8], DH, EPS1)
            rsqrt_mean(rstd, sumsq, D, EPS1)
            pool.wait_ge(zero_st, 16)
            pool.wait_ge(place_rdy, 1)
            for a in range(16):
                pool.indirect_dma_start(out=place_dram[:, :], out_offset=bass.IndirectOffsetOnAxis(ap=place_u[:, a:a + 1], axis=0),
                                        in_=tok_i[:, a // 4:a // 4 + 1], in_offset=None).then_inc(place_st, 16)
            pool.wait_ge(place_st, 16 * 16)
            pool.dma_start(idx_all, place_dram.rearrange("(p i) o -> p (i o)", p=P)).then_inc(idx_ld, 16)
            pool.wait_ge(idx_ld, 16)
            pool.wait_ge(rows_st, 16)
            pool.wait_ge(gT_ev, 1)
            pool.wait_ge(bd_done, 8)

            def gather(i):
                g_.tensor_copy(idx_cur, idx_all[:, ds(i, 1)])
                D_()
                pool.indirect_dma_start(out=xg, out_offset=None, in_=xn_dram[:, :],
                                        in_offset=bass.IndirectOffsetOnAxis(ap=idx_cur.bitcast(U32), axis=0)
                                        ).then_inc(xg_ld, 16)

            n_it = pool.value_load(n_items[0:1, 0:1], min_val=E, max_val=NITEM - 1)
            gather(0)
            with pool.Fori(1, n_it + 1) as i:
                pool.wait_ge(xgT_done, i)
                pool.wait_ge(xg_ld, 16 * i)
                gather(i)
            pool.wait_ge(p_ld, 16)
            for a in range(16):
                pool.indirect_dma_start(out=ygat[:, a, :], out_offset=None, in_=y_dram[:, :],
                                        in_offset=bass.IndirectOffsetOnAxis(ap=slot_u[:, a:a + 1], axis=0)
                                        ).then_inc(yg_ld[a // 4], 16)
            for eps in (EPS1, EPS1, EPS2):
                rsqrt_mean(rstd, sumsq, D, eps)
            for _ in range(2):
                rsqrt_mean(mu, mu, DH, EPS2)
            for n in (Q_LORA, KV_LORA):
                rsqrt_mean(mu[:, 0:NT], mu[:, 0:NT], n, EPS2)
            for _ in range(2 * NT):
                rsqrt_mean(mu[:, 0:8], mu[:, 0:8], DQ_B, EPS2)


INPUTS = ("x", "p", "positions", "w_in", "w_out", "pool_w", "norm_moe_w", "router_w", "expert_w_gate_up",
          "expert_b_gate_up", "expert_w_down", "expert_b_down", "ple_gate_w", "ple_proj_w", "final_norm_w",
          "w_in_2", "w_uq_2", "w_ukv_2", "w_out_2", "small", "constants")


def kernel(**inputs):
    import concourse.bacc as bacc
    from concourse.bass_utils import run_bass_kernel_spmd

    a = {k: np.asarray(v) for k, v in inputs.items()}

    def cols(v):
        return v.reshape(-1, P).T

    def rows(v):
        return np.broadcast_to(v.reshape(1, -1), (P, v.size))

    small = {"g_mix": cols(a["norm_mix_w"]), "gn_w": cols(a["ret_gn_w"]), "pool_scale": cols(a["pool_scale"]),
             "g_ple": cols(a["norm_ple_w"]), "gain2": cols(a["norm_gain_2"]), "bq_lat": cols(a["b_q_latent_norm_2"]),
             "bkv_lat": cols(a["b_kv_latent_norm_2"]), "router_b": rows(a["router_b"]), "aq": rows(a["a_q_norm_2"]),
             "ak": rows(a["a_k_norm_2"]), "bq": rows(a["b_q_norm_2"]), "bk": rows(a["b_k_norm_2"])}
    one = {k: a[k][0] for k in ("x", "p", "w_in", "w_out", "pool_w", "router_w", "expert_w_gate_up", "expert_b_gate_up",
                                "expert_w_down", "expert_b_down", "ple_gate_w", "ple_proj_w", "w_in_2", "w_uq_2",
                                "w_ukv_2", "w_out_2")}
    one["p"] = one["p"].reshape(S, PLE)
    one["positions"] = a["positions"].reshape(NT, P).T
    one["norm_moe_w"] = a["norm_moe_w"].reshape(D)
    one["final_norm_w"] = a["final_norm_w"]
    one["small"] = np.concatenate([small[k] for k in SMALL.at], axis=1)
    one["constants"] = shape_constants()

    nc = bacc.Bacc("TRN2", target_bir_lowering=False, num_devices=1)
    arrays, args = {}, {}
    for name in INPUTS:
        v = np.ascontiguousarray(one[name])
        arrays["in_" + name] = v
        args[name] = nc.dram_tensor("in_" + name, v.shape, mybir.dt.from_np(v.dtype), kind="ExternalInput").ap()
    args["out"] = nc.dram_tensor("out_rows", (S, D), F32, kind="ExternalOutput").ap()
    build_program(nc, args)
    r = run_bass_kernel_spmd(nc, [arrays], core_ids=[0])
    return r.results[0]["out_rows"].reshape(1, S, D)
```

```python
from contextlib import ExitStack

import numpy as np

import concourse.bass as bass
from concourse import mybir

F32 = mybir.dt.float32
F32R = mybir.dt.float32r
BF16 = mybir.dt.bfloat16
I32 = mybir.dt.int32
U32 = mybir.dt.uint32
ALU = mybir.AluOpType
ACT = mybir.ActivationFunctionType
X = mybir.AxisListType.X
ds = bass.ds

P = 128
S, D = 512, 1024
NT = S // P
KD = D // P
HEADS, DH = 8, 64
D_RET = HEADS * DH
WINDOWS = (2, 4, 8, 16)
PAD = max(WINDOWS)
E, TOPK = 32, 4
D_E = 1024
LIMIT, ALPHA = 7.0, 1.702
PLE = 256
NITEM = 48
EPS1, EPS2 = 1e-5, 1e-6
NEG = -1e30
TAKEN = -3e38
KEEP = 128
Q_LORA, KV_LORA = 384, 256
DQ_B, D_ROPE_B = 96, 32
HALF_A, HALF_I = DH // 2, 16
C_QA, C_KA, C_VA, C_GA, C_QI = 0, 512, 1024, 1536, 2048
C_KI, C_WI, C_CQ, C_CKV, C_KR, C_GB = 2560, 2624, 2632, 3016, 3272, 3304
D_IN2 = 3816
NCH2 = -(-D_IN2 // 512)
IN2_ORDER = (4, 5, 0, 1, 6, 2, 3, 7)
INDEX_TURN = (2, 1)
INDEX_SCORES = ((2, 2), (2, 3), (3, 0), (3, 1), (3, 2), (3, 3))
T_IX, T_QA, T_KA, T_LAT, T_B = 0, 5, 9, 13, 18
TWO_PI = 2 * np.pi
PI_A = 6.28125
PI_B = float(np.float32(np.floor((TWO_PI - PI_A) * 2 ** 21) / 2 ** 21))
PI_C = float(np.float32(TWO_PI - PI_A - PI_B))
ROUND = 12582912.0


class Cols:

    def __init__(self, **widths):
        self.at, self.n = {}, 0
        for name, w in widths.items():
            self.at[name] = (self.n, self.n + w)
            self.n += w


CONST = Cols(ident=P, causal=S, ustrict=P, ones=P, chunkbias=S, cos_a=NT * HALF_A, sin_a=NT * HALF_A,
             cos_i=NT * HALF_I, sin_i=NT * HALF_I, gq=NT * HEADS, gk=NT * HEADS, invw=4 * PAD,
             invfreq=HALF_A, iota32=E, iota48=NITEM, pmod=1, tok=NT)
SMALL = Cols(g_mix=KD, gn_w=4, pool_scale=4, g_ple=KD, gain2=KD, bq_lat=3, bkv_lat=2, router_b=E,
             aq=DH, ak=DH, bq=DQ_B, bk=DQ_B)


def shape_constants():
    c = {}
    p = np.arange(P)
    tok = np.arange(NT)[None, :] * P + p[:, None]
    c["ident"] = np.eye(P)
    c["causal"] = np.concatenate([(p[None, :] >= p[:, None]), np.ones((P, S - P))], 1)
    c["ustrict"] = p[:, None] < p[None, :]
    c["ones"] = np.ones((P, P))
    last = np.where((p[:, None] < 64) & (p[None, :] >= 64), NEG, 0.0)
    c["chunkbias"] = np.concatenate([np.zeros((P, S - P)), last], 1)
    f32 = np.float32
    for name, half in (("a", HALF_A), ("i", HALF_I)):
        freq = np.power(f32(10000.0), -np.arange(half, dtype=f32) * f32(2.0) / f32(2 * half)).astype(f32)
        ang = (tok[:, :, None].astype(f32) * freq[None, None, :]).astype(f32).astype(np.float64)
        c["cos_" + name], c["sin_" + name] = np.cos(ang), np.sin(ang)
    lg = np.log1p(-np.power(2.0, -5.0 - np.arange(HEADS)))
    c["gq"] = np.exp(tok[:, :, None] * lg)
    c["gk"] = np.exp(-tok[:, :, None] * lg) * DH ** -0.5
    c["invw"] = np.broadcast_to(np.stack([1.0 / np.minimum(np.arange(PAD) + 1.0, w) for w in WINDOWS])[None],
                                (P, 4, PAD))
    c["invfreq"] = np.broadcast_to(np.power(f32(10000.0), -np.arange(HALF_A, dtype=f32) / f32(HALF_A))[None],
                                   (P, HALF_A))
    c["iota32"] = np.broadcast_to(np.arange(E)[None], (P, E))
    c["iota48"] = np.broadcast_to(np.arange(NITEM)[None], (P, NITEM))
    c["pmod"] = (p % E)[:, None]
    c["tok"] = tok
    return np.concatenate([np.asarray(c[k], np.float64).reshape(P, -1) for k in CONST.at], 1).astype(np.float32)


def build_program(nc, d):
    ctx = ExitStack()
    with ctx:
        def sb(name, shape, dt=F32):
            return ctx.enter_context(nc.sbuf_tensor("sb_" + name, shape, dt))

        def sem(name):
            return ctx.enter_context(nc.semaphore(name))

        def dram(name, shape, dt=F32):
            return nc.dram_tensor("scratch_" + name, shape, dt, kind="Internal").ap()

        ring = sb("ring", [P, 12 * 2048])
        wbuf_at = nc.sbuf_base
        wbuf = sb("wbuf", [P, 2, KD * 512])
        h = sb("h", [P, NT, D])
        xcols_at = nc.sbuf_base
        xcols = sb("xcols", [P, KD * S])
        xrows = sb("xrows", [P, NT * D])
        scr_at = nc.sbuf_base
        scr = sb("scr", [P, 3072])
        cst = sb("cst", [P, CONST.n])
        sml = sb("sml", [P, SMALL.n])
        grow = sb("grow", [P, D])
        rw = sb("rw", [P, KD, E])
        sel_e = sb("sel_e", [96, P], BF16)
        st = sb("st", [P, 512])
        bank = [ctx.enter_context(nc.psum_tensor(f"bank{i}", [P, 512], F32)) for i in range(8)]

        C = {k: cst[:, a:b] for k, (a, b) in CONST.at.items()}
        M = {k: sml[:, a:b] for k, (a, b) in SMALL.at.items()}
        ident = C["ident"]
        xc = xcols[:, :].rearrange("p (k s) -> p k s", k=KD)
        xr = xrows[:, :].rearrange("p (t n) -> p t n", t=NT)

        taken = [0]

        def stat(n, dt=F32):
            a = taken[0]
            taken[0] += n
            assert taken[0] <= 512
            v = st[:, a:a + n]
            return v if dt == F32 else v.bitcast(dt)

        sumsq = stat(NT)
        rstd = stat(NT)
        posf = stat(NT)
        posi = stat(NT, I32)
        mu = stat(HEADS * NT)
        var = stat(HEADS * NT)
        gates = stat(16)
        gsum = stat(NT)
        negv0 = stat(NT)
        slot_u = stat(16, U32)
        place_u = stat(16, U32)
        tok_i = stat(NT, I32)
        item_e = stat(NITEM)
        item_ei = stat(NITEM, I32)
        last_item = stat(1, I32)
        idx_cur = stat(1, I32)
        idx_all = stat(NITEM, I32)
        nmax = stat(4)
        rs_all = stat(16)
        minus_half = stat(HEADS * NT)
        wi_s = stat(NT * HEADS)
        top8 = stat(NT * 8)
        idx8 = stat(NT * 8, U32)

        proj = ring[:, 0:8192].rearrange("p (t n) -> p t n", t=NT)
        tmp4 = ring[:, 8192:12288].rearrange("p (b n) -> p b n", b=4)
        qkT = ring[:, 12288:16384].rearrange("p (w a s) -> p w a s", w=2, a=4)
        scT = ring[:, 16384:20480].rearrange("p (b j s) -> p b j s", b=2, j=NT)
        uT = ring[:, 20480:22592].rearrange("p (g s) -> p g s", g=4)
        win = [ring[:, 22592 + i * 528:22592 + (i + 1) * 528] for i in range(2)]
        poolw = ring[:, 23648:24160].rearrange("p (g n) -> p g n", g=4)
        cos1 = scr[:, 0:128].rearrange("p (t f) -> p t f", t=NT)
        sin1 = scr[:, 128:256].rearrange("p (t f) -> p t f", t=NT)
        ang = scr[:, 256:384]
        turns = scr[:, 384:512]
        ctmp = scr[:, 512:640]
        yzero = scr[:, 1024:1024 + D]

        onehot = scr[:, 0:512].rearrange("p (a e) -> p a e", e=E)
        prod = scr[:, 512:1024].rearrange("p (a e) -> p a e", e=E)
        cmp48 = scr[:, 1024:1024 + NITEM * E].rearrange("p (i e) -> p i e", e=E)
        route = scr[:, 2560:3072]
        logits = route[:, 0:128].rearrange("p (t e) -> p t e", e=E)
        member = route[:, 128:256].rearrange("p (t e) -> p t e", e=E)
        gdense = route[:, 256:384].rearrange("p (t e) -> p t e", e=E)
        nblk, incl, base = route[:, 384:416], route[:, 416:448], route[:, 448:480]
        more = route[:, 480:512]
        gT = xrows[0:E, 0:S]
        bdown = wbuf[0:E, 0, 3072:4096]
        braw = wbuf[0:E, 0, 0:2048]
        bparts = grow[0:96, :].bitcast(BF16)
        bpart2 = scr[0:E, 0:1024].bitcast(BF16)
        bpart3 = scr[0:E, 1024:2048].bitcast(BF16)
        gu_w = [ring[:, c * 2048:(c + 1) * 2048] for c in range(8)]
        dn_w = [ring[:, 16384 + c * 2048:16384 + (c + 1) * 2048].rearrange("p (j n) -> p j n", j=2) for c in range(4)]
        xg, gate_s, up_s, sig_s = (xrows[:, i * 1024:(i + 1) * 1024] for i in range(4))
        y_s = scr[:, 2048:3072]

        def part(name, n, at, words):
            return nc.alloc_sbuf_tensor_at("sb_" + name, [P, n], F32R, offset=at + 4 * words)

        w_hi = [part("w_hi0", 2048, wbuf_at, 0), part("w_hi1", 2048, wbuf_at, 2048), part("w_hi2", 2048, xcols_at, 2048)]
        w_lo = [part("w_lo0", 2048, wbuf_at, 4096), part("w_lo1", 2048, wbuf_at, 6144)]
        xgT_hi, xgT_lo = part("xgT_hi", 1024, xcols_at, 0), part("xgT_lo", 1024, xcols_at, 1024)
        actT_hi, actT_lo = part("actT_hi", 1024, scr_at, 0), part("actT_lo", 1024, scr_at, 1024)

        ygat = ring[:, 0:16384].rearrange("p (a n) -> p a n", a=16)
        p_rows = ring[:, 16384:17408].rearrange("p (t n) -> p t n", t=NT)
        p_cols = ring[:, 17408:18432].rearrange("p (k s) -> p k s", k=2)
        plew = ring[:, 18432:20480].rearrange("p (k n) -> p k n", k=2)
        sig2 = ring[:, 20480:24576].rearrange("p (b n) -> p b n", b=8)

        pr2 = ring[:, 0:NT * D_IN2].rearrange("p (t n) -> p t n", t=NT)
        o2 = NT * D_IN2
        qkaT = ring[:, o2:o2 + 4096].rearrange("p (w a s) -> p w a s", w=2, a=4)
        qiT = ring[:, o2 + 4096:o2 + 6144].rearrange("p (a s) -> p a s", a=4)
        kiT = ring[:, o2 + 6144:o2 + 6656]
        selbias = ring[:, o2 + 6656:o2 + 8704].rearrange("p (t s) -> p t s", t=NT)
        ki2 = ring[:, o2 + 8704:o2 + 8704 + 512].rearrange("p (t n) -> p t n", t=NT)
        rot = xrows[:, :].rearrange("p (b n) -> p b n", b=4)
        lat_cols = xcols[:, 0:5 * S].rearrange("p (k s) -> p k s", k=5)
        qrow = xcols[:, 5 * S:5 * S + 768]
        krow = xcols[:, 5 * S + 768:5 * S + 1536]
        kbT = xrows[:, :].rearrange("p (a s) -> p a s", a=HEADS)
        sS = [scr[:, i * 512:(i + 1) * 512] for i in range(2)]
        index_acc = [scr[:, i * 512:(i + 1) * 512] for i in (0, 1, 4)]
        bsq = grow[:, 0:HEADS * DQ_B].rearrange("p (a n) -> p a n", a=HEADS)
        brot = [kiT[:, b * 128:(b + 1) * 128].rearrange("p (a f) -> p a f", a=HEADS) for b in range(4)]
        sP = [scr[:, 1024 + i * 512:1024 + (i + 1) * 512] for i in range(2)]
        sPT = [scr[:, 2048 + i * 512:2048 + (i + 1) * 512].rearrange("p (j n) -> p j n", j=NT) for i in range(2)]

        def qbT(hd):
            return pr2[:, hd, C_KA:C_KA + S] if hd < 4 else qiT[:, hd - 4, :]

        xn_dram = dram("rows", [S, D])
        place_dram = dram("place", [P * NITEM, 1], I32)
        y_dram = dram("y", [NITEM * P, D])

        yzero_st = sem("yzero_st")
        sums_rdy = sem("sums_rdy")
        rstd_rdy = sem("rstd_rdy")
        cst_ld = sem("cst_ld")
        x_ld = sem("x_ld")
        small_ld = sem("small_ld")
        poolw_ld = sem("poolw_ld")
        trig_in = sem("trig_in")
        trig_out = sem("trig_out")
        silu_sig = sem("silu_sig")
        proj_done = sem("proj_done")
        proj_ev = sem("proj_ev")
        gate_ev = sem("gate_ev")
        rope_done = sem("rope_done")
        qkT_done = sem("qkT_done")
        qkT_ev = sem("qkT_ev")
        pad_zero = sem("pad_zero")
        pooled = sem("pooled")
        mixg_done = sem("mixg_done")
        mixg_ev = sem("mixg_ev")
        sc_done = sem("sc_done")
        sc_ev = sem("sc_ev")
        y1_done = sem("y1_done")
        ret_rows = sem("ret_rows")
        retT_done = sem("retT_done")
        wo_done = sem("wo_done")
        wo_ev = sem("wo_ev")
        rows_st = sem("rows_st")
        lg_done = sem("lg_done")
        gexp_in = sem("gexp_in")
        gexp = sem("gexp")
        member_rdy = sem("member_rdy")
        gd_rdy = sem("gd_rdy")
        rank_done = sem("rank_done")
        gT_done = sem("gT_done")
        gT_ev = sem("gT_ev")
        bd_ld = sem("bd_ld")
        bd_done = sem("bd_done")
        bd_ev = sem("bd_ev")
        braw_ld = sem("braw_ld")
        bsplit = sem("bsplit")
        bp_ld = sem("bp_ld")
        place_rdy = sem("place_rdy")
        place_zero = sem("place_zero")
        zero_st = sem("zero_st")
        place_st = sem("place_st")
        idx_ld = sem("idx_ld")
        item_rdy = sem("item_rdy")
        w_hi_rdy = sem("w_hi_rdy")
        w_lo_rdy = sem("w_lo_rdy")
        w_used = sem("w_used")
        xgT_hi_ev = sem("xgT_hi_ev")
        actT_hi_ev = sem("actT_hi_ev")
        xg_ld = sem("xg_ld")
        xgT_done = sem("xgT_done")
        xgT_ev = sem("xgT_ev")
        gu_done = sem("gu_done")
        gu_ev = sem("gu_ev")
        g_rdy = sem("g_rdy")
        sig_rdy = sem("sig_rdy")
        act_rdy = sem("act_rdy")
        actT_done = sem("actT_done")
        actT_ev = sem("actT_ev")
        y_free = sem("y_free")
        y_st = sem("y_st")
        sel_rdy = sem("sel_rdy")
        combined = sem("combined")
        p_ld = sem("p_ld")
        plew_ld = sem("plew_ld")
        pT_done = sem("pT_done")
        pT_ev = sem("pT_ev")
        plg_done = sem("plg_done")
        plp_done = sem("plp_done")
        plg_sig = sem("plg_sig")
        ple_ev = sem("ple_ev")
        final_rdy = sem("final_rdy")
        pr2_done = sem("pr2_done")
        pr2_ev = sem("pr2_ev")
        ix_rdy = sem("ix_rdy")
        turn_done = sem("turn_done")
        turn_ev = sem("turn_ev")
        y_all = sem("y_all")
        qa_rdy = sem("qa_rdy")
        ix_done = sem("ix_done")
        ix_relu = sem("ix_relu")
        ix_acc = sem("ix_acc")
        lat_rdy = sem("lat_rdy")
        qb_done = sem("qb_done")
        qb_ev = sem("qb_ev")
        kv_done = sem("kv_done")
        k_ev = sem("k_ev")
        qb_rdy = sem("qb_rdy")
        at_done = sem("at_done")
        at_s = sem("at_s")
        at_exp = sem("at_exp")
        pT2_done = sem("pT2_done")
        pT2_ev = sem("pT2_ev")
        pv_done = sem("pv_done")
        o_ev = sem("o_ev")
        gsig2 = sem("gsig2")
        mixed = sem("mixed")
        mxT_done = sem("mxT_done")
        out_done = sem("out_done")
        out_rdy = sem("out_rdy")
        out_st = sem("out_st")
        grow_ld = sem("grow_ld")
        grow2_ld = sem("grow2_ld")
        rw_ld = sem("rw_ld")
        norm_sq = sem("norm_sq")
        norm_rows = sem("norm_rows")
        norm_T = sem("norm_T")
        w_ld = [sem(f"w_ld{i}") for i in range(2)]
        retT_ev = [sem(f"retT_ev{i}") for i in range(2)]
        mxT_ev = [sem(f"mxT_ev{i}") for i in range(2)]
        yg_ld = [sem(f"yg_ld{i}") for i in range(4)]
        gu_ld = [sem(f"gu_ld{i}") for i in range(8)]
        dn_ld = [sem(f"dn_ld{i}") for i in range(4)]
        norm_cols = [sem(f"norm_cols{i}") for i in range(2)]
        NORM = {"mix": 0, "moe": 1, "ple": 2, "two": 3}
        SQ = {"mix": 0, "moe": 1, "ple": 2, "fin": 3, "two": 4}

        block = ctx.enter_context(nc.Block())

        def in_cols(ap, n, w=512):
            return ap[:, n * 512:n * 512 + w].rearrange("(k p) n -> p k n", p=P)

        IN_ORDER = (0, 1, 4, 2, 3)
        chunks = [(in_cols(d["w_in"], n), 8, 512) for n in IN_ORDER]
        chunks += [(in_cols(d["w_out"], n), 8, 512) for n in range(2)]
        L_PLE = len(chunks)
        chunks += [(in_cols(d["ple_gate_w"], n), 8, 512) for n in range(2)]
        L_IN2 = len(chunks)
        for n in IN2_ORDER:
            w = min(512, D_IN2 - n * 512)
            chunks.append((in_cols(d["w_in_2"], n, w), 8, w))
        L_UQ = len(chunks)
        chunks.append((d["w_uq_2"].rearrange("(k p) n -> p k n", p=P), 3, HEADS * DQ_B))
        chunks.append((d["w_ukv_2"].rearrange("(k p) n -> p k n", p=P), 2, D))
        L_OUT2 = len(chunks)
        chunks += [(in_cols(d["w_out_2"], n), 8, 512) for n in range(2)]

        def chunk_used(L):
            if L < 5:
                return proj_done, 4 * (L + 1)
            if L < L_PLE:
                return wo_done, 4 * (L - 4)
            if L < L_IN2:
                return plp_done, 4 * (L - L_PLE + 1)
            if L < L_UQ:
                return pr2_done, 4 * (L - L_IN2 + 1)
            return (qb_done if L == L_UQ else kv_done), NT

        def wview(L):
            _, k, w = chunks[L]
            return wbuf[:, L % 2, 0:k * w].rearrange("p (k n) -> p k n", k=k)

        @block.sync
        def _(sp):
            def load_chunk(L):
                if L >= 2:
                    used, n = chunk_used(L - 2)
                    sp.wait_ge(used, n)
                sp.dma_start(wview(L), chunks[L][0]).then_inc(w_ld[L % 2], 16)

            for L in range(L_PLE):
                load_chunk(L)
            sp.wait_ge(wo_done, 2 * NT)
            sp.dma_start(braw, d["expert_b_gate_up"]).then_inc(braw_ld, 16)
            sp.dma_start(bdown, d["expert_b_down"]).then_inc(bd_ld, 16)

            def load_gu(e, c):
                sp.dma_start(gu_w[c], d["expert_w_gate_up"][ds(e, 1), c * P:(c + 1) * P, :].rearrange("o p n -> p (o n)")
                             ).then_inc(gu_ld[c], 16)

            def load_dn(e, c):
                sp.dma_start(dn_w[c], d["expert_w_down"][ds(e, 1), c * 256:(c + 1) * 256, :]
                             .rearrange("o (j p) n -> p (o j) n", p=P)).then_inc(dn_ld[c], 16)

            sp.wait_ge(wo_ev, 8)
            for c in range(8):
                load_gu(0, c)
            for c in range(4):
                load_dn(0, c)
            sp.wait_ge(item_rdy, 1)
            last = sp.value_load(last_item[0:1, 0:1], min_val=E - 1, max_val=NITEM - 2)
            e1 = sp.value_load(item_ei[0:1, 1:2], min_val=0, max_val=E - 1)
            for c in range(8):
                sp.wait_ge(w_lo_rdy, c + 1)
                load_gu(e1, c)
            with sp.Fori(1, last) as i:
                e_next = sp.value_load(item_ei[0:1, ds(i + 1, 1)], min_val=0, max_val=E - 1)
                for c in range(8):
                    sp.wait_ge(w_lo_rdy, 12 * i + (c - 3))
                    load_gu(e_next, c)
                e = sp.value_load(item_ei[0:1, ds(i, 1)], min_val=0, max_val=E - 1)
                for c in range(4):
                    sp.wait_ge(w_lo_rdy, 12 * i + (c + 5))
                    load_dn(e, c)
            e_last = sp.value_load(item_ei[0:1, ds(last, 1)], min_val=0, max_val=E - 1)
            for c in range(4):
                sp.wait_ge(w_lo_rdy, 12 * last + (c + 5))
                load_dn(e_last, c)
            sp.wait_ge(w_lo_rdy, 12 * last + 10)
            sp.dma_start(p_rows, d["p"].rearrange("(t p) n -> p t n", p=P)).then_inc(p_ld, 16)
            sp.dma_start(plew, d["ple_proj_w"].rearrange("(k p) n -> p k n", p=P)).then_inc(plew_ld, 16)
            sp.wait_ge(w_used, 12 * last + 12)
            sp.wait_ge(yg_ld[NT - 1], 16 * TOPK)
            load_chunk(L_PLE)
            load_chunk(L_PLE + 1)
            for L in range(L_IN2, len(chunks)):
                load_chunk(L)

        @block.tensor
        def _(pe):
            def norm_to_cols(n, src):
                pe.wait_ge(norm_rows, NT * (NORM[n] + 1))
                for k in range(KD):
                    b = bank[4 + k % 4]
                    if k >= 4:
                        pe.wait_ge(norm_cols[k % 2], 4 * NORM[n] + (k - 4) // 2 + 1)
                    for t in range(NT):
                        mm = pe.transpose(b[:, t * P:(t + 1) * P], src[:, t, k * P:(k + 1) * P], ident)
                    mm.then_inc(norm_T, 1)

            def cols_ready(n):
                pe.wait_ge(norm_cols[0], 4 * (NORM[n] + 1))
                pe.wait_ge(norm_cols[1], 4 * (NORM[n] + 1))

            def chunk_ready(L):
                pe.wait_ge(w_ld[L % 2], 16 * (L // 2 + 1))

            def dense_rows(L, lhs, t, b, cols=None):
                wv = wview(L)
                k_n, w = wv.shape[1], wv.shape[2]
                a, z = cols or (0, w)
                for k in range(k_n):
                    mm = pe.matmul(b[:, 0:z - a], lhs[:, k, t * P:(t + 1) * P], wv[:, k, a:z],
                                   start=(k == 0), stop=(k == k_n - 1))
                return mm

            pe.wait_ge(cst_ld, 16)
            norm_to_cols("mix", xr)
            cols_ready("mix")
            for j, n in enumerate(IN_ORDER):
                chunk_ready(j)
                for t in range(NT):
                    g = 4 * j + t
                    if g >= 4:
                        pe.wait_ge(proj_ev, g - 3)
                    b = bank[g % 4]
                    if n < 4:
                        mm = dense_rows(j, xc, t, b)
                    else:
                        wv = wview(j)
                        for k in range(KD):
                            mm = pe.matmul(b[:, :], wv[:, k, t * P:(t + 1) * P], xc[:, k, :],
                                           start=(k == 0), stop=(k == KD - 1))
                    mm.then_inc(proj_done, 1)
            pe.wait_ge(poolw_ld, 16)
            for g in range(4):
                pe.wait_ge(pooled, g + 1)
                pe.matmul(bank[4 + g][:, :], poolw[:, g, :], uT[:, g, PAD:], start=True, stop=True
                          ).then_inc(mixg_done, 1)
            pe.wait_ge(gate_ev, 4)
            for w in range(2):
                pe.wait_ge(rope_done, w + 1)
                for a in range(4):
                    if w == 1:
                        pe.wait_ge(qkT_ev, a + 1)
                    for t in range(NT):
                        mm = pe.transpose(bank[a][:, t * P:(t + 1) * P], proj[:, t, w * D_RET + a * P:w * D_RET + (a + 1) * P], ident)
                    mm.then_inc(qkT_done, 1)
            pe.wait_ge(mixg_ev, 4)

            def scores(hd):
                a, lo = hd // 2, 64 * (hd % 2)
                for j in range(NT):
                    n = 4 * hd + j
                    if n >= 4:
                        pe.wait_ge(sc_ev, n - 3)
                    pe.matmul(bank[j][:, 0:S - j * P], qkT[lo:lo + 64, 1, a, j * P:(j + 1) * P],
                              qkT[lo:lo + 64, 0, a, j * P:S], start=True, stop=True).then_inc(sc_done, 1)

            def values(hd):
                pe.wait_ge(sc_ev, 4 * hd + 4)
                for i in range(NT):
                    for j in range(i + 1):
                        mm = pe.matmul(bank[4 + i][:, hd * DH:(hd + 1) * DH], scT[:, hd % 2, j, i * P:(i + 1) * P],
                                       proj[:, j, 2 * D_RET + hd * DH:2 * D_RET + (hd + 1) * DH],
                                       start=(j == 0), stop=(j == i))
                return mm

            pe.wait_ge(qkT_ev, 8)
            for hd in range(HEADS):
                scores(hd)
                if hd:
                    values(hd - 1)
            values(HEADS - 1).then_inc(y1_done, 1)
            pe.wait_ge(sc_ev, 32)
            for k in range(4):
                for t in range(NT):
                    pe.wait_ge(ret_rows, t + 1)
                    mm = pe.transpose(bank[k][:, t * P:(t + 1) * P], xr[:, t, 512 + k * P:512 + (k + 1) * P], ident)
                mm.then_inc(retT_done, 1)
            pe.wait_ge(retT_ev[0], 2)
            pe.wait_ge(retT_ev[1], 2)
            for n in range(2):
                chunk_ready(5 + n)
                for t in range(NT):
                    if n:
                        pe.wait_ge(wo_ev, t + 1)
                    dense_rows(5 + n, xc, t, bank[t]).then_inc(wo_done, 1)

            norm_to_cols("moe", xr)
            cols_ready("moe")
            pe.wait_ge(rw_ld, 16)
            pe.wait_ge(wo_ev, 8)
            for t in range(NT):
                for k in range(KD):
                    mm = pe.matmul(bank[0][:, t * E:(t + 1) * E], xc[:, k, t * P:(t + 1) * P], rw[:, k, :],
                                   start=(k == 0), stop=(k == KD - 1))
            mm.then_inc(lg_done, 1)
            pe.wait_ge(member_rdy, 1)
            for t in range(NT):
                for j in range(t + 1):
                    pe.matmul(bank[1][:, t * E:(t + 1) * E], C["ustrict"] if j == t else C["ones"], member[:, j, :],
                              start=(j == 0), stop=(j == t))
            for j in range(NT):
                mm = pe.matmul(bank[2][:, 0:E], C["ones"], member[:, j, :], start=(j == 0), stop=(j == NT - 1))
            mm.then_inc(rank_done, 1)
            pe.wait_ge(gd_rdy, 1)
            for t in range(NT):
                mm = pe.transpose(bank[3][0:E, t * P:(t + 1) * P], gdense[:, t, :], ident)
            mm.then_inc(gT_done, 1)
            pe.wait_ge(gT_ev, 1)
            pe.wait_ge(bd_ld, 16)
            for n in range(2):
                for t in range(NT):
                    if n:
                        pe.wait_ge(bd_ev, t + 1)
                    pe.matmul(bank[4 + t][:, :], gT[:, t * P:(t + 1) * P], bdown[:, n * 512:(n + 1) * 512],
                              start=True, stop=True).then_inc(bd_done, 1)

            def item_T(i):
                pe.wait_ge(xg_ld, 16 * i + 16)
                for k in range(KD):
                    mm = pe.transpose(bank[6 + k // 4][:, k % 4 * P:(k % 4 + 1) * P], xg[:, k * P:(k + 1) * P], ident)
                mm.then_inc(xgT_done, 1)

            def act_T(i):
                pe.wait_ge(act_rdy, i + 1)
                for k in range(KD):
                    mm = pe.transpose(bank[6 + k // 4][:, k % 4 * P:(k % 4 + 1) * P], up_s[:, k * P:(k + 1) * P], ident)
                mm.then_inc(actT_done, 1)

            def three_passes(outs, hi, lo, w_h, w_l, first, last):
                for a, w, start, stop in ((hi, w_h, first, False), (hi, w_l, False, False), (lo, w_h, False, last)):
                    for n, b in enumerate(outs):
                        mm = pe.matmul(b[:, :], a, w[:, n * 512:(n + 1) * 512], start=start, stop=stop)
                return mm

            def gate_up(i, m, turn, mid=None):
                pe.wait_ge(xgT_ev, i + 1)
                for c in range(KD):
                    pe.wait_ge(w_lo_rdy, m + (c + 1))
                    three_passes(bank[0:4], xgT_hi[:, c * P:(c + 1) * P], xgT_lo[:, c * P:(c + 1) * P],
                                 w_hi[(c + turn) % 3], w_lo[c % 2], c == 0, False).then_inc(w_used, 1)
                    if c == 3 and mid:
                        mid()
                pe.wait_ge(sel_rdy, i + 1)
                for n in range(4):
                    mm = pe.matmul(bank[n][:, :], sel_e[:, :], bparts[:, n * 512:(n + 1) * 512], start=False, stop=True)
                mm.then_inc(gu_done, 1)

            def down(i, m, turn):
                pe.wait_ge(actT_ev, i + 1)
                pe.wait_ge(y_free, i + 1)
                for c in range(4):
                    pe.wait_ge(w_lo_rdy, m + (c + 1))
                    for j in range(2):
                        k = 2 * c + j
                        mm = three_passes(bank[4:6], actT_hi[:, k * P:(k + 1) * P], actT_lo[:, k * P:(k + 1) * P],
                                          w_hi[(c + turn) % 3][:, j * D:(j + 1) * D], w_lo[c % 2][:, j * D:(j + 1) * D],
                                          k == 0, k == KD - 1)
                    mm.then_inc(w_used, 1)

            pe.wait_ge(bd_ev, 8)
            pe.wait_ge(place_rdy, 1)
            last = pe.value_load(last_item[0:1, 0:1], min_val=E - 1, max_val=NITEM - 2)
            item_T(0)
            pe.wait_ge(bp_ld, 32)
            pe.wait_ge(bsplit, 3)
            gate_up(0, 0, 0)
            item_T(1)
            with pe.Fori(1, last + 1) as i:
                pe.wait_ge(gu_ev, i)
                gate_up(i, 12 * i - 4, 2, lambda: act_T(i - 1))
                pe.wait_ge(actT_ev, i)
                item_T(i + 1)
                down(i - 1, 12 * i + 4, 1)
            pe.wait_ge(xgT_ev, last + 2)
            act_T(last)
            down(last, 12 * last + 8, 2)

            pe.wait_ge(p_ld, 16)
            pe.wait_ge(gu_ev, last + 1)
            for k in range(2):
                for t in range(NT):
                    mm = pe.transpose(bank[k][:, t * P:(t + 1) * P], p_rows[:, t, k * P:(k + 1) * P], ident)
                mm.then_inc(pT_done, 1)
            pe.wait_ge(y_free, last + 2)
            pe.wait_ge(xgT_ev, last + 2)
            norm_to_cols("ple", xr)
            cols_ready("ple")
            pe.wait_ge(pT_ev, 2)
            pe.wait_ge(plew_ld, 16)
            for n in range(2):
                chunk_ready(L_PLE + n)
                for t in range(NT):
                    g = 4 * n + t
                    if g >= 2:
                        pe.wait_ge(ple_ev, g - 1)
                    dense_rows(L_PLE + n, xc, t, bank[2 * (g % 2)]).then_inc(plg_done, 1)
                    for k in range(2):
                        mm = pe.matmul(bank[2 * (g % 2) + 1][:, :], p_cols[:, k, t * P:(t + 1) * P],
                                       plew[:, k, n * 512:(n + 1) * 512], start=(k == 0), stop=(k == 1))
                    mm.then_inc(plp_done, 1)

            norm_to_cols("two", xr)
            cols_ready("two")
            pe.wait_ge(ple_ev, 8)

            def turn(n, blk):
                b = bank[2 + n % 2]
                if n >= 2:
                    pe.wait_ge(turn_ev, n - 1)
                for t in range(NT):
                    mm = pe.transpose(b[:, t * P:(t + 1) * P], blk[:, t, :], ident)
                mm.then_inc(turn_done, 1)

            def index_scores(q):
                for u in range(4 * q, 4 * q + 4):
                    t, hd = 1 + u // HEADS, u % HEADS
                    lo = 64 * (hd % 2)
                    if u >= 4:
                        pe.wait_ge(ix_relu, u - 3)
                    pe.matmul(bank[4 + u % 4][:, 0:P * (t + 1)], qiT[lo:lo + 64, hd // 2, t * P:(t + 1) * P],
                              kiT[lo:lo + 64, 0:P * (t + 1)], start=True, stop=True).then_inc(ix_done, 1)

            for j in range(NCH2):
                chunk_ready(L_IN2 + j)
                for t in range(NT):
                    g = 4 * j + t
                    if g >= 2:
                        pe.wait_ge(pr2_ev, g - 1)
                    dense_rows(L_IN2 + j, xc, t, bank[g % 2]).then_inc(pr2_done, 1)
                    if (j, t) == INDEX_TURN:
                        pe.wait_ge(ix_rdy, 1)
                        for b in range(4):
                            turn(T_IX + b, pr2[:, :, C_QI + b * P:C_QI + (b + 1) * P])
                        turn(T_IX + 4, ki2)
                    if (j, t) in INDEX_SCORES:
                        pe.wait_ge(turn_ev, T_IX + 5)
                        index_scores(INDEX_SCORES.index((j, t)))
            for w in range(2):
                pe.wait_ge(qa_rdy, w + 1)
                for b in range(4):
                    turn((T_QA, T_KA)[w] + b, pr2[:, :, w * 512 + b * P:w * 512 + (b + 1) * P])
            pe.wait_ge(lat_rdy, 2)
            for b in range(5):
                turn(T_LAT + b, pr2[:, :, C_CQ + b * P:C_CQ + (b + 1) * P])
            pe.wait_ge(turn_ev, T_B)
            pe.wait_ge(pr2_ev, 4 * NCH2)
            pe.wait_ge(ix_relu, 24)
            chunk_ready(L_UQ)
            chunk_ready(L_UQ + 1)

            def turn_heads(t, w):
                pe.wait_ge(qb_rdy, 2 * t + w + 1)
                pe.wait_ge(k_ev, t + 1)
                for half in range(2):
                    n = T_B + 4 * t + 2 * w + half
                    pe.wait_ge(turn_ev, n - 1)
                    for a in range(4):
                        hd = 4 * half + a
                        mm = pe.transpose(bank[6 + half][0:DQ_B, a * P:(a + 1) * P],
                                          (qrow, krow)[w][:, hd * DQ_B:(hd + 1) * DQ_B], ident)
                    mm.then_inc(turn_done, 1)

            def latent_step(u):
                t, step = u // 8, u % 8
                if step == 0:
                    pe.wait_ge(turn_ev, T_B + 4 * t)
                    dense_rows(L_UQ, lat_cols, t, bank[6], (0, 512))
                    dense_rows(L_UQ, lat_cols, t, bank[7], (512, 768)).then_inc(qb_done, 1)
                if step == 1:
                    pe.wait_ge(qb_ev, t + 1)
                    dense_rows(L_UQ + 1, lat_cols[:, 3:5, :], t, bank[6], (0, 512))
                    dense_rows(L_UQ + 1, lat_cols[:, 3:5, :], t, bank[7], (512, 1024)).then_inc(kv_done, 1)
                if step == 5:
                    turn_heads(t, 0)
                if step == 7:
                    turn_heads(t, 1)

            def unit(u):
                att, t, hd = u // 32, u // 8 % 4, u % 8
                return att, t, hd, P * (t + 1)

            def at_scores(u):
                att, t, hd, w = unit(u)
                if u >= 2:
                    pe.wait_ge(at_s, u - 1)
                if att == 0:
                    lo = 64 * (hd % 2)
                    q = qkaT[lo:lo + 64, 0, hd // 2, t * P:(t + 1) * P]
                    k = qkaT[lo:lo + 64, 1, hd // 2, 0:w]
                else:
                    if hd == 0:
                        pe.wait_ge(turn_ev, T_B + 4 * (t + 1))
                    q, k = qbT(hd)[0:DQ_B, t * P:(t + 1) * P], kbT[0:DQ_B, hd, 0:w]
                pe.matmul(bank[u % 2][:, 0:w], q, k, start=True, stop=True).then_inc(at_done, 1)

            def at_T(u):
                att, t, hd, w = unit(u)
                pe.wait_ge(at_exp, u + 1)
                if u >= 2:
                    pe.wait_ge(pT2_ev, u - 1)
                for j in range(t + 1):
                    mm = pe.transpose(bank[2 + u % 2][:, j * P:(j + 1) * P], sP[u % 2][:, j * P:(j + 1) * P], ident)
                mm.then_inc(pT2_done, 1)

            def at_values(u):
                att, t, hd, w = unit(u)
                pe.wait_ge(pT2_ev, u + 1)
                g = u // 8
                if hd == 0 and g >= 2:
                    pe.wait_ge(o_ev, g - 1)
                for j in range(t + 1):
                    v = pr2[:, j, (C_VA, C_QI)[att] + hd * DH:(C_VA, C_QI)[att] + (hd + 1) * DH]
                    mm = pe.matmul(bank[4 + g % 2][:, hd * DH:(hd + 1) * DH], sPT[u % 2][:, j, :], v,
                                   start=(j == 0), stop=(j == t))
                mm.then_inc(pv_done, 1)

            for u in range(64 + 2):
                if u < 64:
                    at_scores(u)
                if 1 <= u <= 64:
                    at_T(u - 1)
                if u >= 2:
                    at_values(u - 2)
                if u < 32:
                    latent_step(u)
            pe.wait_ge(mixed, 8)
            for k in range(KD):
                if k >= 4:
                    pe.wait_ge(mxT_ev[k % 2], (k - 4) // 2 + 1)
                for t in range(NT):
                    c = C_QA + k * P if k < 4 else C_CQ + (k - 4) * P
                    mm = pe.transpose(bank[k % 4][:, t * P:(t + 1) * P], pr2[:, t, c:c + P], ident)
                mm.then_inc(mxT_done, 1)
            pe.wait_ge(mxT_ev[0], 4)
            pe.wait_ge(mxT_ev[1], 4)
            for n in range(2):
                chunk_ready(L_OUT2 + n)
                for t in range(NT):
                    dense_rows(L_OUT2 + n, xc, t, bank[4 * (n == 0) + t]).then_inc(out_done, 1)

        @block.scalar
        def _(act):
            def copy(out, in_, scale=1.0):
                return nc.scalar.activation(out, in_, ACT.Copy, scale=scale)

            def squares(n, tile_rdy=None):
                for t in range(NT):
                    if tile_rdy is not None:
                        act.wait_ge(tile_rdy, t + 1)
                    ins = nc.scalar.activation(xr[:, t, :], h[:, t, :], ACT.Square, accum_out=sumsq[:, t:t + 1])
                    ins.then_inc(norm_sq, 1)

            def cols_evac(n, gain):
                for k in range(0, KD, 2):
                    act.wait_ge(norm_T, KD * NORM[n] + k + 1)
                    copy(xc[:, k, :], bank[4 + k % 4][:, :], gain[:, k:k + 1] if gain is not None else 1.0
                         ).then_inc(norm_cols[0], 1)

            act.dma_start(h[:, :, :], d["x"].rearrange("(t p) n -> p t n", p=P)).then_inc(x_ld, 16)
            act.dma_start(cst[:, :], d["constants"]).then_inc(cst_ld, 16)
            act.dma_start(sml[:, :], d["small"]).then_inc(small_ld, 16)
            act.dma_start(posi, d["positions"]).then_inc(small_ld, 16)
            act.dma_start(poolw, d["pool_w"].rearrange("g c n -> c g n")).then_inc(poolw_ld, 16)
            act.dma_start(rw[:, :, :], d["router_w"].rearrange("(k p) e -> p k e", p=P)).then_inc(rw_ld, 16)
            act.dma_start(grow[:, :], d["norm_moe_w"].partition_broadcast(P)).then_inc(grow_ld, 16)
            act.wait_ge(x_ld, 16)
            squares("mix")
            act.wait_ge(trig_in, 1)
            nc.scalar.activation(sin1, ang.rearrange("p (t f) -> p t f", t=NT), ACT.Sin)
            nc.scalar.activation(cos1, ctmp.rearrange("p (t f) -> p t f", t=NT), ACT.Sin).then_inc(trig_out, 1)
            act.wait_ge(small_ld, 32)
            cols_evac("mix", M["g_mix"])
            act.wait_ge(pad_zero, 1)
            for g in range(16):
                act.wait_ge(proj_done, g + 1)
                n, t = IN_ORDER[g // 4], g % 4
                dst = uT[:, t, PAD:] if n == 4 else proj[:, t, n * 512:(n + 1) * 512]
                copy(dst, bank[g % 4][:, :]).then_inc(proj_ev, 1)
            for t in range(NT):
                act.wait_ge(proj_done, 17 + t)
                nc.scalar.activation(xr[:, t, 0:512], bank[t][:, :], ACT.Sigmoid).then_inc(silu_sig, 1)
            for g in range(4):
                act.wait_ge(mixg_done, g + 1)
                copy(xc[:, 4 + g, :], bank[4 + g][:, :], M["pool_scale"][:, g:g + 1]).then_inc(mixg_ev, 1)
            for n in range(8):
                act.wait_ge(qkT_done, n + 1)
                copy(qkT[:, n // 4, n % 4, :], bank[n % 4][:, :]).then_inc(qkT_ev, 1)
            for k in (0, 2):
                act.wait_ge(retT_done, k + 1)
                copy(xc[:, k, :], bank[k][:, :], M["gn_w"][:, k:k + 1]).then_inc(retT_ev[0], 1)

            act.wait_ge(wo_ev, 8)
            squares("moe")
            act.wait_ge(norm_rows, 2 * NT)
            act.dma_start(xn_dram.rearrange("(t p) n -> p t n", p=P), xr).then_inc(rows_st, 16)
            cols_evac("moe", None)
            act.wait_ge(gexp_in, 1)
            for t in range(NT):
                ins = nc.scalar.activation(gates[:, t * 4:(t + 1) * 4], top8[:, t * 8:t * 8 + 4], ACT.Exp,
                                           bias=negv0[:, t:t + 1], accum_out=gsum[:, t:t + 1])
            act.drain().then_inc(gexp, 1)
            act.wait_ge(gT_done, 1)
            act.wait_ge(rows_st, 16)
            copy(gT, bank[3][0:E, :]).then_inc(gT_ev, 1)
            act.wait_ge(bsplit, 3)
            act.dma_start(bparts[32:64, :], bpart2).then_inc(bp_ld, 16)
            act.dma_start(bparts[64:96, :], bpart3).then_inc(bp_ld, 16)

            def chunk_src(c):
                return gu_w[c] if c < 8 else dn_w[c - 8].rearrange("p j n -> p (j n)")

            def cast_w(i, c, m, turn):
                act.wait_ge((gu_ld + dn_ld)[c], 16 * i + 16)
                if not isinstance(m, int) or m >= 3:
                    act.wait_ge(w_used, m - 2)
                copy(w_hi[(c + turn) % 3][:, :], chunk_src(c)).then_inc(w_hi_rdy, 1)

            def cols_hi(i, done, ev, dst):
                act.wait_ge(done, i + 1)
                copy(dst[:, 0:512], bank[6][:, :])
                copy(dst[:, 512:1024], bank[7][:, :])
                act.drain().then_inc(ev, 1)

            def sigmoid(i):
                act.wait_ge(g_rdy, i + 1)
                nc.scalar.activation(sig_s, gate_s, ACT.Sigmoid, scale=ALPHA).then_inc(sig_rdy, 1)

            def store_y(i, used):
                act.wait_ge(w_used, used)
                copy(y_s[:, 0:512], bank[4][:, :])
                copy(y_s[:, 512:1024], bank[5][:, :])
                act.drain().then_inc(y_free, 1)
                act.dma_start(y_dram[ds(i * P, P), :], y_s).then_inc(y_st, 16)

            def item(i):
                m = 12 * i - 4
                for c in range(3):
                    cast_w(i, c, m + c, 2)
                if not isinstance(i, int):
                    store_y(i - 2, 12 * i - 4)
                for c in range(3, 7):
                    cast_w(i, c, m + c, 2)
                cols_hi(i - 1, actT_done, actT_hi_ev, actT_hi)
                cast_w(i, 7, m + 7, 2)
                for c in (8, 9):
                    cast_w(i - 1, c, m + c, 2)
                cols_hi(i + 1, xgT_done, xgT_hi_ev, xgT_hi)
                sigmoid(i)
                for c in (10, 11):
                    cast_w(i - 1, c, m + c, 2)
                if not isinstance(i, int):
                    act.wait_ge(y_st, 16 * i - 16)

            act.nop().then_inc(y_free, 1)
            act.wait_ge(item_rdy, 1)
            last = act.value_load(last_item[0:1, 0:1], min_val=E - 1, max_val=NITEM - 2)
            cols_hi(0, xgT_done, xgT_hi_ev, xgT_hi)
            for c in range(8):
                cast_w(0, c, c, 0)
            cols_hi(1, xgT_done, xgT_hi_ev, xgT_hi)
            sigmoid(0)
            item(1)
            with act.Fori(2, last + 1) as i:
                item(i)
            store_y(last - 1, 12 * last + 8)
            cols_hi(last, actT_done, actT_hi_ev, actT_hi)
            for c in range(8, 12):
                cast_w(last, c, 12 * last + c, 0)
            act.wait_ge(y_st, 16 * last)
            store_y(last, 12 * last + 12)

            act.wait_ge(y_st, 16 * last + 16)
            act.dma_start(grow[:, :], d["final_norm_w"].partition_broadcast(P)).then_inc(grow2_ld, 16)
            act.drain().then_inc(y_all, 1)
            for k in range(2):
                act.wait_ge(pT_done, k + 1)
                copy(p_cols[:, k, :], bank[k][:, :]).then_inc(pT_ev, 1)
            squares("ple", combined)
            cols_evac("ple", M["g_ple"])
            for g in range(8):
                act.wait_ge(plg_done, g + 1)
                nc.scalar.activation(sig2[:, g, :], bank[2 * (g % 2)][:, :], ACT.Sigmoid).then_inc(plg_sig, 1)
            act.wait_ge(ple_ev, 8)
            squares("fin")
            act.wait_ge(final_rdy, 1)
            squares("two")
            cols_evac("two", M["gain2"])

            def turned(n, dst, gain=1.0):
                act.wait_ge(turn_done, n + 1)
                copy(dst, bank[2 + n % 2][:, :], gain).then_inc(turn_ev, 1)

            def index_relu(q):
                for u in range(4 * q, 4 * q + 4):
                    t = 1 + u // HEADS
                    act.wait_ge(ix_done, u + 1)
                    if u >= 2:
                        act.wait_ge(ix_acc, u - 1)
                    nc.scalar.activation(sP[u % 2][:, 0:P * (t + 1)], bank[4 + u % 4][:, 0:P * (t + 1)], ACT.Relu
                                         ).then_inc(ix_relu, 1)

            for j, n in enumerate(IN2_ORDER):
                for t in range(NT):
                    g = 4 * j + t
                    act.wait_ge(pr2_done, g + 1)
                    w = min(512, D_IN2 - n * 512)
                    copy(pr2[:, t, n * 512:n * 512 + w], bank[g % 2][:, 0:w]).then_inc(pr2_ev, 1)
                    if (j, t) == INDEX_TURN:
                        for b in range(4):
                            turned(T_IX + b, qiT[:, b, :])
                        turned(T_IX + 4, kiT)
                    if (j, t) in INDEX_SCORES:
                        index_relu(INDEX_SCORES.index((j, t)))
            for w in range(2):
                for b in range(4):
                    turned((T_QA, T_KA)[w] + b, qkaT[:, w, b, :])
            for b in range(5):
                turned(T_LAT + b, lat_cols[:, b, :], M["bq_lat"][:, b:b + 1] if b < 3 else M["bkv_lat"][:, b - 3:b - 2])

            def turned_heads(t, w):
                for half in range(2):
                    n = T_B + 4 * t + 2 * w + half
                    act.wait_ge(turn_done, n + 1)
                    if w:
                        dst = kbT[:, 4 * half:4 * half + 4, t * P:(t + 1) * P]
                    elif half:
                        dst = qiT[:, :, t * P:(t + 1) * P]
                    else:
                        dst = pr2[:, :, C_KA + t * P:C_KA + (t + 1) * P]
                    copy(dst[0:DQ_B], bank[6 + half][0:DQ_B, :].rearrange("p (a n) -> p a n", a=4)).then_inc(turn_ev, 1)

            def latent_step(u):
                t, step = u // 8, u % 8
                if step == 0:
                    act.wait_ge(qb_done, t + 1)
                    copy(qrow[:, 0:512], bank[6][:, :])
                    copy(qrow[:, 512:768], bank[7][:, 0:256]).then_inc(qb_ev, 1)
                if step == 1:
                    act.wait_ge(kv_done, t + 1)
                    for half in range(2):
                        src = bank[6 + half][:, :].rearrange("p (a n) -> p a n", a=4)
                        copy(pr2[:, t, C_QI + half * 256:C_QI + (half + 1) * 256].rearrange("p (a n) -> p a n", a=4),
                             src[:, :, 64:128])
                        ins = copy(krow[:, half * 384:(half + 1) * 384].rearrange("p (a n) -> p a n", a=4)[:, :, 0:64],
                                   src[:, :, 0:64])
                    ins.then_inc(k_ev, 1)
                if step == 5:
                    turned_heads(t, 0)
                if step == 7:
                    turned_heads(t, 1)

            def unit(u):
                t = u // 8 % 4
                return t, P * (t + 1)

            def exponentials(u):
                t, w = unit(u)
                act.wait_ge(at_s, u + 1)
                if u >= 2:
                    act.wait_ge(pT2_done, u - 1)
                nc.scalar.activation(sP[u % 2][:, 0:w], sS[u % 2][:, 0:w], ACT.Exp, bias=nmax[:, u % 4:u % 4 + 1],
                                     scale=-1.0, accum_out=rs_all[:, u % 16:u % 16 + 1]).then_inc(at_exp, 1)

            def at_copy(u):
                t, w = unit(u)
                act.wait_ge(pT2_done, u + 1)
                if u >= 2:
                    act.wait_ge(pv_done, u - 1)
                copy(sPT[u % 2][:, 0:t + 1, :], bank[2 + u % 2][:, 0:w].rearrange("p (j n) -> p j n", j=t + 1)
                     ).then_inc(pT2_ev, 1)

            for u in range(64 + 1):
                if u < 64:
                    if u % 8 == 0 and u >= 16:
                        act.wait_ge(o_ev, u // 8 - 1)
                    exponentials(u)
                if u:
                    at_copy(u - 1)
                if u < 32:
                    latent_step(u)
            for g in range(8):
                att, t = g // 4, g % 4
                c = (C_GA, C_GB)[att]
                act.wait_ge(o_ev, g + 1)
                nc.scalar.activation(sS[g % 2], pr2[:, t, c:c + 512], ACT.Sigmoid).then_inc(gsig2, 1)
                act.wait_ge(mixed, g + 1)
            for k in range(0, KD, 2):
                act.wait_ge(mxT_done, k + 1)
                copy(xc[:, k, :], bank[k % 4][:, :]).then_inc(mxT_ev[0], 1)
            for t in range(NT):
                act.wait_ge(out_rdy, NT + t + 1)
                act.dma_start(d["out"][t * P:(t + 1) * P, :], h[:, t, :]).then_inc(out_st, 16)
            act.wait_ge(out_st, 16 * NT)

        @block.vector
        def _(dve):
            v = nc.vector
            D_ = dve.drain

            asked = [0]

            def ask_rsqrt():
                asked[0] += 1
                dve.drain().then_inc(sums_rdy, 1)

            def get_rsqrt():
                dve.wait_ge(rstd_rdy, asked[0])

            def rsqrt_mean():
                ask_rsqrt()
                get_rsqrt()

            def norm_to_rows(n, eps, gain=None):
                dve.wait_ge(norm_sq, NT * (SQ[n] + 1))
                rsqrt_mean()
                for t in range(NT):
                    if gain is None:
                        ins = v.tensor_scalar(xr[:, t, :], h[:, t, :], rstd[:, t:t + 1], None, ALU.mult)
                    else:
                        ins = v.scalar_tensor_tensor(out=xr[:, t, :], in0=h[:, t, :], scalar=rstd[:, t:t + 1],
                                                     in1=gain, op0=ALU.mult, op1=ALU.mult)
                    ins.then_inc(norm_rows, 1)

            def cols_evac(n, gain):
                for k in range(1, KD, 2):
                    dve.wait_ge(norm_T, KD * NORM[n] + k + 1)
                    if gain is None:
                        ins = v.tensor_copy(xc[:, k, :], bank[4 + k % 4][:, :])
                    else:
                        ins = v.tensor_scalar(xc[:, k, :], bank[4 + k % 4][:, :], gain[:, k:k + 1], None, ALU.mult)
                    ins.then_inc(norm_cols[1], 1)

            def rope(x1, x2, cos, sin, t):
                v.tensor_tensor(t[0], x1, cos, ALU.mult)
                v.tensor_tensor(t[1], x2, sin, ALU.mult)
                v.tensor_tensor(t[2], x2, cos, ALU.mult)
                v.tensor_tensor(t[3], x1, sin, ALU.mult)
                D_()
                v.tensor_tensor(x1, t[0], t[1], ALU.subtract)
                return v.tensor_tensor(x2, t[2], t[3], ALU.add)

            def over(ap, axis, n):
                u = ap.unsqueeze(axis)
                shape = list(u.shape)
                shape[axis] = n
                return u.to_broadcast(shape)

            dve.wait_ge(cst_ld, 16)
            dve.wait_ge(small_ld, 32)
            v.tensor_copy(posf, posi)
            D_()
            a3 = ang.rearrange("p (t f) -> p t f", t=NT)
            v.tensor_tensor(a3, over(posf, 2, HALF_A), over(C["invfreq"], 1, NT), ALU.mult)
            D_()
            v.tensor_scalar(turns, ang, float(1 / TWO_PI), ROUND, ALU.mult, ALU.add)
            D_()
            v.tensor_scalar(turns, turns, ROUND, None, ALU.subtract)
            D_()
            for part in (PI_A, PI_B, PI_C):
                v.scalar_tensor_tensor(out=ang, in0=turns, scalar=-part, in1=ang, op0=ALU.mult, op1=ALU.add)
                D_()
            v.tensor_scalar(ang, ang, 3.1415925, -3.1415925, ALU.min, ALU.max)
            D_()
            v.scalar_tensor_tensor(out=ctmp, in0=ang, scalar=-1.0, in1=ang, op0=ALU.mult, op1=ALU.max)
            D_()
            v.tensor_scalar(ctmp, ctmp, -1.0, float(np.pi / 2), ALU.mult, ALU.add).then_inc(trig_in, 1)
            norm_to_rows("mix", EPS1)
            cols_evac("mix", M["g_mix"])
            dve.wait_ge(trig_out, 1)
            t4 = [tmp4[:, b, :].rearrange("p (t a f) -> p t a f", t=NT, a=HEADS) for b in range(4)]
            for w in range(2):
                dve.wait_ge(proj_ev, 4 * w + 4)
                x = proj[:, :, w * D_RET:(w + 1) * D_RET].rearrange("p t (a f) -> p t a f", a=HEADS)
                rope(x[:, :, :, 0:HALF_A], x[:, :, :, HALF_A:DH], over(cos1, 2, HEADS), over(sin1, 2, HEADS), t4)
                D_()
                g = C[("gq", "gk")[w]].rearrange("p (t a) -> p t a", t=NT)
                v.tensor_tensor(x, x, over(g, 3, DH), ALU.mult).then_inc(rope_done, 1)
            for t in range(NT):
                dve.wait_ge(silu_sig, t + 1)
                v.tensor_tensor(proj[:, t, 1536:2048], bank[t][:, :], xr[:, t, 0:512], ALU.mult).then_inc(gate_ev, 1)
            for n in range(32):
                j = n % 4
                dve.wait_ge(sc_done, n + 1)
                w = S - j * P
                v.tensor_tensor(scT[:, n // 4 % 2, j, j * P:S], bank[j][:, 0:w], C["causal"][:, 0:w], ALU.mult
                                ).then_inc(sc_ev, 1)
            dve.wait_ge(y1_done, 1)
            for t in range(NT):
                y = bank[4 + t][:, :].rearrange("p (a n) -> p a n", a=HEADS)
                yc = xr[:, t, 512:1024].rearrange("p (a n) -> p a n", a=HEADS)
                sq = tmp4[:, t, 0:512].rearrange("p (a n) -> p a n", a=HEADS)
                m, q = mu[:, t * 8:(t + 1) * 8], var[:, t * 8:(t + 1) * 8]
                v.tensor_reduce(m, y, X, ALU.add)
                D_()
                v.tensor_scalar(m, m, 1.0 / DH, None, ALU.mult)
                D_()
                v.tensor_tensor(yc, y, over(m, 2, DH), ALU.subtract)
                D_()
                v.tensor_tensor(sq, yc, yc, ALU.mult)
                D_()
                v.tensor_reduce(q, sq, X, ALU.add)
                D_()
                rsqrt_mean()
                v.tensor_tensor(yc, yc, over(q, 2, DH), ALU.mult)
                D_()
                v.tensor_tensor(xr[:, t, 512:1024], xr[:, t, 512:1024], proj[:, t, 1536:2048], ALU.mult
                                ).then_inc(ret_rows, 1)
            for k in (1, 3):
                dve.wait_ge(retT_done, k + 1)
                v.tensor_scalar(xc[:, k, :], bank[k][:, :], M["gn_w"][:, k:k + 1], None, ALU.mult).then_inc(retT_ev[1], 1)
            for g in range(8):
                n, t = g // 4, g % 4
                dve.wait_ge(wo_done, g + 1)
                hv = h[:, t, n * 512:(n + 1) * 512]
                v.tensor_tensor(hv, hv, bank[t][:, :], ALU.add).then_inc(wo_ev, 1)

            dve.wait_ge(grow_ld, 16)
            norm_to_rows("moe", EPS1, grow[:, :])
            cols_evac("moe", None)
            dve.wait_ge(lg_done, 1)
            v.tensor_tensor(logits, bank[0][:, 0:NT * E].rearrange("p (t e) -> p t e", e=E), over(M["router_b"], 1, NT), ALU.add)
            D_()
            for t in range(NT):
                v.max(top8[:, t * 8:(t + 1) * 8], logits[:, t, :])
                D_()
                v.max_index(idx8[:, t * 8:(t + 1) * 8], top8[:, t * 8:(t + 1) * 8], logits[:, t, :])
            D_()
            t8 = top8.rearrange("p (t a) -> p t a", a=8)
            v.tensor_scalar(negv0.unsqueeze(2), t8[:, :, 0:1], -1.0, None, ALU.mult).then_inc(gexp_in, 1)
            idxf = more[:, 0:16]
            v.tensor_copy(idxf.rearrange("p (t a) -> p t a", a=TOPK), idx8.rearrange("p (t a) -> p t a", a=8)[:, :, 0:TOPK])
            D_()
            v.tensor_tensor(onehot, over(C["iota32"], 1, 16), over(idxf, 2, E), ALU.is_equal)
            D_()
            v.tensor_reduce(member, onehot.rearrange("p (t a) e -> p t e a", t=NT), X, ALU.add).then_inc(member_rdy, 1)
            dve.wait_ge(gexp, 1)
            v.reciprocal(gsum, gsum)
            D_()
            g3 = gates.rearrange("p (t a) -> p t a", a=TOPK)
            v.tensor_tensor(g3, g3, over(gsum, 2, TOPK), ALU.mult)
            D_()
            v.tensor_tensor(prod, onehot, over(gates, 2, E), ALU.mult)
            D_()
            v.tensor_reduce(gdense, prod.rearrange("p (t a) e -> p t e a", t=NT), X, ALU.add).then_inc(gd_rdy, 1)
            dve.wait_ge(rank_done, 1)
            dve.wait_ge(yzero_st, 16)
            cnt = bank[2][:, 0:E]
            v.tensor_scalar(nblk, cnt, float(P), 1.0, ALU.is_gt, ALU.add)
            D_()
            for m in (2, 3):
                v.tensor_scalar(more, cnt, float(m * P), None, ALU.is_gt)
                D_()
                v.tensor_tensor(nblk, nblk, more, ALU.add)
                D_()
            v.tensor_tensor_scan(incl, C["ones"][:, 0:E], nblk, 0.0, ALU.mult, ALU.add)
            D_()
            v.tensor_scalar(last_item, incl[:, E - 1:E], 1.0, None, ALU.subtract)
            v.tensor_tensor(base, incl, nblk, ALU.subtract)
            v.tensor_tensor(cmp48, over(incl, 1, NITEM), over(C["iota48"], 2, E), ALU.is_le)
            D_()
            v.tensor_scalar(base, base, float(P), None, ALU.mult)
            v.tensor_reduce(item_e, cmp48, X, ALU.add)
            D_()
            v.tensor_scalar(item_e, item_e, float(E - 1), None, ALU.min)
            slot3 = logits
            v.tensor_tensor(slot3, bank[1][:, 0:NT * E].rearrange("p (t e) -> p t e", e=E), over(base, 1, NT), ALU.add)
            D_()
            v.tensor_copy(item_ei, item_e)
            v.tensor_tensor(prod.rearrange("p (t a) e -> p t a e", t=NT), onehot.rearrange("p (t a) e -> p t a e", t=NT),
                            over(slot3, 2, TOPK), ALU.mult)
            D_()
            slotf, placef = more[:, 0:16], more[:, 16:32]
            v.tensor_reduce(slotf, prod, X, ALU.add)
            v.tensor_copy(tok_i, C["tok"])
            D_()
            v.tensor_copy(slot_u, slotf)
            D_()
            v.tensor_scalar(place_u, slot_u, 7, None, ALU.logical_shift_right)
            v.tensor_scalar(idx8[:, 0:16], slot_u, P - 1, None, ALU.bitwise_and)
            D_()
            v.tensor_copy(placef, place_u)
            v.tensor_copy(slotf, idx8[:, 0:16])
            D_()
            v.scalar_tensor_tensor(out=placef, in0=slotf, scalar=float(NITEM), in1=placef, op0=ALU.mult, op1=ALU.add)
            D_()
            v.tensor_copy(place_u, placef)
            dve.drain().then_inc(place_rdy, 1)
            dve.drain().then_inc(item_rdy, 1)
            for g in range(8):
                n, t = g // 4, g % 4
                dve.wait_ge(bd_done, g + 1)
                hv = h[:, t, n * 512:(n + 1) * 512]
                v.tensor_tensor(hv, hv, bank[4 + t][:, :], ALU.add).then_inc(bd_ev, 1)
            dve.wait_ge(braw_ld, 16)
            v.tensor_copy(bparts[0:E, :], braw).then_inc(bsplit, 1)
            D_()
            for out, left in ((bpart2, bparts[0:E, :]), (bpart3, bpart2)):
                v.tensor_tensor(braw, braw, left, ALU.subtract)
                D_()
                v.tensor_copy(out, braw).then_inc(bsplit, 1)
                D_()

            def pick(i):
                v.tensor_scalar(sel_e[:, :], item_e[0:96, ds(i, 1)].to_broadcast([96, P]), C["pmod"][0:96, :], None,
                                ALU.is_equal).then_inc(sel_rdy, 1)

            def rest_w(i, c, m, turn):
                dve.wait_ge((gu_ld + dn_ld)[c], 16 * i + 16)
                dve.wait_ge(w_hi_rdy, m + 1)
                if not isinstance(m, int) or m >= 2:
                    dve.wait_ge(w_used, m - 1)
                src = gu_w[c] if c < 8 else dn_w[c - 8].rearrange("p j n -> p (j n)")
                v.tensor_tensor(w_lo[c % 2][:, :], src, w_hi[(c + turn) % 3][:, :].bitcast(F32), ALU.subtract).then_inc(w_lo_rdy, 1)

            def cols_lo(i, hi_ev, ev, hi, lo):
                dve.wait_ge(hi_ev, i + 1)
                for n in range(2):
                    cut = slice(n * 512, (n + 1) * 512)
                    v.tensor_tensor(lo[:, cut], bank[6 + n][:, :], hi[:, cut].bitcast(F32), ALU.subtract)
                dve.drain().then_inc(ev, 1)

            def clamp(i):
                dve.wait_ge(gu_done, i + 1)
                for n in range(4):
                    pair = bank[n][:, :].rearrange("p (n two) -> p n two", two=2)
                    v.tensor_scalar(gate_s[:, n * 256:(n + 1) * 256].unsqueeze(2), pair[:, :, 0:1], LIMIT, None, ALU.min)
                dve.drain().then_inc(g_rdy, 1)
                for n in range(4):
                    pair = bank[n][:, :].rearrange("p (n two) -> p n two", two=2)
                    v.tensor_scalar(up_s[:, n * 256:(n + 1) * 256].unsqueeze(2), pair[:, :, 1:2], LIMIT, -LIMIT, ALU.min, ALU.max)
                dve.drain().then_inc(gu_ev, 1)

            def up_times_gate():
                v.scalar_tensor_tensor(out=up_s, in0=up_s, scalar=1.0, in1=gate_s, op0=ALU.add, op1=ALU.mult)

            def times_sigmoid(i):
                dve.wait_ge(sig_rdy, i + 1)
                v.tensor_tensor(up_s, up_s, sig_s, ALU.mult).then_inc(act_rdy, 1)

            pick(0)
            last = dve.value_load(last_item[0:1, 0:1], min_val=E - 1, max_val=NITEM - 2)
            cols_lo(0, xgT_hi_ev, xgT_ev, xgT_hi, xgT_lo)
            for c in range(8):
                rest_w(0, c, c, 0)
            clamp(0)
            cols_lo(1, xgT_hi_ev, xgT_ev, xgT_hi, xgT_lo)
            pick(1)
            with dve.Fori(1, last + 1) as i:
                m = 12 * i - 4
                rest_w(i, 0, m, 2)
                up_times_gate()
                rest_w(i, 1, m + 1, 2)
                D_()
                times_sigmoid(i - 1)
                for c in range(2, 6):
                    rest_w(i, c, m + c, 2)
                cols_lo(i - 1, actT_hi_ev, actT_ev, actT_hi, actT_lo)
                for c in (6, 7):
                    rest_w(i, c, m + c, 2)
                for c in (8, 9):
                    rest_w(i - 1, c, m + c, 2)
                clamp(i)
                rest_w(i - 1, 10, m + 10, 2)
                cols_lo(i + 1, xgT_hi_ev, xgT_ev, xgT_hi, xgT_lo)
                pick(i + 1)
                rest_w(i - 1, 11, m + 11, 2)
            up_times_gate()
            D_()
            times_sigmoid(last)
            cols_lo(last, actT_hi_ev, actT_ev, actT_hi, actT_lo)
            for c in range(8, 12):
                rest_w(last, c, 12 * last + c, 0)

            for a in range(16):
                t = a // 4
                if a % 4 == 0:
                    dve.wait_ge(yg_ld[t], 16 * TOPK)
                v.scalar_tensor_tensor(out=h[:, t, :], in0=ygat[:, a, :], scalar=gates[:, a:a + 1], in1=h[:, t, :],
                                       op0=ALU.mult, op1=ALU.add)
                if a % 4 == 3:
                    dve.drain().then_inc(combined, 1)
                else:
                    D_()
            norm_to_rows("ple", EPS1)
            cols_evac("ple", M["g_ple"])
            for g in range(8):
                n, t = g // 4, g % 4
                hv = h[:, t, n * 512:(n + 1) * 512]
                dve.wait_ge(plg_sig, g + 1)
                dve.wait_ge(plp_done, g + 1)
                v.tensor_tensor(sig2[:, g, :], sig2[:, g, :], bank[2 * (g % 2) + 1][:, :], ALU.mult)
                D_()
                v.tensor_tensor(hv, hv, sig2[:, g, :], ALU.add).then_inc(ple_ev, 1)
            dve.wait_ge(norm_sq, NT * (SQ["fin"] + 1))
            dve.wait_ge(grow2_ld, 16)
            rsqrt_mean()
            for t in range(NT):
                v.scalar_tensor_tensor(out=h[:, t, :], in0=h[:, t, :], scalar=rstd[:, t:t + 1], in1=grow[:, :],
                                       op0=ALU.mult, op1=ALU.mult)
            dve.drain().then_inc(final_rdy, 1)
            norm_to_rows("two", EPS2)
            cols_evac("two", M["gain2"])
            ci = C["cos_i"].rearrange("p (t f) -> p t f", t=NT)
            si = C["sin_i"].rearrange("p (t f) -> p t f", t=NT)
            dve.wait_ge(pr2_ev, 4 * 2)
            xi = pr2[:, :, C_QI:C_QI + 512].rearrange("p t (a f) -> p t a f", a=HEADS)
            i4 = [rot[:, b, 0:512].rearrange("p (t a f) -> p t a f", t=NT, a=HEADS) for b in range(4)]
            rope(xi[:, :, :, 0:16], xi[:, :, :, 16:32], over(ci, 2, HEADS), over(si, 2, HEADS), i4)
            D_()
            xk = pr2[:, :, C_KI:C_KI + 64]
            k4 = [rot[:, b, 0:64].rearrange("p (t f) -> p t f", t=NT) for b in range(4)]
            rope(xk[:, :, 0:16], xk[:, :, 16:32], ci, si, k4)
            D_()
            v.tensor_copy(ki2[:, :, 0:64], xk)
            v.tensor_copy(ki2[:, :, 64:128], xk)
            v.tensor_scalar(wi_s.rearrange("p (t a) -> p t a", t=NT), pr2[:, :, C_WI:C_WI + 8], float((64 * 8) ** -0.5), None, ALU.mult)
            dve.drain().then_inc(ix_rdy, 1)
            v.tensor_copy(selbias[:, 0, 0:P], C["chunkbias"][:, S - P:S])
            for u in range(24):
                t, hd = 1 + u // HEADS, u % HEADS
                w = P * (t + 1)
                acc, rel = index_acc[t - 1][:, 0:w], sP[u % 2][:, 0:w]
                wcol = wi_s[:, t * 8 + hd:t * 8 + hd + 1]
                dve.wait_ge(ix_relu, u + 1)
                if hd == 0:
                    v.tensor_scalar(acc, rel, wcol, None, ALU.mult).then_inc(ix_acc, 1)
                else:
                    v.scalar_tensor_tensor(out=acc, in0=rel, scalar=wcol, in1=acc, op0=ALU.mult, op1=ALU.add
                                           ).then_inc(ix_acc, 1)
                D_()
            for t in range(1, NT):
                w = P * (t + 1)
                acc = index_acc[t - 1][:, 0:w]
                v.tensor_tensor(acc, acc, C["chunkbias"][:, S - w:S], ALU.add)
                D_()
                for r in range(KEEP // 8):
                    v.max(top8[:, 0:8], acc)
                    D_()
                    v.match_replace(acc, top8[:, 0:8], acc, TAKEN)
                    D_()
                v.tensor_scalar(selbias[:, t, 0:w], acc, TAKEN / 2, NEG, ALU.is_gt, ALU.mult)
            r4 = [rot[:, b, :].rearrange("p (t a f) -> p t a f", t=NT, a=HEADS) for b in range(4)]
            ca = C["cos_a"].rearrange("p (t f) -> p t f", t=NT)
            sa = C["sin_a"].rearrange("p (t f) -> p t f", t=NT)
            for w in range(2):
                dve.wait_ge(pr2_ev, 4 * (IN2_ORDER.index(w) + 1))
                x = pr2[:, :, w * 512:(w + 1) * 512]
                x4 = x.rearrange("p t (a f) -> p t a f", a=HEADS)
                sq = xrows[:, 0:2048].rearrange("p (t n) -> p t n", t=NT)
                v.tensor_tensor(sq, x, x, ALU.mult)
                D_()
                v.tensor_reduce(mu, xrows[:, 0:2048].rearrange("p (a f) -> p a f", f=DH), X, ALU.add)
                D_()
                rsqrt_mean()
                v.tensor_tensor(x4, x4, over(mu.rearrange("p (t a) -> p t a", t=NT), 3, DH), ALU.mult)
                D_()
                for t in range(NT):
                    v.tensor_tensor(x4[:, t], x4[:, t], over(M[("aq", "ak")[w]], 1, HEADS), ALU.mult)
                D_()
                rope(x4[:, :, :, 0:HALF_A], x4[:, :, :, HALF_A:DH], over(ca, 2, HEADS), over(sa, 2, HEADS), r4
                     ).then_inc(qa_rdy, 1)
                D_()
            dve.wait_ge(pr2_ev, 4 * (IN2_ORDER.index(6) + 1))
            for j, (c, n) in enumerate(((C_CQ, Q_LORA), (C_CKV, KV_LORA))):
                x = pr2[:, :, c:c + n]
                sq = xrows[:, 0:NT * n].rearrange("p (t n) -> p t n", t=NT)
                v.tensor_tensor(sq, x, x, ALU.mult)
                D_()
                v.tensor_reduce(mu[:, 0:NT], sq, X, ALU.add)
                D_()
                rsqrt_mean()
                v.tensor_tensor(x, x, over(mu[:, 0:NT], 2, n), ALU.mult).then_inc(lat_rdy, 1)
                D_()
            dve.wait_ge(pr2_ev, 4 * NCH2)

            def latent_piece(u):
                t, w, piece = u // 8, (u % 8 - 1) // 3, (u % 8 - 1) % 3
                r = (qrow, krow)[w].rearrange("p (a n) -> p a n", a=HEADS)
                if piece == 0:
                    if w == 0:
                        dve.wait_ge(qb_ev, t + 1)
                    else:
                        dve.wait_ge(k_ev, t + 1)
                        v.tensor_copy(r[:, :, 64:96], over(pr2[:, t, C_KR:C_KR + 32], 1, HEADS))
                        D_()
                    v.tensor_tensor(bsq, r, r, ALU.mult)
                    D_()
                    v.tensor_reduce(mu[:, 0:8], bsq, X, ALU.add)
                    ask_rsqrt()
                if piece == 1:
                    get_rsqrt()
                    v.tensor_tensor(r, r, over(mu[:, 0:8], 2, DQ_B), ALU.mult)
                    D_()
                    v.tensor_tensor(r, r, over(M[("bq", "bk")[w]], 1, HEADS), ALU.mult)
                if piece == 2:
                    D_()
                    rope(r[:, :, 64:80], r[:, :, 80:96], over(ci[:, t, :], 1, HEADS), over(si[:, t, :], 1, HEADS), brot
                         ).then_inc(qb_rdy, 1)

            def at_mask(u):
                att, t = u // 32, u // 8 % 4
                w = P * (t + 1)
                dve.wait_ge(at_done, u + 1)
                if u >= 2:
                    dve.wait_ge(at_exp, u - 1)
                bias = selbias[:, t, 0:w] if att == 0 else C["chunkbias"][:, S - w:S]
                v.tensor_tensor_reduce(sS[u % 2][:, 0:w], bank[u % 2][:, 0:w], bias, -float((DH, DQ_B)[att]) ** -0.5, 3e38,
                                       ALU.add, ALU.min, nmax[:, u % 4:u % 4 + 1])
                dve.drain().then_inc(at_s, 1)

            def at_out(g):
                att, t = g // 4, g % 4
                dve.wait_ge(pv_done, 8 * (g + 1))
                r = rs_all[:, 8 * (g % 2):8 * (g % 2) + 8]
                v.reciprocal(var[:, 0:8], r)
                D_()
                c = (C_QA, C_CQ)[att]
                v.tensor_tensor(pr2[:, t, c:c + 512].rearrange("p (a n) -> p a n", a=HEADS),
                                bank[4 + g % 2][:, :].rearrange("p (a n) -> p a n", a=HEADS),
                                over(var[:, 0:8], 2, DH), ALU.mult).then_inc(o_ev, 1)

            for u in range(64):
                at_mask(u)
                if u % 8 == 3 and u > 8:
                    at_out(u // 8 - 1)
                if u < 32 and 1 <= u % 8 <= 6:
                    latent_piece(u)
            at_out(7)
            for g in range(8):
                att, t = g // 4, g % 4
                c, cg = (C_QA, C_CQ)[att], (C_GA, C_GB)[att]
                ov = pr2[:, t, c:c + 512]
                D_()
                v.tensor_tensor(ov, ov, pr2[:, t, cg:cg + 512], ALU.mult)
                D_()
                dve.wait_ge(gsig2, g + 1)
                v.tensor_tensor(ov, ov, sS[g % 2], ALU.mult).then_inc(mixed, 1)
            for k in range(1, KD, 2):
                dve.wait_ge(mxT_done, k + 1)
                v.tensor_copy(xc[:, k, :], bank[k % 4][:, :]).then_inc(mxT_ev[1], 1)
            for g in range(8):
                n, t = g // 4, g % 4
                hv = h[:, t, n * 512:(n + 1) * 512]
                dve.wait_ge(out_done, g + 1)
                v.tensor_tensor(hv, hv, bank[4 * (n == 0) + t][:, :], ALU.add).then_inc(out_rdy, 1)

        @block.gpsimd
        def _(pool):
            g_ = nc.gpsimd
            D_ = pool.drain
            done = [0]

            def rsqrt_mean(out, sums, n, eps):
                done[0] += 1
                pool.wait_ge(sums_rdy, done[0])
                g_.tensor_scalar(out, sums, 1.0 / n, eps, ALU.mult, ALU.add)
                D_()
                g_.tensor_tensor(out, out, minus_half[:, 0:out.shape[1]], ALU.pow).then_inc(rstd_rdy, 1)

            g_.memset(idx_all, 0).then_inc(place_zero, 1)
            pool.wait_ge(place_zero, 1)
            pool.dma_start(place_dram.rearrange("(p i) o -> p (i o)", p=P), idx_all).then_inc(zero_st, 16)
            g_.memset(minus_half, -0.5)
            g_.memset(uT[:, :, 0:PAD], 0.0)
            g_.memset(yzero, 0.0)
            g_.memset(win[0][:, 0:PAD], 0.0)
            g_.memset(win[1][:, 0:PAD], 0.0)
            D_().then_inc(pad_zero, 1)
            rsqrt_mean(rstd, sumsq, D, EPS1)
            pool.wait_ge(proj_ev, 12)
            pool.dma_start(y_dram[E * P:, :].rearrange("(i p) n -> p i n", p=P),
                           yzero.unsqueeze(1).to_broadcast([P, NITEM - E, D])).then_inc(yzero_st, 16)
            pool.wait_ge(cst_ld, 16)
            iw = C["invw"].rearrange("p (g n) -> p g n", g=4)
            for g, w in enumerate(WINDOWS):
                src, step, at = uT[:, g, :], 1, 0
                while step < w:
                    g_.tensor_tensor(win[at][:, PAD:], src[:, PAD:], src[:, PAD - step:PAD + S - step], ALU.add)
                    D_()
                    src, step, at = win[at], 2 * step, 1 - at
                mean = win[at]
                g_.tensor_scalar(mean[:, PAD:], src[:, PAD:], 1.0 / w, None, ALU.mult)
                D_()
                g_.tensor_tensor(mean[:, PAD:2 * PAD], src[:, PAD:2 * PAD], iw[:, g, :], ALU.mult)
                D_()
                g_.tensor_tensor(uT[:, g, PAD:], mean[:, PAD:], uT[:, g, PAD:], ALU.subtract).then_inc(pooled, 1)
                D_()
            for t in range(NT):
                rsqrt_mean(var[:, t * 8:(t + 1) * 8], var[:, t * 8:(t + 1) * 8], DH, EPS1)
            rsqrt_mean(rstd, sumsq, D, EPS1)
            pool.wait_ge(zero_st, 16)
            pool.wait_ge(place_rdy, 1)
            for a in range(16):
                pool.indirect_dma_start(out=place_dram[:, :], out_offset=bass.IndirectOffsetOnAxis(ap=place_u[:, a:a + 1], axis=0),
                                        in_=tok_i[:, a // 4:a // 4 + 1], in_offset=None).then_inc(place_st, 16)
            pool.wait_ge(place_st, 16 * 16)
            pool.dma_start(idx_all, place_dram.rearrange("(p i) o -> p (i o)", p=P)).then_inc(idx_ld, 16)
            pool.wait_ge(idx_ld, 16)
            pool.wait_ge(rows_st, 16)
            pool.wait_ge(gT_ev, 1)
            pool.wait_ge(bd_done, 8)

            def gather(i):
                g_.tensor_copy(idx_cur, idx_all[:, ds(i, 1)])
                D_()
                pool.indirect_dma_start(out=xg, out_offset=None, in_=xn_dram[:, :],
                                        in_offset=bass.IndirectOffsetOnAxis(ap=idx_cur.bitcast(U32), axis=0)
                                        ).then_inc(xg_ld, 16)

            last = pool.value_load(last_item[0:1, 0:1], min_val=E - 1, max_val=NITEM - 2)
            gather(0)
            with pool.Fori(1, last + 2) as i:
                pool.wait_ge(xgT_done, i)
                pool.wait_ge(xg_ld, 16 * i)
                gather(i)
            pool.wait_ge(y_all, 1)
            for a in range(16):
                pool.indirect_dma_start(out=ygat[:, a, :], out_offset=None, in_=y_dram[:, :],
                                        in_offset=bass.IndirectOffsetOnAxis(ap=slot_u[:, a:a + 1], axis=0)
                                        ).then_inc(yg_ld[a // 4], 16)
            for eps in (EPS1, EPS1, EPS2):
                rsqrt_mean(rstd, sumsq, D, eps)
            for _ in range(2):
                rsqrt_mean(mu, mu, DH, EPS2)
            for n in (Q_LORA, KV_LORA):
                rsqrt_mean(mu[:, 0:NT], mu[:, 0:NT], n, EPS2)
            for _ in range(2 * NT):
                rsqrt_mean(mu[:, 0:8], mu[:, 0:8], DQ_B, EPS2)


INPUTS = ("x", "p", "positions", "w_in", "w_out", "pool_w", "norm_moe_w", "router_w", "expert_w_gate_up",
          "expert_b_gate_up", "expert_w_down", "expert_b_down", "ple_gate_w", "ple_proj_w", "final_norm_w",
          "w_in_2", "w_uq_2", "w_ukv_2", "w_out_2", "small", "constants")


def kernel(**inputs):
    import concourse.bacc as bacc
    from concourse.bass_utils import run_bass_kernel_spmd

    a = {k: np.asarray(v) for k, v in inputs.items()}

    def cols(v):
        return v.reshape(-1, P).T

    def rows(v):
        return np.broadcast_to(v.reshape(1, -1), (P, v.size))

    small = {"g_mix": cols(a["norm_mix_w"]), "gn_w": cols(a["ret_gn_w"]), "pool_scale": cols(a["pool_scale"]),
             "g_ple": cols(a["norm_ple_w"]), "gain2": cols(a["norm_gain_2"]), "bq_lat": cols(a["b_q_latent_norm_2"]),
             "bkv_lat": cols(a["b_kv_latent_norm_2"]), "router_b": rows(a["router_b"]), "aq": rows(a["a_q_norm_2"]),
             "ak": rows(a["a_k_norm_2"]), "bq": rows(a["b_q_norm_2"]), "bk": rows(a["b_k_norm_2"])}
    one = {k: a[k][0] for k in ("x", "p", "w_in", "w_out", "pool_w", "router_w", "expert_w_gate_up", "expert_b_gate_up",
                                "expert_w_down", "expert_b_down", "ple_gate_w", "ple_proj_w", "w_in_2", "w_uq_2",
                                "w_ukv_2", "w_out_2")}
    one["p"] = one["p"].reshape(S, PLE)
    one["positions"] = a["positions"].reshape(NT, P).T
    one["norm_moe_w"] = a["norm_moe_w"].reshape(D)
    one["final_norm_w"] = a["final_norm_w"]
    one["small"] = np.concatenate([small[k] for k in SMALL.at], axis=1)
    one["constants"] = shape_constants()

    nc = bacc.Bacc("TRN2", target_bir_lowering=False, num_devices=1)
    arrays, args = {}, {}
    for name in INPUTS:
        v = np.ascontiguousarray(one[name])
        arrays["in_" + name] = v
        args[name] = nc.dram_tensor("in_" + name, v.shape, mybir.dt.from_np(v.dtype), kind="ExternalInput").ap()
    args["out"] = nc.dram_tensor("out_rows", (S, D), F32, kind="ExternalOutput").ap()
    build_program(nc, args)
    r = run_bass_kernel_spmd(nc, [arrays], core_ids=[0])
    return r.results[0]["out_rows"].reshape(1, S, D)
```

```python
from contextlib import ExitStack

import numpy as np

import concourse.bass as bass
from concourse import mybir

F32 = mybir.dt.float32
F32R = mybir.dt.float32r
BF16 = mybir.dt.bfloat16
I32 = mybir.dt.int32
U32 = mybir.dt.uint32
ALU = mybir.AluOpType
ACT = mybir.ActivationFunctionType
X = mybir.AxisListType.X
ds = bass.ds

P = 128
S, D = 512, 1024
NT = S // P
KD = D // P
HEADS, DH = 8, 64
D_RET = HEADS * DH
WINDOWS = (2, 4, 8, 16)
PAD = max(WINDOWS)
E, TOPK = 32, 4
LIMIT, ALPHA = 7.0, 1.702
PLE = 256
NITEM = 48
EPS1, EPS2 = 1e-5, 1e-6
NEG = -1e30
TAKEN = -3e38
KEEP = 128
Q_LORA, KV_LORA = 384, 256
DQ_B = 96
HALF_A, HALF_I = DH // 2, 16
C_QA, C_KA, C_VA, C_GA, C_QI = 0, 512, 1024, 1536, 2048
C_KI, C_WI, C_CQ, C_CKV, C_KR, C_GB = 2560, 2624, 2632, 3016, 3272, 3304
D_IN2 = 3816
NCH2 = -(-D_IN2 // 512)
IN2_ORDER = (4, 5, 0, 1, 6, 2, 3, 7)
INDEX_TURN = (2, 2)
INDEX_SCORES = ((2, 3), (3, 0), (3, 0), (3, 1), (3, 2), (3, 3))
T_IX, T_QA, T_KA, T_LAT, T_B = 0, 5, 9, 13, 18
TWO_PI = 2 * np.pi
PI_A = 6.28125
PI_B = float(np.float32(np.floor((TWO_PI - PI_A) * 2 ** 21) / 2 ** 21))
PI_C = float(np.float32(TWO_PI - PI_A - PI_B))
ROUND = 12582912.0


class Cols:

    def __init__(self, **widths):
        self.at, self.n = {}, 0
        for name, w in widths.items():
            self.at[name] = (self.n, self.n + w)
            self.n += w


CONST = Cols(ident=P, causal=S, ustrict=P, ones=P, chunkbias=S, cos_a=NT * HALF_A, sin_a=NT * HALF_A,
             cos_i=NT * HALF_I, sin_i=NT * HALF_I, gq=NT * HEADS, gk=NT * HEADS, invw=4 * PAD,
             invfreq=HALF_A, iota32=E, iota48=NITEM, pmod=1, tok=NT)
SMALL = Cols(g_mix=KD, gn_w=4, pool_scale=4, g_ple=KD, gain2=KD, bq_lat=3, bkv_lat=2, router_b=E,
             aq=DH, ak=DH, bq=DQ_B, bk=DQ_B)


def shape_constants():
    c = {}
    p = np.arange(P)
    tok = np.arange(NT)[None, :] * P + p[:, None]
    c["ident"] = np.eye(P)
    c["causal"] = np.concatenate([(p[None, :] >= p[:, None]), np.ones((P, S - P))], 1)
    c["ustrict"] = p[:, None] < p[None, :]
    c["ones"] = np.ones((P, P))
    last = np.where((p[:, None] < 64) & (p[None, :] >= 64), NEG, 0.0)
    c["chunkbias"] = np.concatenate([np.zeros((P, S - P)), last], 1)
    f32 = np.float32
    for name, half in (("a", HALF_A), ("i", HALF_I)):
        freq = np.power(f32(10000.0), -np.arange(half, dtype=f32) * f32(2.0) / f32(2 * half)).astype(f32)
        ang = (tok[:, :, None].astype(f32) * freq[None, None, :]).astype(f32).astype(np.float64)
        c["cos_" + name], c["sin_" + name] = np.cos(ang), np.sin(ang)
    lg = np.log1p(-np.power(2.0, -5.0 - np.arange(HEADS)))
    c["gq"] = np.exp(tok[:, :, None] * lg)
    c["gk"] = np.exp(-tok[:, :, None] * lg) * DH ** -0.5
    c["invw"] = np.broadcast_to(np.stack([1.0 / np.minimum(np.arange(PAD) + 1.0, w) for w in WINDOWS])[None],
                                (P, 4, PAD))
    c["invfreq"] = np.broadcast_to(np.power(f32(10000.0), -np.arange(HALF_A, dtype=f32) / f32(HALF_A))[None],
                                   (P, HALF_A))
    c["iota32"] = np.broadcast_to(np.arange(E)[None], (P, E))
    c["iota48"] = np.broadcast_to(np.arange(NITEM)[None], (P, NITEM))
    c["pmod"] = (p % E)[:, None]
    c["tok"] = tok
    return np.concatenate([np.asarray(c[k], np.float64).reshape(P, -1) for k in CONST.at], 1).astype(np.float32)


def build_program(nc, d):
    ctx = ExitStack()
    with ctx:
        def sb(name, shape, dt=F32):
            return ctx.enter_context(nc.sbuf_tensor("sb_" + name, shape, dt))

        def sem(name):
            return ctx.enter_context(nc.semaphore(name))

        def dram(name, shape, dt=F32):
            return nc.dram_tensor("scratch_" + name, shape, dt, kind="Internal").ap()

        ring_at = -(-nc.sbuf_base // 32) * 32
        ring = sb("ring", [P, 12 * 2048])
        wbuf_at = nc.sbuf_base
        wbuf = sb("wbuf", [P, 2, KD * 512])
        h_at = nc.sbuf_base
        h = sb("h", [P, NT, D])
        xcols_at = nc.sbuf_base
        xcols = sb("xcols", [P, KD * S])
        xrows_at = nc.sbuf_base
        xrows = sb("xrows", [P, NT * D])
        scr_at = nc.sbuf_base
        scr = sb("scr", [P, 3072])
        cst = sb("cst", [P, CONST.n])
        sml = sb("sml", [P, SMALL.n])
        grow = sb("grow", [P, D])
        rw = sb("rw", [P, KD, E])
        sel_e = sb("sel_e", [96, P], BF16)
        st = sb("st", [P, 512])
        bank = [ctx.enter_context(nc.psum_tensor(f"bank{i}", [P, 512], F32)) for i in range(8)]

        C = {k: cst[:, a:b] for k, (a, b) in CONST.at.items()}
        M = {k: sml[:, a:b] for k, (a, b) in SMALL.at.items()}
        ident = C["ident"]
        xc = xcols[:, :].rearrange("p (k s) -> p k s", k=KD)
        xr = xrows[:, :].rearrange("p (t n) -> p t n", t=NT)

        taken = [0]

        def stat(n, dt=F32):
            a = taken[0]
            taken[0] += n
            assert taken[0] <= 512
            v = st[:, a:a + n]
            return v if dt == F32 else v.bitcast(dt)

        sumsq = stat(NT)
        rstd = stat(NT)
        posf = stat(NT)
        posi = stat(NT, I32)
        mu = stat(HEADS * NT)
        var = stat(HEADS * NT)
        gates = stat(16)
        gsum = stat(NT)
        negv0 = stat(NT)
        slot_u = stat(16, U32)
        place_u = stat(16, U32)
        tok_i = stat(NT, I32)
        item_e = stat(NITEM)
        item_ei = stat(NITEM, I32)
        last_item = stat(1, I32)
        idx_cur = stat(1, I32)
        idx_all = stat(NITEM, I32)
        nmax = stat(4)
        rs_all = stat(16)
        minus_half = stat(HEADS * NT)
        wi_s = stat(NT * HEADS)
        top8 = stat(NT * 8)
        idx8 = stat(NT * 8, U32)
        lat_sum = stat(2 * NT)

        proj = ring[:, 0:8192].rearrange("p (t n) -> p t n", t=NT)
        tmp4 = ring[:, 8192:12288].rearrange("p (b n) -> p b n", b=4)
        qkT = ring[:, 12288:16384].rearrange("p (w a s) -> p w a s", w=2, a=4)
        scT = ring[:, 16384:20480].rearrange("p (b j s) -> p b j s", b=2, j=NT)
        uT = ring[:, 20480:22592].rearrange("p (g s) -> p g s", g=4)
        win = [ring[:, 22592 + i * 528:22592 + (i + 1) * 528] for i in range(2)]
        poolw = ring[:, 23648:24160].rearrange("p (g n) -> p g n", g=4)
        cos1 = scr[:, 0:128].rearrange("p (t f) -> p t f", t=NT)
        sin1 = scr[:, 128:256].rearrange("p (t f) -> p t f", t=NT)
        ang = scr[:, 256:384]
        turns = scr[:, 384:512]
        ctmp = scr[:, 512:640]
        yzero = scr[:, 1024:1024 + D]

        onehot = scr[:, 0:512].rearrange("p (a e) -> p a e", e=E)
        prod = scr[:, 512:1024].rearrange("p (a e) -> p a e", e=E)
        cmp48 = scr[:, 1024:1024 + NITEM * E].rearrange("p (i e) -> p i e", e=E)
        route = scr[:, 2560:3072]
        logits = route[:, 0:128].rearrange("p (t e) -> p t e", e=E)
        member = route[:, 128:256].rearrange("p (t e) -> p t e", e=E)
        gdense = route[:, 256:384].rearrange("p (t e) -> p t e", e=E)
        nblk, incl, base = route[:, 384:416], route[:, 416:448], route[:, 448:480]
        more = route[:, 480:512]
        gT = xrows[0:E, 0:S]
        bdown = xrows[0:E, D:2 * D]
        braw = wbuf[0:E, 0, 0:2048]
        bparts = grow[0:96, :].bitcast(BF16)
        bpart2 = wbuf[0:E, 1, 0:1024].bitcast(BF16)
        bpart3 = wbuf[0:E, 1, 1024:2048].bitcast(BF16)
        gu_w = [ring[:, c * 2048:(c + 1) * 2048] for c in range(8)]
        dn_w = [ring[:, 16384 + c * 2048:16384 + (c + 1) * 2048].rearrange("p (j n) -> p j n", j=2) for c in range(4)]
        xg, gate_s, up_s, sig_s = (xrows[:, i * 1024:(i + 1) * 1024] for i in range(4))
        y_s = scr[:, 2048:3072]

        def part(name, n, at, words):
            return nc.alloc_sbuf_tensor_at("sb_" + name, [P, n], F32R, offset=at + 4 * words)

        x_hi = part("x_hi", KD * S, xcols_at, 0)[:, :].rearrange("p (k s) -> p k s", k=KD)
        x_lo = part("x_lo", NT * D, xrows_at, 0)[:, :].rearrange("p (t n) -> p t n", t=NT)
        dense_hi = [[part(f"dense_hi{b}{i}", 1024, ring_at, at + i * 1024) for i in range(2)]
                    for b, at in enumerate((12288, NT * D_IN2))]
        dense_lo = [[part(f"dense_lo{b}{i}", 1024, ring_at, at + 2048 + i * 1024) for i in range(2)]
                    for b, at in enumerate((12288, NT * D_IN2))]
        w_hi = [part("w_hi0", 2048, wbuf_at, 0), part("w_hi1", 2048, wbuf_at, 2048), part("w_hi2", 2048, xcols_at, 2048)]
        w_lo = [part("w_lo0", 2048, wbuf_at, 4096), part("w_lo1", 2048, wbuf_at, 6144), part("w_lo2", 2048, h_at, 0)]
        xgT_hi, xgT_lo = part("xgT_hi", 1024, xcols_at, 0), part("xgT_lo", 1024, xcols_at, 1024)
        actT_hi, actT_lo = part("actT_hi", 1024, scr_at, 0), part("actT_lo", 1024, scr_at, 1024)

        ygat = ring[:, 0:16384].rearrange("p (a n) -> p a n", a=16)
        p_rows = ring[:, 16384:17408].rearrange("p (t n) -> p t n", t=NT)
        p_cols = ring[:, 17408:18432].rearrange("p (k s) -> p k s", k=2)
        plew = ring[:, 18432:20480].rearrange("p (k n) -> p k n", k=2)
        pproj = ring[:, 20480:24576].rearrange("p (g n) -> p g n", g=8)
        gate_sig = [scr[:, i * 512:(i + 1) * 512] for i in range(4)]

        pr2 = ring[:, 0:NT * D_IN2].rearrange("p (t n) -> p t n", t=NT)
        o2 = NT * D_IN2
        qkaT = ring[:, o2:o2 + 4096].rearrange("p (w a s) -> p w a s", w=2, a=4)
        qiT = ring[:, o2 + 4096:o2 + 6144].rearrange("p (a s) -> p a s", a=4)
        kiT = ring[:, o2 + 6144:o2 + 6656]
        selbias = ring[:, o2 + 6656:o2 + 8704].rearrange("p (t s) -> p t s", t=NT)
        ki2 = ring[:, o2 + 8704:o2 + 8704 + 512].rearrange("p (t n) -> p t n", t=NT)
        hspill = h[:, :, :].rearrange("p t n -> p (t n)")
        rot = hspill.rearrange("p (b n) -> p b n", b=4)
        out_sig = hspill.rearrange("p (g n) -> p g n", g=8)
        lat_junk = scr[:, 2560:2560 + Q_LORA]
        lat_cols = xcols[:, 0:5 * S].rearrange("p (k s) -> p k s", k=5)
        qrow = xcols[:, 5 * S:5 * S + 768]
        krow = xcols[:, 5 * S + 768:5 * S + 1536]
        kbT = xrows[:, :].rearrange("p (a s) -> p a s", a=HEADS)
        sS = [scr[:, i * 512:(i + 1) * 512] for i in range(3)]
        index_acc = [scr[:, 0:512], scr[:, 512:1024], ring[:, o2 + 8704:o2 + 9216]]
        bsq = grow[:, 0:HEADS * DQ_B].rearrange("p (a n) -> p a n", a=HEADS)
        brot = [kiT[:, b * 128:(b + 1) * 128].rearrange("p (a f) -> p a f", a=HEADS) for b in range(4)]
        ix_rel = [scr[:, 1024 + i * 512:1024 + (i + 1) * 512] for i in range(2)]
        sPT = [scr[:, 2048 + i * 512:2048 + (i + 1) * 512].rearrange("p (j n) -> p j n", j=NT) for i in range(2)]

        def out_gate(g):
            c = (C_GA, C_GB)[g // 4]
            return pr2[:, g % 4, c:c + 512]

        def qbT(hd):
            return pr2[:, hd, C_KA:C_KA + S] if hd < 4 else qiT[:, hd - 4, :]

        xn_dram = dram("rows", [S, D])
        place_dram = dram("place", [P * NITEM, 1], I32)
        y_dram = dram("y", [NITEM * P, D])
        h_dram = dram("h", [S, D])

        yzero_st = sem("yzero_st")
        sums_rdy = sem("sums_rdy")
        rstd_rdy = sem("rstd_rdy")
        mean_rdy = sem("mean_rdy")
        cst_ld = sem("cst_ld")
        ident_ld = sem("ident_ld")
        cols_done = sem("cols_done")
        hi_ev = sem("hi_ev")
        lo_ev = sem("lo_ev")
        dense_hi_rdy = sem("dense_hi_rdy")
        dense_lo_rdy = sem("dense_lo_rdy")
        dense_done = sem("dense_done")
        gn_mid = sem("gn_mid")
        gn_sq = sem("gn_sq")
        pp_done = sem("pp_done")
        pp_ev = sem("pp_ev")
        h_st = sem("h_st")
        h_half_st = sem("h_half_st")
        h_half_ld = sem("h_half_ld")
        h_ld = sem("h_ld")
        qk_sq = sem("qk_sq")
        lat_sq = sem("lat_sq")
        small_ld = sem("small_ld")
        poolw_ld = sem("poolw_ld")
        trig_in = sem("trig_in")
        trig_out = sem("trig_out")
        silu_sig = sem("silu_sig")
        proj_ev = sem("proj_ev")
        gate_ev = sem("gate_ev")
        rope_done = sem("rope_done")
        qkT_done = sem("qkT_done")
        qkT_ev = sem("qkT_ev")
        pad_zero = sem("pad_zero")
        pooled = sem("pooled")
        sc_done = sem("sc_done")
        sc_ev = sem("sc_ev")
        y1_done = sem("y1_done")
        ret_rows = sem("ret_rows")
        wo_ev = sem("wo_ev")
        rows_st = sem("rows_st")
        lg_done = sem("lg_done")
        gexp_in = sem("gexp_in")
        gexp = sem("gexp")
        member_rdy = sem("member_rdy")
        gd_rdy = sem("gd_rdy")
        rank_done = sem("rank_done")
        gT_done = sem("gT_done")
        gT_ev = sem("gT_ev")
        bd_ld = sem("bd_ld")
        bd_done = sem("bd_done")
        bd_ev = sem("bd_ev")
        braw_ld = sem("braw_ld")
        bsplit = sem("bsplit")
        bp_ld = sem("bp_ld")
        place_rdy = sem("place_rdy")
        place_zero = sem("place_zero")
        zero_st = sem("zero_st")
        place_st = sem("place_st")
        idx_ld = sem("idx_ld")
        item_rdy = sem("item_rdy")
        w_hi_rdy = sem("w_hi_rdy")
        w_lo_rdy = sem("w_lo_rdy")
        w_used = sem("w_used")
        xgT_hi_ev = sem("xgT_hi_ev")
        actT_hi_ev = sem("actT_hi_ev")
        xg_ld = sem("xg_ld")
        xgT_done = sem("xgT_done")
        xgT_ev = sem("xgT_ev")
        gu_done = sem("gu_done")
        gu_ev = sem("gu_ev")
        g_rdy = sem("g_rdy")
        sig_rdy = sem("sig_rdy")
        act_rdy = sem("act_rdy")
        actT_done = sem("actT_done")
        actT_ev = sem("actT_ev")
        y_free = sem("y_free")
        y_st = sem("y_st")
        sel_rdy = sem("sel_rdy")
        combined = sem("combined")
        p_ld = sem("p_ld")
        plew_ld = sem("plew_ld")
        pT_done = sem("pT_done")
        pT_ev = sem("pT_ev")
        plg_sig = sem("plg_sig")
        ple_ev = sem("ple_ev")
        final_rdy = sem("final_rdy")
        pr2_ev = sem("pr2_ev")
        ix_rdy = sem("ix_rdy")
        turn_done = sem("turn_done")
        turn_ev = sem("turn_ev")
        y_all = sem("y_all")
        qa_rdy = sem("qa_rdy")
        ix_done = sem("ix_done")
        ix_relu = sem("ix_relu")
        ix_acc = sem("ix_acc")
        lat_rdy = sem("lat_rdy")
        qb_done = sem("qb_done")
        qb_ev = sem("qb_ev")
        kv_done = sem("kv_done")
        k_ev = sem("k_ev")
        qb_rdy = sem("qb_rdy")
        at_done = sem("at_done")
        at_s = sem("at_s")
        at_exp = sem("at_exp")
        pT2_done = sem("pT2_done")
        pT2_ev = sem("pT2_ev")
        pv_done = sem("pv_done")
        o_ev = sem("o_ev")
        gate_sg = sem("gate_sg")
        silu_rdy = sem("silu_rdy")
        bsq_rdy = sem("bsq_rdy")
        bsq_used = sem("bsq_used")
        mixed = sem("mixed")
        out_rdy = sem("out_rdy")
        out_st = sem("out_st")
        grow_ld = sem("grow_ld")
        grow2_ld = sem("grow2_ld")
        rw_ld = sem("rw_ld")
        norm_T = sem("norm_T")
        norm_sq = sem("norm_sq")
        norm_rows = sem("norm_rows")
        w_ld = [sem(f"w_ld{i}") for i in range(2)]
        yg_ld = [sem(f"yg_ld{i}") for i in range(4)]
        gu_ld = [sem(f"gu_ld{i}") for i in range(8)]
        dn_ld = [sem(f"dn_ld{i}") for i in range(4)]
        plain_cols = [sem(f"plain_cols{i}") for i in range(2)]
        x_ld = [sem(f"x_ld{i}") for i in range(NT)]
        SQ = {"mix": 0, "moe": 1, "ple": 2, "fin": 3, "two": 4}
        NORM = {"mix": 0, "moe": 1, "ple": 2, "two": 3}
        B_MIX, B_POOL, B_RET, B_PLE, B_TWO, B_OUT = 0, 8, 12, 16, 24, 32

        block = ctx.enter_context(nc.Block())

        def in_cols(ap, n, w=512):
            return ap[:, n * 512:n * 512 + w].rearrange("(k p) n -> p k n", p=P)

        IN_ORDER = (0, 1, 4, 2, 3)
        chunks = [(in_cols(d["w_in"], n), 8, 512) for n in IN_ORDER]
        chunks += [(in_cols(d["w_out"], n), 8, 512) for n in range(2)]
        L_PLE = len(chunks)
        chunks += [(in_cols(d["ple_gate_w"], n), 8, 512) for n in range(2)]
        L_IN2 = len(chunks)
        for n in IN2_ORDER:
            w = min(512, D_IN2 - n * 512)
            chunks.append((in_cols(d["w_in_2"], n, w), 8, w))
        L_UQ = len(chunks)
        chunks.append((d["w_uq_2"].rearrange("(k p) n -> p k n", p=P), 3, HEADS * DQ_B))
        chunks.append((d["w_ukv_2"].rearrange("(k p) n -> p k n", p=P), 2, D))
        L_OUT2 = len(chunks)
        chunks += [(in_cols(d["w_out_2"], n), 8, 512) for n in range(2)]

        def dense_no(L):
            return L if L < L_UQ else L - 2

        def step_used(m):
            return 7 * (m // 4) + (m % 4 + 1 if m % 4 < 3 else 7)

        def result_done(q, t):
            return 7 * q + 4 + t

        def step_chunk(m):
            q = m // 4
            L = q if q < L_UQ else q + 2
            return L, int(L >= L_IN2), chunks[L][2]

        def chunk_used(L):
            if L in (L_UQ, L_UQ + 1):
                return (qb_done if L == L_UQ else kv_done), NT
            return dense_lo_rdy, 4 * (dense_no(L) + 1)

        def wview(L):
            _, k, w = chunks[L]
            return wbuf[:, L % 2, 0:k * w].rearrange("p (k n) -> p k n", k=k)

        @block.sync
        def _(sp):
            def load_chunk(L):
                if L >= 2:
                    used, n = chunk_used(L - 2)
                    sp.wait_ge(used, n)
                sp.dma_start(wview(L), chunks[L][0]).then_inc(w_ld[L % 2], 16)

            sp.wait_ge(x_ld[NT - 1], 16)
            for L in range(L_PLE):
                load_chunk(L)
            sp.wait_ge(dense_lo_rdy, 4 * L_PLE)
            sp.dma_start(braw, d["expert_b_gate_up"]).then_inc(braw_ld, 16)

            def load_gu(e, c):
                sp.dma_start(gu_w[c], d["expert_w_gate_up"][ds(e, 1), c * P:(c + 1) * P, :].rearrange("o p n -> p (o n)")
                             ).then_inc(gu_ld[c], 16)

            def load_dn(e, c):
                sp.dma_start(dn_w[c], d["expert_w_down"][ds(e, 1), c * 256:(c + 1) * 256, :]
                             .rearrange("o (j p) n -> p (o j) n", p=P)).then_inc(dn_ld[c], 16)

            sp.wait_ge(wo_ev, 8)
            for c in range(8):
                load_gu(0, c)
            for c in range(4):
                load_dn(0, c)
            sp.wait_ge(rows_st, 16)
            sp.wait_ge(norm_T, KD)
            sp.dma_start(bdown, d["expert_b_down"]).then_inc(bd_ld, 16)
            sp.wait_ge(item_rdy, 1)
            last = sp.value_load(last_item[0:1, 0:1], min_val=E - 1, max_val=NITEM - 2)
            e1 = sp.value_load(item_ei[0:1, 1:2], min_val=0, max_val=E - 1)
            for c in range(8):
                sp.wait_ge(w_lo_rdy, c + 1)
                load_gu(e1, c)
            with sp.Fori(1, last) as i:
                e_next = sp.value_load(item_ei[0:1, ds(i + 1, 1)], min_val=0, max_val=E - 1)
                for c in range(8):
                    sp.wait_ge(w_lo_rdy, 12 * i + (c - 3))
                    load_gu(e_next, c)
                e = sp.value_load(item_ei[0:1, ds(i, 1)], min_val=0, max_val=E - 1)
                for c in range(4):
                    sp.wait_ge(w_lo_rdy, 12 * i + (c + 5))
                    load_dn(e, c)
            e_last = sp.value_load(item_ei[0:1, ds(last, 1)], min_val=0, max_val=E - 1)
            for c in range(4):
                sp.wait_ge(w_lo_rdy, 12 * last + (c + 5))
                load_dn(e_last, c)
            sp.wait_ge(w_lo_rdy, 12 * last + 10)
            sp.dma_start(p_rows, d["p"].rearrange("(t p) n -> p t n", p=P)).then_inc(p_ld, 16)
            sp.dma_start(plew, d["ple_proj_w"].rearrange("(k p) n -> p k n", p=P)).then_inc(plew_ld, 16)
            sp.wait_ge(w_used, 12 * last + 12)
            sp.dma_start(h[:, 0:2, :], h_dram[0:2 * P, :].rearrange("(t p) n -> p t n", p=P)).then_inc(h_half_ld, 16)
            sp.wait_ge(yg_ld[NT - 1], 16 * TOPK)
            load_chunk(L_PLE)
            load_chunk(L_PLE + 1)
            for L in range(L_IN2, L_OUT2):
                load_chunk(L)
            sp.wait_ge(h_st, 16)
            sp.wait_ge(silu_rdy, 8)
            sp.dma_start(h[:, :, :], h_dram.rearrange("(t p) n -> p t n", p=P)).then_inc(h_ld, 16)
            for L in range(L_OUT2, len(chunks)):
                load_chunk(L)

        @block.tensor
        def _(pe):
            def to_cols(first, src, b0):
                for k in range(KD):
                    b = bank[b0 + k % 4]
                    if k >= 4:
                        pe.wait_ge(lo_ev, first + k - 3)
                    for t in range(NT):
                        mm = pe.transpose(b[:, t * P:(t + 1) * P], src(k, t), ident)
                    mm.then_inc(cols_done, 1)

            def norm_to_cols(n, first):
                pe.wait_ge(norm_rows, NT * (NORM[n] + 1))
                to_cols(first, lambda k, t: xr[:, t, k * P:(k + 1) * P], 4)
                pe.wait_ge(lo_ev, first + KD)

            def chunk_ready(L):
                pe.wait_ge(w_ld[L % 2], 16 * (L // 2 + 1))

            def dense_rows(L, lhs, t, b, cols=None):
                wv = wview(L)
                k_n, w = wv.shape[1], wv.shape[2]
                a, z = cols or (0, w)
                for k in range(k_n):
                    mm = pe.matmul(b[:, 0:z - a], lhs[:, k, t * P:(t + 1) * P], wv[:, k, a:z],
                                   start=(k == 0), stop=(k == k_n - 1))
                return mm

            def dense_step(L, step, outs, turned=False, free=None):
                m = 4 * dense_no(L) + step
                _, b, w = step_chunk(m)
                pe.wait_ge(dense_lo_rdy, m + 1)
                hi, lo = (a[b][m % 2][:, 0:2 * w].rearrange("p (k n) -> p k n", k=2) for a in (dense_hi, dense_lo))
                for t in range(NT):
                    if step == 0 and free is not None:
                        pe.wait_ge(*free(t))
                    for j in range(2):
                        k = 2 * step + j
                        first, last = k == 0, k == KD - 1
                        if turned:
                            cut = slice(t * P, (t + 1) * P)
                            out = outs[t][:, :]
                            pe.matmul(out, hi[:, j, cut], x_hi[:, k, :], start=first, stop=False)
                            pe.matmul(out.rearrange("p (t n) -> p t n", t=NT), hi[:, j, cut], x_lo[:, :, k * P:(k + 1) * P],
                                      start=False, stop=False)
                            mm = pe.matmul(out, lo[:, j, cut], x_hi[:, k, :], start=False, stop=last)
                        else:
                            out = outs[t][:, 0:w]
                            xh = x_hi[:, k, t * P:(t + 1) * P]
                            pe.matmul(out, xh, hi[:, j, :], start=first, stop=False)
                            pe.matmul(out, xh, lo[:, j, :], start=False, stop=False)
                            mm = pe.matmul(out, x_lo[:, t, k * P:(k + 1) * P], hi[:, j, :], start=False, stop=last)
                    if step == 3:
                        mm.then_inc(dense_done, 1)
                if step < 3:
                    mm.then_inc(dense_done, 1)

            pe.wait_ge(ident_ld, 16)
            norm_to_cols("mix", B_MIX)
            for j, n in enumerate(IN_ORDER):
                for step in range(4):
                    dense_step(j, step, bank[4 * (j % 2):4 * (j % 2) + 4], turned=(n == 4),
                               free=(lambda t: (proj_ev, 4 * (j - 2) + t + 1)) if j >= 2 else None)
            pe.wait_ge(proj_ev, 16)
            for w in range(2):
                pe.wait_ge(rope_done, w + 1)
                if w == 1:
                    pe.wait_ge(gate_ev, 4)
                for a in range(4):
                    for t in range(NT):
                        mm = pe.transpose(bank[4 * (1 - w) + a][:, t * P:(t + 1) * P], proj[:, t, w * D_RET + a * P:w * D_RET + (a + 1) * P], ident)
                    mm.then_inc(qkT_done, 1)

            def scores(hd):
                a, lo = hd // 2, 64 * (hd % 2)
                for j in range(NT):
                    n = 4 * hd + j
                    if n >= 4:
                        pe.wait_ge(sc_ev, n - 3)
                    pe.matmul(bank[j][:, 0:S - j * P], qkT[lo:lo + 64, 1, a, j * P:(j + 1) * P],
                              qkT[lo:lo + 64, 0, a, j * P:S], start=True, stop=True).then_inc(sc_done, 1)

            def values(hd):
                pe.wait_ge(sc_ev, 4 * hd + 4)
                for i in range(NT):
                    for j in range(i + 1):
                        mm = pe.matmul(bank[4 + i][:, hd * DH:(hd + 1) * DH], scT[:, hd % 2, j, i * P:(i + 1) * P],
                                       proj[:, j, 2 * D_RET + hd * DH:2 * D_RET + (hd + 1) * DH],
                                       start=(j == 0), stop=(j == i))
                return mm

            pe.wait_ge(qkT_ev, 8)
            for hd in range(HEADS):
                scores(hd)
                if hd:
                    values(hd - 1)
            values(HEADS - 1).then_inc(y1_done, 1)
            pe.wait_ge(poolw_ld, 16)
            pe.wait_ge(sc_ev, 32)
            for g in range(4):
                pe.wait_ge(pooled, g + 1)
                pe.matmul(bank[g][:, :], poolw[:, g, :], uT[:, g, PAD:], start=True, stop=True).then_inc(cols_done, 1)
            for k in range(4):
                pe.wait_ge(lo_ev, B_POOL + k + 1)
                for t in range(NT):
                    pe.wait_ge(ret_rows, t + 1)
                    mm = pe.transpose(bank[k][:, t * P:(t + 1) * P], xr[:, t, k * P:(k + 1) * P], ident)
                mm.then_inc(cols_done, 1)
            pe.wait_ge(lo_ev, B_RET + 4)
            for n in range(2):
                for step in range(4):
                    dense_step(5 + n, step, bank[4 * (1 - n):4 * (1 - n) + 4])

            pe.wait_ge(norm_rows, NT * (NORM["moe"] + 1))
            for k in range(KD):
                b = bank[4 + k % 4]
                if k >= 4:
                    pe.wait_ge(plain_cols[k % 2], (k - 4) // 2 + 1)
                for t in range(NT):
                    mm = pe.transpose(b[:, t * P:(t + 1) * P], xr[:, t, k * P:(k + 1) * P], ident)
                mm.then_inc(norm_T, 1)
            pe.wait_ge(plain_cols[0], 4)
            pe.wait_ge(plain_cols[1], 4)
            pe.wait_ge(rw_ld, 16)
            pe.wait_ge(wo_ev, 8)
            for t in range(NT):
                for k in range(KD):
                    mm = pe.matmul(bank[0][:, t * E:(t + 1) * E], xc[:, k, t * P:(t + 1) * P], rw[:, k, :],
                                   start=(k == 0), stop=(k == KD - 1))
            mm.then_inc(lg_done, 1)
            pe.wait_ge(member_rdy, 1)
            for t in range(NT):
                for j in range(t + 1):
                    pe.matmul(bank[1][:, t * E:(t + 1) * E], C["ustrict"] if j == t else C["ones"], member[:, j, :],
                              start=(j == 0), stop=(j == t))
            for j in range(NT):
                mm = pe.matmul(bank[2][:, 0:E], C["ones"], member[:, j, :], start=(j == 0), stop=(j == NT - 1))
            mm.then_inc(rank_done, 1)
            pe.wait_ge(gd_rdy, 1)
            for t in range(NT):
                mm = pe.transpose(bank[3][0:E, t * P:(t + 1) * P], gdense[:, t, :], ident)
            mm.then_inc(gT_done, 1)
            pe.wait_ge(gT_ev, 1)
            pe.wait_ge(bd_ld, 16)
            for n in range(2):
                for t in range(NT):
                    if n:
                        pe.wait_ge(bd_ev, t + 1)
                    pe.matmul(bank[4 + t][:, :], gT[:, t * P:(t + 1) * P], bdown[:, n * 512:(n + 1) * 512],
                              start=True, stop=True).then_inc(bd_done, 1)

            def item_T(i):
                pe.wait_ge(xg_ld, 16 * i + 16)
                for k in range(KD):
                    mm = pe.transpose(bank[6 + k // 4][:, k % 4 * P:(k % 4 + 1) * P], xg[:, k * P:(k + 1) * P], ident)
                mm.then_inc(xgT_done, 1)

            def act_T(i):
                pe.wait_ge(act_rdy, i + 1)
                for k in range(KD):
                    mm = pe.transpose(bank[6 + k // 4][:, k % 4 * P:(k % 4 + 1) * P], up_s[:, k * P:(k + 1) * P], ident)
                mm.then_inc(actT_done, 1)

            def three_passes(outs, hi, lo, w_h, w_l, first, last):
                for a, w, start, stop in ((hi, w_h, first, False), (hi, w_l, False, False), (lo, w_h, False, last)):
                    for n, b in enumerate(outs):
                        mm = pe.matmul(b[:, :], a, w[:, n * 512:(n + 1) * 512], start=start, stop=stop)
                return mm

            def gate_up(i, m, turn, mid=None):
                pe.wait_ge(xgT_ev, i + 1)
                for c in range(KD):
                    pe.wait_ge(w_lo_rdy, m + (c + 1))
                    three_passes(bank[0:4], xgT_hi[:, c * P:(c + 1) * P], xgT_lo[:, c * P:(c + 1) * P],
                                 w_hi[(c + turn) % 3], w_lo[(c + turn) % 3], c == 0, False).then_inc(w_used, 1)
                    if c == 3 and mid:
                        mid()
                pe.wait_ge(sel_rdy, i + 1)
                for n in range(4):
                    mm = pe.matmul(bank[n][:, :], sel_e[:, :], bparts[:, n * 512:(n + 1) * 512], start=False, stop=True)
                mm.then_inc(gu_done, 1)

            def down(i, m, turn):
                pe.wait_ge(actT_ev, i + 1)
                pe.wait_ge(y_free, i + 1)
                for c in range(4):
                    pe.wait_ge(w_lo_rdy, m + (c + 1))
                    for j in range(2):
                        k = 2 * c + j
                        mm = three_passes(bank[4:6], actT_hi[:, k * P:(k + 1) * P], actT_lo[:, k * P:(k + 1) * P],
                                          w_hi[(c + turn) % 3][:, j * D:(j + 1) * D], w_lo[(c + turn) % 3][:, j * D:(j + 1) * D],
                                          k == 0, k == KD - 1)
                    mm.then_inc(w_used, 1)

            pe.wait_ge(bd_ev, 8)
            pe.wait_ge(place_rdy, 1)
            last = pe.value_load(last_item[0:1, 0:1], min_val=E - 1, max_val=NITEM - 2)
            item_T(0)
            pe.wait_ge(bp_ld, 32)
            pe.wait_ge(bsplit, 3)
            gate_up(0, 0, 0)
            item_T(1)
            with pe.Fori(1, last + 1) as i:
                pe.wait_ge(gu_ev, i)
                gate_up(i, 12 * i - 4, 2, lambda: act_T(i - 1))
                pe.wait_ge(actT_ev, i)
                item_T(i + 1)
                down(i - 1, 12 * i + 4, 1)
            pe.wait_ge(xgT_ev, last + 2)
            act_T(last)
            down(last, 12 * last + 8, 2)

            pe.wait_ge(p_ld, 16)
            pe.wait_ge(gu_ev, last + 1)
            for k in range(2):
                for t in range(NT):
                    mm = pe.transpose(bank[k][:, t * P:(t + 1) * P], p_rows[:, t, k * P:(k + 1) * P], ident)
                mm.then_inc(pT_done, 1)
            pe.wait_ge(pT_ev, 2)
            pe.wait_ge(plew_ld, 16)
            for g in range(8):
                n, t = g // 4, g % 4
                if g >= 4:
                    pe.wait_ge(pp_ev, g - 3)
                for k in range(2):
                    mm = pe.matmul(bank[g % 4][:, :], p_cols[:, k, t * P:(t + 1) * P],
                                   plew[:, k, n * 512:(n + 1) * 512], start=(k == 0), stop=(k == 1))
                mm.then_inc(pp_done, 1)
            pe.wait_ge(y_free, last + 2)
            pe.wait_ge(xgT_ev, last + 2)
            pe.wait_ge(pp_ev, 8)
            norm_to_cols("ple", B_PLE)
            for n in range(2):
                for step in range(4):
                    dense_step(L_PLE + n, step, bank[4 * n:4 * n + 4])

            pe.wait_ge(ple_ev, 8)
            norm_to_cols("two", B_TWO)

            def turn(n, blk):
                b = bank[4 + n % 2]
                if n >= 2:
                    pe.wait_ge(turn_ev, n - 1)
                for t in range(NT):
                    mm = pe.transpose(b[:, t * P:(t + 1) * P], blk[:, t, :], ident)
                mm.then_inc(turn_done, 1)

            def index_scores(q):
                for u in range(4 * q, 4 * q + 4):
                    t, hd = 1 + u // HEADS, u % HEADS
                    lo = 64 * (hd % 2)
                    if u >= 2:
                        pe.wait_ge(ix_relu, u - 1)
                    pe.matmul(bank[6 + u % 2][:, 0:P * (t + 1)], qiT[lo:lo + 64, hd // 2, t * P:(t + 1) * P],
                              kiT[lo:lo + 64, 0:P * (t + 1)], start=True, stop=True).then_inc(ix_done, 1)

            def turn_qk(w):
                pe.wait_ge(qa_rdy, w + 1)
                for b in range(4):
                    turn((T_QA, T_KA)[w] + b, pr2[:, :, w * 512 + b * P:w * 512 + (b + 1) * P])

            for j in range(NCH2):
                for step in range(4):
                    dense_step(L_IN2 + j, step, bank[0:4], free=(lambda t: (pr2_ev, 4 * (j - 1) + t + 1)) if j else None)
                    if (j, step) == INDEX_TURN:
                        pe.wait_ge(ix_rdy, 1)
                        for b in range(4):
                            turn(T_IX + b, pr2[:, :, C_QI + b * P:C_QI + (b + 1) * P])
                        turn(T_IX + 4, ki2)
                    for q in range(6):
                        if (j, step) == INDEX_SCORES[q]:
                            pe.wait_ge(turn_ev, T_IX + 5)
                            index_scores(q)
            turn_qk(0)
            turn_qk(1)
            pe.wait_ge(lat_rdy, 2)
            for b in range(5):
                turn(T_LAT + b, pr2[:, :, C_CQ + b * P:C_CQ + (b + 1) * P])
            pe.wait_ge(turn_ev, T_B)
            pe.wait_ge(pr2_ev, 4 * NCH2)
            pe.wait_ge(ix_relu, 24)
            chunk_ready(L_UQ)
            chunk_ready(L_UQ + 1)

            def turn_heads(t, w):
                pe.wait_ge(qb_rdy, 2 * t + w + 1)
                pe.wait_ge(k_ev, t + 1)
                for half in range(2):
                    n = T_B + 4 * t + 2 * w + half
                    pe.wait_ge(turn_ev, n - 1)
                    for a in range(4):
                        hd = 4 * half + a
                        mm = pe.transpose(bank[6 + half][0:DQ_B, a * P:(a + 1) * P],
                                          (qrow, krow)[w][:, hd * DQ_B:(hd + 1) * DQ_B], ident)
                    mm.then_inc(turn_done, 1)

            def latent_step(u):
                t, step = u // 8, u % 8
                if step == 0 and t:
                    turn_heads(t - 1, 1)
                if step == 0 and t < NT:
                    pe.wait_ge(turn_ev, T_B + 4 * t)
                    dense_rows(L_UQ, lat_cols, t, bank[6], (0, 512))
                    dense_rows(L_UQ, lat_cols, t, bank[7], (512, 768)).then_inc(qb_done, 1)
                if step == 1:
                    pe.wait_ge(qb_ev, t + 1)
                    dense_rows(L_UQ + 1, lat_cols[:, 3:5, :], t, bank[6], (0, 512))
                    dense_rows(L_UQ + 1, lat_cols[:, 3:5, :], t, bank[7], (512, 1024)).then_inc(kv_done, 1)
                if step == 6:
                    turn_heads(t, 0)

            def unit(u):
                att, t, hd = u // 32, u // 8 % 4, u % 8
                return att, t, hd, P * (t + 1)

            def at_scores(u):
                att, t, hd, w = unit(u)
                if u >= 3:
                    pe.wait_ge(at_s, u - 2)
                if att == 0:
                    lo = 64 * (hd % 2)
                    q = qkaT[lo:lo + 64, 0, hd // 2, t * P:(t + 1) * P]
                    k = qkaT[lo:lo + 64, 1, hd // 2, 0:w]
                else:
                    if hd == 0:
                        pe.wait_ge(turn_ev, T_B + 4 * (t + 1))
                    q, k = qbT(hd)[0:DQ_B, t * P:(t + 1) * P], kbT[0:DQ_B, hd, 0:w]
                pe.matmul(bank[(0, 1, 5)[u % 3]][:, 0:w], q, k, start=True, stop=True).then_inc(at_done, 1)

            def at_T(u):
                att, t, hd, w = unit(u)
                pe.wait_ge(at_exp, u + 1)
                if u >= 2:
                    pe.wait_ge(pT2_ev, u - 1)
                for j in range(t + 1):
                    mm = pe.transpose(bank[2 + u % 2][:, j * P:(j + 1) * P], sS[u % 3][:, j * P:(j + 1) * P], ident)
                mm.then_inc(pT2_done, 1)

            def at_values(u):
                att, t, hd, w = unit(u)
                pe.wait_ge(pT2_ev, u + 1)
                g = u // 8
                if hd == 0 and g:
                    pe.wait_ge(o_ev, g)
                for j in range(t + 1):
                    v = pr2[:, j, (C_VA, C_QI)[att] + hd * DH:(C_VA, C_QI)[att] + (hd + 1) * DH]
                    mm = pe.matmul(bank[4][:, hd * DH:(hd + 1) * DH], sPT[u % 2][:, j, :], v,
                                   start=(j == 0), stop=(j == t))
                mm.then_inc(pv_done, 1)

            for u in range(64 + 3):
                if u < 64:
                    at_scores(u)
                if 2 <= u < 66:
                    at_T(u - 2)
                if u >= 3:
                    at_values(u - 3)
                if u <= 32:
                    latent_step(u)
            pe.wait_ge(mixed, 8)
            to_cols(B_OUT, lambda k, t: pr2[:, t, (C_QA + k * P if k < 4 else C_CQ + (k - 4) * P):][:, 0:P], 0)
            pe.wait_ge(lo_ev, B_OUT + KD)
            for n in range(2):
                for step in range(4):
                    dense_step(L_OUT2 + n, step, bank[4 * (1 - n):4 * (1 - n) + 4])

        @block.scalar
        def _(act):
            def copy(out, in_, scale=1.0):
                return nc.scalar.activation(out, in_, ACT.Copy, scale=scale)

            def squares(n, rdy):
                for t in range(NT):
                    act.wait_ge(*rdy(t))
                    ins = nc.scalar.activation(xr[:, t, :], h[:, t, :], ACT.Square, accum_out=sumsq[:, t:t + 1])
                    ins.then_inc(norm_sq, 1)

            def high_part(n, k, b, gain=1.0):
                act.wait_ge(cols_done, n + 1)
                copy(x_hi[:, k, :], b[:, :], gain).then_inc(hi_ev, 1)

            def high_parts(first, b0, gain=None):
                for k in range(KD):
                    high_part(first + k, k, bank[b0 + k % 4], gain[:, k:k + 1] if gain is not None else 1.0)

            def cast_dense(m):
                L, b, w = step_chunk(m)
                if m % 4 == 0:
                    act.wait_ge(w_ld[L % 2], 16 * (L // 2 + 1))
                if m >= 2:
                    act.wait_ge(dense_done, step_used(m - 2))
                copy(dense_hi[b][m % 2][:, 0:2 * w].rearrange("p (k n) -> p k n", k=2),
                     wview(L)[:, 2 * (m % 4):2 * (m % 4) + 2, :]).then_inc(dense_hi_rdy, 1)

            for t in range(NT):
                act.dma_start(h[:, t, :], d["x"][t * P:(t + 1) * P, :]).then_inc(x_ld[t], 16)
            act.dma_start(cst[:, 0:P], d["constants"][:, 0:P]).then_inc(ident_ld, 16)
            act.dma_start(sml[:, :], d["small"]).then_inc(small_ld, 16)
            act.dma_start(posi, d["positions"]).then_inc(small_ld, 16)
            squares("mix", lambda t: (x_ld[t], 16))
            act.wait_ge(small_ld, 32)
            high_parts(B_MIX, 4, M["g_mix"])
            cast_dense(0)
            act.dma_start(cst[:, P:], d["constants"][:, P:]).then_inc(cst_ld, 16)
            act.dma_start(poolw, d["pool_w"].rearrange("g c n -> c g n")).then_inc(poolw_ld, 16)
            act.dma_start(rw[:, :, :], d["router_w"].rearrange("(k p) e -> p k e", p=P)).then_inc(rw_ld, 16)
            act.dma_start(grow[:, :], d["norm_moe_w"].partition_broadcast(P)).then_inc(grow_ld, 16)
            cast_dense(1)
            act.wait_ge(pad_zero, 1)
            for j, n in enumerate(IN_ORDER):
                for step in range(4):
                    if j < 4 and step == 3:
                        for t in range(NT):
                            act.wait_ge(dense_done, result_done(j, t))
                            dst = uT[:, t, PAD:] if n == 4 else proj[:, t, n * 512:(n + 1) * 512]
                            copy(dst, bank[4 * (j % 2) + t][:, :]).then_inc(proj_ev, 1)
                    if (j, step) == (1, 0):
                        act.wait_ge(trig_in, 1)
                        nc.scalar.activation(sin1, ang.rearrange("p (t f) -> p t f", t=NT), ACT.Sin)
                        nc.scalar.activation(cos1, ctmp.rearrange("p (t f) -> p t f", t=NT), ACT.Sin).then_inc(trig_out, 1)
                    if 4 * j + step + 2 < 20:
                        cast_dense(4 * j + step + 2)
            for t in range(NT):
                act.wait_ge(dense_done, result_done(4, t))
                nc.scalar.activation(xr[:, t, 0:512], bank[t][:, :], ACT.Sigmoid).then_inc(silu_sig, 1)
            for n in range(8):
                act.wait_ge(qkT_done, n + 1)
                copy(qkT[:, n // 4, n % 4, :], bank[4 * (1 - n // 4) + n % 4][:, :]).then_inc(qkT_ev, 1)
            for g in range(4):
                high_part(B_POOL + g, 4 + g, bank[g], M["pool_scale"][:, g:g + 1])
            for t in range(NT):
                act.wait_ge(gn_mid, t + 1)
                nc.scalar.activation(tmp4[:, t, 0:512], xr[:, t, 0:512], ACT.Square).then_inc(gn_sq, 1)
            cast_dense(20)
            cast_dense(21)
            for k in range(4):
                high_part(B_RET + k, k, bank[k], M["gn_w"][:, k:k + 1])
            for m in range(22, 28):
                cast_dense(m)

            squares("moe", lambda t: (wo_ev, NT + t + 1))
            act.wait_ge(norm_rows, 2 * NT)
            act.dma_start(xn_dram.rearrange("(t p) n -> p t n", p=P), xr).then_inc(rows_st, 16)
            for k in range(0, KD, 2):
                act.wait_ge(norm_T, k + 1)
                copy(xc[:, k, :], bank[4 + k % 4][:, :]).then_inc(plain_cols[0], 1)
            act.wait_ge(bsplit, 3)
            act.dma_start(bparts[32:64, :], bpart2).then_inc(bp_ld, 16)
            act.dma_start(bparts[64:96, :], bpart3).then_inc(bp_ld, 16)
            act.wait_ge(gexp_in, 1)
            for t in range(NT):
                ins = nc.scalar.activation(gates[:, t * 4:(t + 1) * 4], top8[:, t * 8:t * 8 + 4], ACT.Exp,
                                           bias=negv0[:, t:t + 1], accum_out=gsum[:, t:t + 1])
            act.drain().then_inc(gexp, 1)
            def chunk_src(c):
                return gu_w[c] if c < 8 else dn_w[c - 8].rearrange("p j n -> p (j n)")

            def cast_w(i, c, m, turn):
                act.wait_ge((gu_ld + dn_ld)[c], 16 * i + 16)
                if not isinstance(m, int) or m >= 3:
                    act.wait_ge(w_used, m - 2)
                copy(w_hi[(c + turn) % 3][:, :], chunk_src(c)).then_inc(w_hi_rdy, 1)

            for c in range(2):
                cast_w(0, c, c, 0)
            act.wait_ge(gT_done, 1)
            act.wait_ge(rows_st, 16)
            copy(gT, bank[3][0:E, :]).then_inc(gT_ev, 1)
            act.wait_ge(bd_ev, 8)
            act.dma_start(h_dram[0:2 * P, :].rearrange("(t p) n -> p t n", p=P), h[:, 0:2, :]).then_inc(h_half_st, 16)

            def cols_hi(i, done, ev, dst):
                act.wait_ge(done, i + 1)
                copy(dst[:, 0:512], bank[6][:, :])
                copy(dst[:, 512:1024], bank[7][:, :])
                act.drain().then_inc(ev, 1)

            def sigmoid(i):
                act.wait_ge(g_rdy, i + 1)
                nc.scalar.activation(sig_s, gate_s, ACT.Sigmoid, scale=ALPHA).then_inc(sig_rdy, 1)

            def store_y(i, used):
                act.wait_ge(w_used, used)
                copy(y_s[:, 0:512], bank[4][:, :])
                copy(y_s[:, 512:1024], bank[5][:, :])
                act.drain().then_inc(y_free, 1)
                act.dma_start(y_dram[ds(i * P, P), :], y_s).then_inc(y_st, 16)

            def item(i):
                m = 12 * i - 4
                for c in range(3):
                    cast_w(i, c, m + c, 2)
                if not isinstance(i, int):
                    store_y(i - 2, 12 * i - 4)
                for c in range(3, 7):
                    cast_w(i, c, m + c, 2)
                cols_hi(i - 1, actT_done, actT_hi_ev, actT_hi)
                cast_w(i, 7, m + 7, 2)
                for c in (8, 9, 10):
                    cast_w(i - 1, c, m + c, 2)
                cols_hi(i + 1, xgT_done, xgT_hi_ev, xgT_hi)
                sigmoid(i)
                cast_w(i - 1, 11, m + 11, 2)
                if not isinstance(i, int):
                    act.wait_ge(y_st, 16 * i - 16)

            act.nop().then_inc(y_free, 1)
            act.wait_ge(item_rdy, 1)
            last = act.value_load(last_item[0:1, 0:1], min_val=E - 1, max_val=NITEM - 2)
            cast_w(0, 2, 2, 0)
            cols_hi(0, xgT_done, xgT_hi_ev, xgT_hi)
            for c in range(3, 8):
                cast_w(0, c, c, 0)
            cols_hi(1, xgT_done, xgT_hi_ev, xgT_hi)
            sigmoid(0)
            item(1)
            with act.Fori(2, last + 1) as i:
                item(i)
            for c in (8, 9):
                cast_w(last, c, 12 * last + c, 0)
            store_y(last - 1, 12 * last + 8)
            cols_hi(last, actT_done, actT_hi_ev, actT_hi)
            for c in (10, 11):
                cast_w(last, c, 12 * last + c, 0)
            act.wait_ge(y_st, 16 * last)
            store_y(last, 12 * last + 12)

            act.wait_ge(y_st, 16 * last + 16)
            act.dma_start(grow[:, :], d["final_norm_w"].partition_broadcast(P)).then_inc(grow2_ld, 16)
            act.drain().then_inc(y_all, 1)
            for k in range(2):
                act.wait_ge(pT_done, k + 1)
                copy(p_cols[:, k, :], bank[k][:, :]).then_inc(pT_ev, 1)
            for g in range(8):
                act.wait_ge(pp_done, g + 1)
                copy(pproj[:, g, :], bank[g % 4][:, :]).then_inc(pp_ev, 1)
            squares("ple", lambda t: (combined, t + 1))
            cast_dense(28)
            cast_dense(29)
            high_parts(B_PLE, 4, M["g_ple"])
            for n in range(2):
                for step in range(4):
                    if n and step == 0:
                        for t in range(NT):
                            act.wait_ge(dense_done, result_done(L_PLE, t))
                            nc.scalar.activation(gate_sig[t], bank[t][:, :], ACT.Sigmoid).then_inc(plg_sig, 1)
                    if 4 * n + step + 30 < 36:
                        cast_dense(4 * n + step + 30)
            for t in range(NT):
                act.wait_ge(dense_done, result_done(L_PLE + 1, t))
                act.wait_ge(ple_ev, t + 1)
                nc.scalar.activation(gate_sig[t], bank[4 + t][:, :], ACT.Sigmoid).then_inc(plg_sig, 1)
            squares("fin", lambda t: (ple_ev, NT + t + 1))
            squares("two", lambda t: (final_rdy, t + 1))
            cast_dense(36)
            cast_dense(37)
            act.wait_ge(norm_rows, NT * (NORM["two"] + 1))
            act.dma_start(h_dram.rearrange("(t p) n -> p t n", p=P), h[:, :, :]).then_inc(h_st, 16)
            high_parts(B_TWO, 4, M["gain2"])

            def turned(n, dst, gain=1.0):
                act.wait_ge(turn_done, n + 1)
                copy(dst, bank[4 + n % 2][:, :], gain).then_inc(turn_ev, 1)

            def index_relu(q):
                for u in range(4 * q, 4 * q + 4):
                    t = 1 + u // HEADS
                    act.wait_ge(ix_done, u + 1)
                    if u >= 2:
                        act.wait_ge(ix_acc, u - 1)
                    nc.scalar.activation(ix_rel[u % 2][:, 0:P * (t + 1)], bank[6 + u % 2][:, 0:P * (t + 1)], ACT.Relu
                                         ).then_inc(ix_relu, 1)

            def projected(j):
                n = IN2_ORDER[j]
                w = min(512, D_IN2 - n * 512)
                for t in range(NT):
                    act.wait_ge(dense_done, result_done(dense_no(L_IN2 + j), t))
                    copy(pr2[:, t, n * 512:n * 512 + w], bank[t][:, 0:w]).then_inc(pr2_ev, 1)

            def squares_qk(w):
                act.wait_ge(pr2_ev, 4 * (IN2_ORDER.index(w) + 1))
                nc.scalar.activation(hspill[:, 0:2048].rearrange("p (t n) -> p t n", t=NT), pr2[:, :, w * 512:(w + 1) * 512],
                                     ACT.Square).then_inc(qk_sq, 1)

            act.wait_ge(h_st, 16)
            for j in range(NCH2):
                for step in range(4):
                    m = 4 * dense_no(L_IN2 + j) + step
                    if step == 3:
                        projected(j)
                    if (j, step) == INDEX_TURN:
                        for b in range(4):
                            turned(T_IX + b, qiT[:, b, :])
                        turned(T_IX + 4, kiT)
                    if (j, step) == (3, 0):
                        act.wait_ge(ix_rdy, 1)
                        squares_qk(0)
                    if (j, step) == (4, 2):
                        act.wait_ge(qa_rdy, 1)
                        squares_qk(1)
                    if (j, step) == (5, 1):
                        act.wait_ge(pr2_ev, 4 * (IN2_ORDER.index(6) + 1))
                        for i, (c, n) in enumerate(((C_CQ, Q_LORA), (C_CKV, KV_LORA))):
                            for t in range(NT):
                                nc.scalar.activation(lat_junk[:, 0:n], pr2[:, t, c:c + n], ACT.Square,
                                                     accum_out=lat_sum[:, i * NT + t:i * NT + t + 1])
                                act.drain().then_inc(lat_sq, 1)
                    for q in range(6):
                        if (j, step) == INDEX_SCORES[q]:
                            index_relu(q)
                    if 4 * j + step + 2 < 4 * NCH2:
                        cast_dense(m + 2)
            for w in range(2):
                for b in range(4):
                    turned((T_QA, T_KA)[w] + b, qkaT[:, w, b, :])
            for b in range(5):
                turned(T_LAT + b, lat_cols[:, b, :], M["bq_lat"][:, b:b + 1] if b < 3 else M["bkv_lat"][:, b - 3:b - 2])

            act.wait_ge(qa_rdy, 2)
            for g in range(8):
                nc.scalar.activation(out_sig[:, g, :], out_gate(g), ACT.Sigmoid).then_inc(gate_sg, 1)

            def turned_heads(t, w):
                for half in range(2):
                    n = T_B + 4 * t + 2 * w + half
                    act.wait_ge(turn_done, n + 1)
                    if w:
                        dst = kbT[:, 4 * half:4 * half + 4, t * P:(t + 1) * P]
                    elif half:
                        dst = qiT[:, :, t * P:(t + 1) * P]
                    else:
                        dst = pr2[:, :, C_KA + t * P:C_KA + (t + 1) * P]
                    copy(dst[0:DQ_B], bank[6 + half][0:DQ_B, :].rearrange("p (a n) -> p a n", a=4)).then_inc(turn_ev, 1)

            def squares_b(n, row):
                if n:
                    act.wait_ge(bsq_used, n)
                nc.scalar.activation(bsq, row.rearrange("p (a n) -> p a n", a=HEADS), ACT.Square).then_inc(bsq_rdy, 1)

            def latent_step(u):
                t, step = u // 8, u % 8
                if step == 0 and t:
                    turned_heads(t - 1, 1)
                if step == 0 and t < NT:
                    act.wait_ge(qb_done, t + 1)
                    copy(qrow[:, 0:512], bank[6][:, :])
                    copy(qrow[:, 512:768], bank[7][:, 0:256]).then_inc(qb_ev, 1)
                    act.wait_ge(qb_ev, t + 1)
                    squares_b(2 * t, qrow)
                if step == 1:
                    act.wait_ge(kv_done, t + 1)
                    for half in range(2):
                        src = bank[6 + half][:, :].rearrange("p (a n) -> p a n", a=4)
                        copy(pr2[:, t, C_QI + half * 256:C_QI + (half + 1) * 256].rearrange("p (a n) -> p a n", a=4),
                             src[:, :, 64:128])
                        copy(krow[:, half * 384:(half + 1) * 384].rearrange("p (a n) -> p a n", a=4)[:, :, 0:64],
                                   src[:, :, 0:64])
                    copy(krow.rearrange("p (a n) -> p a n", a=HEADS)[:, :, 64:96],
                         pr2[:, t, C_KR:C_KR + 32].unsqueeze(1).to_broadcast([P, HEADS, 32])).then_inc(k_ev, 1)
                if step == 2:
                    act.wait_ge(k_ev, t + 1)
                    squares_b(2 * t + 1, krow)
                if step == 6:
                    turned_heads(t, 0)

            def unit(u):
                t = u // 8 % 4
                return t, P * (t + 1)

            def exponentials(u):
                t, w = unit(u)
                act.wait_ge(at_s, u + 1)
                nc.scalar.activation(sS[u % 3][:, 0:w], sS[u % 3][:, 0:w], ACT.Exp, bias=nmax[:, u % 4:u % 4 + 1],
                                     scale=-1.0, accum_out=rs_all[:, u % 16:u % 16 + 1]).then_inc(at_exp, 1)

            def at_copy(u):
                t, w = unit(u)
                act.wait_ge(pT2_done, u + 1)
                if u >= 2:
                    act.wait_ge(pv_done, u - 1)
                copy(sPT[u % 2][:, 0:t + 1, :], bank[2 + u % 2][:, 0:w].rearrange("p (j n) -> p j n", j=t + 1)
                     ).then_inc(pT2_ev, 1)

            for u in range(64 + 2):
                if 1 <= u <= 64:
                    if (u - 1) % 8 == 0 and u > 16:
                        act.wait_ge(o_ev, (u - 1) // 8 - 1)
                    exponentials(u - 1)
                if u >= 2:
                    at_copy(u - 2)
                if u <= 32:
                    latent_step(u)
            for m in (68, 69):
                cast_dense(m)
            high_parts(B_OUT, 0)
            for m in range(70, 76):
                cast_dense(m)
            for t in range(NT):
                act.wait_ge(out_rdy, NT + t + 1)
                act.dma_start(d["out"][t * P:(t + 1) * P, :], h[:, t, :]).then_inc(out_st, 16)
            act.wait_ge(out_st, 16 * NT)

        @block.vector
        def _(dve):
            v = nc.vector
            D_ = dve.drain

            asked = [0]

            def ask_rsqrt():
                asked[0] += 1
                dve.drain().then_inc(sums_rdy, 1)

            def get_rsqrt():
                dve.wait_ge(rstd_rdy, asked[0])

            def rsqrt_mean():
                ask_rsqrt()
                get_rsqrt()

            def by_tile(n, apply):
                base = NT * SQ[n]
                dve.wait_ge(norm_sq, base + 1)
                ask_rsqrt()
                for t in range(NT):
                    rdy = asked[0]
                    if t + 1 < NT:
                        dve.wait_ge(norm_sq, base + t + 2)
                        ask_rsqrt()
                    dve.wait_ge(rstd_rdy, rdy)
                    apply(t)

            def norm_to_rows(n, gain=None):
                def apply(t):
                    if gain is None:
                        ins = v.tensor_scalar(xr[:, t, :], h[:, t, :], rstd[:, t:t + 1], None, ALU.mult)
                    else:
                        ins = v.scalar_tensor_tensor(out=xr[:, t, :], in0=h[:, t, :], scalar=rstd[:, t:t + 1],
                                                     in1=gain, op0=ALU.mult, op1=ALU.mult)
                    ins.then_inc(norm_rows, 1)
                by_tile(n, apply)

            def rest(n, k, b, gain=None):
                dve.wait_ge(hi_ev, n + 1)
                src = b[:, :].rearrange("p (t n) -> p t n", t=NT)
                out = x_lo[:, :, k * P:(k + 1) * P]
                hi = x_hi[:, k, :].bitcast(F32).rearrange("p (t n) -> p t n", t=NT)
                if gain is None:
                    ins = v.tensor_tensor(out, src, hi, ALU.subtract)
                else:
                    ins = v.scalar_tensor_tensor(out=out, in0=src, scalar=gain, in1=hi, op0=ALU.mult, op1=ALU.subtract)
                ins.then_inc(lo_ev, 1)

            def rests(first, b0, gain=None):
                for k in range(KD):
                    rest(first + k, k, bank[b0 + k % 4], gain[:, k:k + 1] if gain is not None else None)

            def rest_dense(m):
                L, b, w = step_chunk(m)
                if m % 4 == 0:
                    dve.wait_ge(w_ld[L % 2], 16 * (L // 2 + 1))
                dve.wait_ge(dense_hi_rdy, m + 1)
                if m >= 2:
                    dve.wait_ge(dense_done, step_used(m - 2))
                hi, lo = (a[b][m % 2][:, 0:2 * w].rearrange("p (k n) -> p k n", k=2) for a in (dense_hi, dense_lo))
                v.tensor_tensor(lo, wview(L)[:, 2 * (m % 4):2 * (m % 4) + 2, :], hi.bitcast(F32), ALU.subtract
                                ).then_inc(dense_lo_rdy, 1)

            def rope(x1, x2, cos, sin, t):
                v.tensor_tensor(t[0], x1, cos, ALU.mult)
                v.tensor_tensor(t[1], x2, sin, ALU.mult)
                v.tensor_tensor(t[2], x2, cos, ALU.mult)
                v.tensor_tensor(t[3], x1, sin, ALU.mult)
                D_()
                v.tensor_tensor(x1, t[0], t[1], ALU.subtract)
                return v.tensor_tensor(x2, t[2], t[3], ALU.add)

            def over(ap, axis, n):
                u = ap.unsqueeze(axis)
                shape = list(u.shape)
                shape[axis] = n
                return u.to_broadcast(shape)

            def angles():
                dve.wait_ge(cst_ld, 16)
                dve.wait_ge(small_ld, 32)
                v.tensor_copy(posf, posi)
                D_()
                a3 = ang.rearrange("p (t f) -> p t f", t=NT)
                v.tensor_tensor(a3, over(posf, 2, HALF_A), over(C["invfreq"], 1, NT), ALU.mult)
                D_()
                v.tensor_scalar(turns, ang, float(1 / TWO_PI), ROUND, ALU.mult, ALU.add)
                D_()
                v.tensor_scalar(turns, turns, ROUND, None, ALU.subtract)
                D_()
                for part in (PI_A, PI_B, PI_C):
                    v.scalar_tensor_tensor(out=ang, in0=turns, scalar=-part, in1=ang, op0=ALU.mult, op1=ALU.add)
                    D_()
                v.tensor_scalar(ang, ang, 3.1415925, -3.1415925, ALU.min, ALU.max)
                D_()
                v.scalar_tensor_tensor(out=ctmp, in0=ang, scalar=-1.0, in1=ang, op0=ALU.mult, op1=ALU.max)
                D_()
                v.tensor_scalar(ctmp, ctmp, -1.0, float(np.pi / 2), ALU.mult, ALU.add).then_inc(trig_in, 1)

            norm_to_rows("mix")
            dve.wait_ge(small_ld, 32)
            rests(B_MIX, 4, M["g_mix"])
            rest_dense(0)
            rest_dense(1)
            t4 = [tmp4[:, b, :].rearrange("p (t a f) -> p t a f", t=NT, a=HEADS) for b in range(4)]

            def rope_piece(w, piece):
                x = proj[:, :, w * D_RET:(w + 1) * D_RET].rearrange("p t (a f) -> p t a f", a=HEADS)
                x1, x2 = x[:, :, :, 0:HALF_A], x[:, :, :, HALF_A:DH]
                cos, sin = over(cos1, 2, HEADS), over(sin1, 2, HEADS)
                if piece == 0:
                    dve.wait_ge(proj_ev, 4 * w + 4)
                    dve.wait_ge(trig_out, 1)
                    v.tensor_tensor(t4[0], x1, cos, ALU.mult)
                    v.tensor_tensor(t4[1], x2, sin, ALU.mult)
                if piece == 1:
                    v.tensor_tensor(t4[2], x2, cos, ALU.mult)
                    v.tensor_tensor(t4[3], x1, sin, ALU.mult)
                    D_()
                if piece == 2:
                    v.tensor_tensor(x1, t4[0], t4[1], ALU.subtract)
                    v.tensor_tensor(x2, t4[2], t4[3], ALU.add)
                    D_()
                if piece == 3:
                    g = C[("gq", "gk")[w]].rearrange("p (t a) -> p t a", t=NT)
                    v.tensor_tensor(x, x, over(g, 3, DH), ALU.mult).then_inc(rope_done, 1)

            for j in range(5):
                for step in range(4):
                    if (j, step) == (0, 3):
                        angles()
                    n = 4 * j + step - 5
                    if 0 <= n < 8:
                        rope_piece(n // 4, n % 4)
                    if 4 * j + step + 2 < 20:
                        rest_dense(4 * j + step + 2)
            for t in range(NT):
                dve.wait_ge(silu_sig, t + 1)
                v.tensor_tensor(proj[:, t, 1536:2048], bank[t][:, :], xr[:, t, 0:512], ALU.mult).then_inc(gate_ev, 1)
            for n in range(32):
                j = n % 4
                dve.wait_ge(sc_done, n + 1)
                w = S - j * P
                v.tensor_tensor(scT[:, n // 4 % 2, j, j * P:S], bank[j][:, 0:w], C["causal"][:, 0:w], ALU.mult
                                ).then_inc(sc_ev, 1)
            dve.wait_ge(y1_done, 1)
            y = [bank[4 + t][:, :].rearrange("p (a n) -> p a n", a=HEADS) for t in range(NT)]
            yc = [xr[:, t, 0:512].rearrange("p (a n) -> p a n", a=HEADS) for t in range(NT)]
            for t in range(NT):
                v.tensor_reduce(mu[:, t * 8:(t + 1) * 8], y[t], X, ALU.add)
            D_()
            v.tensor_scalar(mu, mu, 1.0 / DH, None, ALU.mult)
            D_()
            for t in range(NT):
                v.tensor_tensor(yc[t], y[t], over(mu[:, t * 8:(t + 1) * 8], 2, DH), ALU.subtract).then_inc(gn_mid, 1)
            for t in range(NT):
                dve.wait_ge(gn_sq, t + 1)
                v.tensor_reduce(var[:, t * 8:(t + 1) * 8], tmp4[:, t, 0:512].rearrange("p (a n) -> p a n", a=HEADS), X, ALU.add)
                ask_rsqrt()
                rest(B_POOL + t, 4 + t, bank[t], M["pool_scale"][:, t:t + 1])
            for t in range(NT):
                dve.wait_ge(rstd_rdy, asked[0] - NT + t + 1)
                v.tensor_tensor(yc[t], yc[t], over(var[:, t * 8:(t + 1) * 8], 2, DH), ALU.mult)
            D_()
            for t in range(NT):
                v.tensor_tensor(xr[:, t, 0:512], xr[:, t, 0:512], proj[:, t, 1536:2048], ALU.mult).then_inc(ret_rows, 1)
            rest_dense(20)
            rest_dense(21)
            for k in range(4):
                rest(B_RET + k, k, bank[k], M["gn_w"][:, k:k + 1])
            for m in range(22, 28):
                rest_dense(m)
            for g in range(8):
                n, t = g // 4, g % 4
                dve.wait_ge(dense_done, result_done(5 + n, t))
                hv = h[:, t, n * 512:(n + 1) * 512]
                v.tensor_tensor(hv, hv, bank[4 * (1 - n) + t][:, :], ALU.add).then_inc(wo_ev, 1)

            dve.wait_ge(grow_ld, 16)
            norm_to_rows("moe", grow[:, :])
            for k in range(1, KD, 2):
                dve.wait_ge(norm_T, k + 1)
                v.tensor_copy(xc[:, k, :], bank[4 + k % 4][:, :]).then_inc(plain_cols[1], 1)
            dve.wait_ge(braw_ld, 16)
            v.tensor_copy(bparts[0:E, :], braw).then_inc(bsplit, 1)
            D_()
            for out, left in ((bpart2, bparts[0:E, :]), (bpart3, bpart2)):
                v.tensor_tensor(braw, braw, left, ALU.subtract)
                D_()
                v.tensor_copy(out, braw).then_inc(bsplit, 1)
                D_()
            dve.wait_ge(lg_done, 1)
            v.tensor_tensor(logits, bank[0][:, 0:NT * E].rearrange("p (t e) -> p t e", e=E), over(M["router_b"], 1, NT), ALU.add)
            D_()
            for t in range(NT):
                v.max(top8[:, t * 8:(t + 1) * 8], logits[:, t, :])
                D_()
                v.max_index(idx8[:, t * 8:(t + 1) * 8], top8[:, t * 8:(t + 1) * 8], logits[:, t, :])
            D_()
            t8 = top8.rearrange("p (t a) -> p t a", a=8)
            v.tensor_scalar(negv0.unsqueeze(2), t8[:, :, 0:1], -1.0, None, ALU.mult).then_inc(gexp_in, 1)
            idxf = more[:, 0:16]
            v.tensor_copy(idxf.rearrange("p (t a) -> p t a", a=TOPK), idx8.rearrange("p (t a) -> p t a", a=8)[:, :, 0:TOPK])
            D_()
            v.tensor_tensor(onehot, over(C["iota32"], 1, 16), over(idxf, 2, E), ALU.is_equal)
            D_()
            v.tensor_reduce(member, onehot.rearrange("p (t a) e -> p t e a", t=NT), X, ALU.add).then_inc(member_rdy, 1)
            dve.wait_ge(gexp, 1)
            v.reciprocal(gsum, gsum)
            D_()
            g3 = gates.rearrange("p (t a) -> p t a", a=TOPK)
            v.tensor_tensor(g3, g3, over(gsum, 2, TOPK), ALU.mult)
            D_()
            v.tensor_tensor(prod, onehot, over(gates, 2, E), ALU.mult)
            D_()
            v.tensor_reduce(gdense, prod.rearrange("p (t a) e -> p t e a", t=NT), X, ALU.add).then_inc(gd_rdy, 1)
            dve.wait_ge(rank_done, 1)
            dve.wait_ge(yzero_st, 16)
            cnt = bank[2][:, 0:E]
            v.tensor_scalar(nblk, cnt, float(P), 1.0, ALU.is_gt, ALU.add)
            D_()
            for m in (2, 3):
                v.tensor_scalar(more, cnt, float(m * P), None, ALU.is_gt)
                D_()
                v.tensor_tensor(nblk, nblk, more, ALU.add)
                D_()
            v.tensor_tensor_scan(incl, C["ones"][:, 0:E], nblk, 0.0, ALU.mult, ALU.add)
            D_()
            v.tensor_scalar(last_item, incl[:, E - 1:E], 1.0, None, ALU.subtract)
            v.tensor_tensor(base, incl, nblk, ALU.subtract)
            v.tensor_tensor(cmp48, over(incl, 1, NITEM), over(C["iota48"], 2, E), ALU.is_le)
            D_()
            v.tensor_scalar(base, base, float(P), None, ALU.mult)
            v.tensor_reduce(item_e, cmp48, X, ALU.add)
            D_()
            v.tensor_scalar(item_e, item_e, float(E - 1), None, ALU.min)
            slot3 = logits
            v.tensor_tensor(slot3, bank[1][:, 0:NT * E].rearrange("p (t e) -> p t e", e=E), over(base, 1, NT), ALU.add)
            D_()
            v.tensor_copy(item_ei, item_e)
            v.tensor_tensor(prod.rearrange("p (t a) e -> p t a e", t=NT), onehot.rearrange("p (t a) e -> p t a e", t=NT),
                            over(slot3, 2, TOPK), ALU.mult)
            D_()
            slotf, placef = more[:, 0:16], more[:, 16:32]
            v.tensor_reduce(slotf, prod, X, ALU.add)
            v.tensor_copy(tok_i, C["tok"])
            D_()
            v.tensor_copy(slot_u, slotf)
            D_()
            v.tensor_scalar(place_u, slot_u, 7, None, ALU.logical_shift_right)
            v.tensor_scalar(idx8[:, 0:16], slot_u, P - 1, None, ALU.bitwise_and)
            D_()
            v.tensor_copy(placef, place_u)
            v.tensor_copy(slotf, idx8[:, 0:16])
            D_()
            v.scalar_tensor_tensor(out=placef, in0=slotf, scalar=float(NITEM), in1=placef, op0=ALU.mult, op1=ALU.add)
            D_()
            v.tensor_copy(place_u, placef)
            dve.drain().then_inc(place_rdy, 1)
            dve.drain().then_inc(item_rdy, 1)

            def rest_w(i, c, m, turn):
                dve.wait_ge((gu_ld + dn_ld)[c], 16 * i + 16)
                dve.wait_ge(w_hi_rdy, m + 1)
                if not isinstance(m, int) or m >= 3:
                    dve.wait_ge(w_used, m - 2)
                src = gu_w[c] if c < 8 else dn_w[c - 8].rearrange("p j n -> p (j n)")
                v.tensor_tensor(w_lo[(c + turn) % 3][:, :], src, w_hi[(c + turn) % 3][:, :].bitcast(F32), ALU.subtract).then_inc(w_lo_rdy, 1)

            dve.wait_ge(bp_ld, 32)
            for c in range(2):
                rest_w(0, c, c, 0)
            for g in range(8):
                n, t = g // 4, g % 4
                dve.wait_ge(bd_done, g + 1)
                hv = h[:, t, n * 512:(n + 1) * 512]
                v.tensor_tensor(hv, hv, bank[4 + t][:, :], ALU.add).then_inc(bd_ev, 1)
            def pick(i):
                v.tensor_scalar(sel_e[:, :], item_e[0:96, ds(i, 1)].to_broadcast([96, P]), C["pmod"][0:96, :], None,
                                ALU.is_equal).then_inc(sel_rdy, 1)

            def cols_lo(i, hi_ev, ev, hi, lo):
                dve.wait_ge(hi_ev, i + 1)
                for n in range(2):
                    cut = slice(n * 512, (n + 1) * 512)
                    v.tensor_tensor(lo[:, cut], bank[6 + n][:, :], hi[:, cut].bitcast(F32), ALU.subtract)
                dve.drain().then_inc(ev, 1)

            def clamp(i):
                dve.wait_ge(gu_done, i + 1)
                for n in range(4):
                    pair = bank[n][:, :].rearrange("p (n two) -> p n two", two=2)
                    v.tensor_scalar(gate_s[:, n * 256:(n + 1) * 256].unsqueeze(2), pair[:, :, 0:1], LIMIT, None, ALU.min)
                dve.drain().then_inc(g_rdy, 1)
                for n in range(4):
                    pair = bank[n][:, :].rearrange("p (n two) -> p n two", two=2)
                    v.tensor_scalar(up_s[:, n * 256:(n + 1) * 256].unsqueeze(2), pair[:, :, 1:2], LIMIT, -LIMIT, ALU.min, ALU.max)
                dve.drain().then_inc(gu_ev, 1)

            def up_times_gate():
                v.scalar_tensor_tensor(out=up_s, in0=up_s, scalar=1.0, in1=gate_s, op0=ALU.add, op1=ALU.mult)

            def times_sigmoid(i):
                dve.wait_ge(sig_rdy, i + 1)
                v.tensor_tensor(up_s, up_s, sig_s, ALU.mult).then_inc(act_rdy, 1)

            pick(0)
            last = dve.value_load(last_item[0:1, 0:1], min_val=E - 1, max_val=NITEM - 2)
            dve.wait_ge(h_half_st, 16)
            rest_w(0, 2, 2, 0)
            cols_lo(0, xgT_hi_ev, xgT_ev, xgT_hi, xgT_lo)
            for c in range(3, 8):
                rest_w(0, c, c, 0)
            clamp(0)
            cols_lo(1, xgT_hi_ev, xgT_ev, xgT_hi, xgT_lo)
            pick(1)
            with dve.Fori(1, last + 1) as i:
                m = 12 * i - 4
                rest_w(i, 0, m, 2)
                up_times_gate()
                rest_w(i, 1, m + 1, 2)
                D_()
                times_sigmoid(i - 1)
                for c in range(2, 6):
                    rest_w(i, c, m + c, 2)
                cols_lo(i - 1, actT_hi_ev, actT_ev, actT_hi, actT_lo)
                for c in (6, 7):
                    rest_w(i, c, m + c, 2)
                for c in (8, 9, 10):
                    rest_w(i - 1, c, m + c, 2)
                clamp(i)
                cols_lo(i + 1, xgT_hi_ev, xgT_ev, xgT_hi, xgT_lo)
                pick(i + 1)
                rest_w(i - 1, 11, m + 11, 2)
            up_times_gate()
            D_()
            times_sigmoid(last)
            for c in (8, 9):
                rest_w(last, c, 12 * last + c, 0)
            cols_lo(last, actT_hi_ev, actT_ev, actT_hi, actT_lo)
            for c in (10, 11):
                rest_w(last, c, 12 * last + c, 0)

            def combine(t):
                dve.wait_ge(yg_ld[t], 16 * TOPK)
                for a in range(4 * t, 4 * t + 4):
                    ins = v.scalar_tensor_tensor(out=h[:, t, :], in0=ygat[:, a, :], scalar=gates[:, a:a + 1], in1=h[:, t, :],
                                                 op0=ALU.mult, op1=ALU.add)
                    if a % 4 < 3:
                        D_()
                ins.then_inc(combined, 1)

            def ask_norm(t):
                dve.wait_ge(norm_sq, NT * SQ["ple"] + t + 1)
                ask_rsqrt()

            def ple_rows(t):
                get_rsqrt()
                v.tensor_scalar(xr[:, t, :], h[:, t, :], rstd[:, t:t + 1], None, ALU.mult).then_inc(norm_rows, 1)

            dve.wait_ge(h_half_ld, 16)
            combine(0)
            for t in range(1, NT):
                combine(t)
                if t > 1:
                    ple_rows(t - 2)
                ask_norm(t - 1)
            ple_rows(NT - 2)
            ask_norm(NT - 1)
            ple_rows(NT - 1)
            rest_dense(28)
            rest_dense(29)
            rests(B_PLE, 4, M["g_ple"])

            def gated(g):
                n, t = g // 4, g % 4
                hv = h[:, t, n * 512:(n + 1) * 512]
                dve.wait_ge(plg_sig, g + 1)
                v.tensor_tensor(pproj[:, g, :], pproj[:, g, :], gate_sig[t], ALU.mult)
                D_()
                v.tensor_tensor(hv, hv, pproj[:, g, :], ALU.add).then_inc(ple_ev, 1)

            for m in range(30, 34):
                rest_dense(m)
            for g in range(4):
                gated(g)
                if g < 2:
                    rest_dense(34 + g)
            for g in range(4, 8):
                gated(g)
            dve.wait_ge(grow2_ld, 16)

            def final(t):
                v.scalar_tensor_tensor(out=h[:, t, :], in0=h[:, t, :], scalar=rstd[:, t:t + 1], in1=grow[:, :],
                                       op0=ALU.mult, op1=ALU.mult).then_inc(final_rdy, 1)

            by_tile("fin", final)
            norm_to_rows("two")
            rest_dense(36)
            rest_dense(37)
            rests(B_TWO, 4, M["gain2"])
            ci = C["cos_i"].rearrange("p (t f) -> p t f", t=NT)
            si = C["sin_i"].rearrange("p (t f) -> p t f", t=NT)
            xi = pr2[:, :, C_QI:C_QI + 512].rearrange("p t (a f) -> p t a f", a=HEADS)
            i4 = [rot[:, b, 0:512].rearrange("p (t a f) -> p t a f", t=NT, a=HEADS) for b in range(4)]
            xk = pr2[:, :, C_KI:C_KI + 64]
            k4 = [rot[:, b, 512:576].rearrange("p (t f) -> p t f", t=NT) for b in range(4)]

            def index_heads():
                rope(xk[:, :, 0:16], xk[:, :, 16:32], ci, si, k4)
                rope(xi[:, :, :, 0:16], xi[:, :, :, 16:32], over(ci, 2, HEADS), over(si, 2, HEADS), i4)
                v.tensor_scalar(wi_s.rearrange("p (t a) -> p t a", t=NT), pr2[:, :, C_WI:C_WI + 8], float((64 * 8) ** -0.5), None, ALU.mult)
                v.tensor_copy(ki2[:, :, 0:64], xk)
                v.tensor_copy(ki2[:, :, 64:128], xk)
                dve.drain().then_inc(ix_rdy, 1)
                v.tensor_copy(selbias[:, 0, 0:P], C["chunkbias"][:, S - P:S])

            def index_sum(q):
                for u in range(4 * q, 4 * q + 4):
                    t, hd = 1 + u // HEADS, u % HEADS
                    w = P * (t + 1)
                    acc, rel = index_acc[t - 1][:, 0:w], ix_rel[u % 2][:, 0:w]
                    wcol = wi_s[:, t * 8 + hd:t * 8 + hd + 1]
                    dve.wait_ge(ix_relu, u + 1)
                    if hd == 0:
                        v.tensor_scalar(acc, rel, wcol, None, ALU.mult).then_inc(ix_acc, 1)
                    else:
                        v.scalar_tensor_tensor(out=acc, in0=rel, scalar=wcol, in1=acc, op0=ALU.mult, op1=ALU.add
                                               ).then_inc(ix_acc, 1)
                    D_()

            def keep_keys(rounds):
                for r in rounds:
                    t = 1 + r // (KEEP // 8)
                    w = P * (t + 1)
                    acc = index_acc[t - 1][:, 0:w]
                    if r % (KEEP // 8) == 0:
                        v.tensor_tensor(acc, acc, C["chunkbias"][:, S - w:S], ALU.add)
                        D_()
                    v.max(top8[:, 0:8], acc)
                    D_()
                    v.match_replace(acc, top8[:, 0:8], acc, TAKEN)
                    D_()
                    if r % (KEEP // 8) == KEEP // 8 - 1:
                        v.tensor_scalar(selbias[:, t, 0:w], acc, TAKEN / 2, NEG, ALU.is_gt, ALU.mult)
                        D_()

            r4 = [rot[:, b, :].rearrange("p (t a f) -> p t a f", t=NT, a=HEADS) for b in range(4)]
            ca = over(C["cos_a"].rearrange("p (t f) -> p t f", t=NT), 2, HEADS)
            sa = over(C["sin_a"].rearrange("p (t f) -> p t f", t=NT), 2, HEADS)

            def qk_piece(w, piece):
                x4 = pr2[:, :, w * 512:(w + 1) * 512].rearrange("p t (a f) -> p t a f", a=HEADS)
                x1, x2 = x4[:, :, :, 0:HALF_A], x4[:, :, :, HALF_A:DH]
                if piece == 0:
                    dve.wait_ge(qk_sq, w + 1)
                    v.tensor_reduce(mu, hspill[:, 0:2048].rearrange("p (a f) -> p a f", f=DH), X, ALU.add)
                    ask_rsqrt()
                if piece == 1:
                    get_rsqrt()
                    v.tensor_tensor(x4, x4, over(mu.rearrange("p (t a) -> p t a", t=NT), 3, DH), ALU.mult)
                    D_()
                if piece == 2:
                    for t in range(NT):
                        v.tensor_tensor(x4[:, t], x4[:, t], over(M[("aq", "ak")[w]], 1, HEADS), ALU.mult)
                    D_()
                if piece == 3:
                    v.tensor_tensor(r4[0], x1, ca, ALU.mult)
                    v.tensor_tensor(r4[1], x2, sa, ALU.mult)
                    v.tensor_tensor(r4[2], x2, ca, ALU.mult)
                    v.tensor_tensor(r4[3], x1, sa, ALU.mult)
                    D_()
                if piece == 4:
                    v.tensor_tensor(x1, r4[0], r4[1], ALU.subtract)
                    v.tensor_tensor(x2, r4[2], r4[3], ALU.add).then_inc(qa_rdy, 1)
                    D_()

            def latent_norms():
                for j, (c, n) in enumerate(((C_CQ, Q_LORA), (C_CKV, KV_LORA))):
                    x = pr2[:, :, c:c + n]
                    v.tensor_tensor(x, x, over(lat_sum[:, j * NT:(j + 1) * NT], 2, n), ALU.mult).then_inc(lat_rdy, 1)

            for j in range(NCH2):
                for step in range(4):
                    m = 4 * dense_no(L_IN2 + j) + step
                    for q in range(6):
                        if (j, step) == INDEX_SCORES[q]:
                            index_sum(q)
                    if 4 * j + step + 2 < 4 * NCH2:
                        rest_dense(m + 2)
                    if (j, step) == (2, 0):
                        dve.wait_ge(h_st, 16)
                        dve.wait_ge(pr2_ev, 4 * 2)
                        index_heads()
                    if (3, 1) <= (j, step) <= (4, 1):
                        qk_piece(0, 4 * j + step - 13)
                    if (j, step) == (5, 0):
                        qk_piece(1, 0)
                    if (4, 2) <= (j, step) <= (6, 1):
                        n = 4 * j + step - 18
                        keep_keys(range((0, 4, 8, 10, 14, 17, 20, 23)[n], (4, 8, 10, 14, 17, 20, 23, 26)[n]))
                    if (j, step) in ((6, 3), (7, 2), (7, 3)):
                        n = 26 + 2 * ((6, 3), (7, 2), (7, 3)).index((j, step))
                        keep_keys(range(n, n + 2))
                    if (j, step) == (6, 2):
                        get_rsqrt()
                        qk_piece(1, 3)
                    if (j, step) == (6, 3):
                        dve.wait_ge(lat_sq, 2 * NT)
                        ask_rsqrt()
                        ask_rsqrt()
                        qk_piece(1, 4)
                    if (j, step) == (7, 1):
                        get_rsqrt()
                        latent_norms()
            dve.wait_ge(pr2_ev, 4 * NCH2)

            def head_rows(w):
                return (qrow, krow)[w].rearrange("p (a n) -> p a n", a=HEADS)

            def sum_squares(t, w):
                dve.wait_ge(bsq_rdy, 2 * t + w + 1)
                v.tensor_reduce(mu[:, 8 * w:8 * w + 8], bsq, X, ALU.add).then_inc(bsq_used, 1)
                ask_rsqrt()

            def turn_row(t, w):
                r = head_rows(w)
                rope(r[:, :, 64:80], r[:, :, 80:96], over(ci[:, t, :], 1, HEADS), over(si[:, t, :], 1, HEADS), brot
                     ).then_inc(qb_rdy, 1)
                D_()

            def latent_piece(u):
                t, step = u // 8, u % 8
                r = head_rows(0)
                if step == 1:
                    sum_squares(t, 0)
                if step == 2:
                    get_rsqrt()
                    v.tensor_tensor(r, r, over(mu[:, 0:8], 2, DQ_B), ALU.mult)
                    D_()
                if step == 3:
                    sum_squares(t, 1)
                    v.tensor_tensor(r, r, over(M["bq"], 1, HEADS), ALU.mult)
                    D_()
                if step == 4:
                    turn_row(t, 0)
                if step == 7:
                    get_rsqrt()
                    turn_row(t, 1)

            def at_mask(u):
                att, t = u // 32, u // 8 % 4
                w = P * (t + 1)
                dve.wait_ge(at_done, u + 1)
                if u >= 3:
                    dve.wait_ge(pT2_done, u - 2)
                bias = selbias[:, t, 0:w] if att == 0 else C["chunkbias"][:, S - w:S]
                v.tensor_tensor_reduce(sS[u % 3][:, 0:w], bank[(0, 1, 5)[u % 3]][:, 0:w], bias, -float((DH, DQ_B)[att]) ** -0.5, 3e38,
                                       ALU.add, ALU.min, nmax[:, u % 4:u % 4 + 1])
                dve.drain().then_inc(at_s, 1)

            def at_out(g):
                att, t = g // 4, g % 4
                dve.wait_ge(pv_done, 8 * (g + 1))
                r = rs_all[:, 8 * (g % 2):8 * (g % 2) + 8]
                v.reciprocal(var[:, 0:8], r)
                D_()
                c = (C_QA, C_CQ)[att]
                v.tensor_tensor(pr2[:, t, c:c + 512].rearrange("p (a n) -> p a n", a=HEADS),
                                bank[4][:, :].rearrange("p (a n) -> p a n", a=HEADS),
                                over(var[:, 0:8], 2, DH), ALU.mult).then_inc(o_ev, 1)
                D_()
                dve.wait_ge(silu_rdy, g + 1)
                v.tensor_tensor(pr2[:, t, c:c + 512], pr2[:, t, c:c + 512], out_gate(g), ALU.mult).then_inc(mixed, 1)

            for u in range(64):
                at_mask(u)
                if u % 8 == 2 and u > 8:
                    at_out(u // 8 - 1)
                if u < 32:
                    latent_piece(u)
                if u < 24:
                    n = 6 * (u // 8) + (0, 2, 3, 3, 3, 3, 3, 4)[u % 8] + 2 * (KEEP // 8)
                    keep_keys(range(n, min(n + (2, 1, 0, 0, 0, 0, 1, 2)[u % 8], NT * (KEEP // 8) - KEEP // 8)))
            at_out(7)
            rest_dense(68)
            rest_dense(69)
            rests(B_OUT, 0)
            for m in range(70, 76):
                rest_dense(m)
            dve.wait_ge(h_ld, 16)
            for g in range(8):
                n, t = g // 4, g % 4
                hv = h[:, t, n * 512:(n + 1) * 512]
                dve.wait_ge(dense_done, result_done(dense_no(L_OUT2 + n), t))
                v.tensor_tensor(hv, hv, bank[4 * (1 - n) + t][:, :], ALU.add).then_inc(out_rdy, 1)

        @block.gpsimd
        def _(pool):
            g_ = nc.gpsimd
            D_ = pool.drain
            done, means = [0], [0]

            def rsqrt_mean(out, sums, n, eps):
                done[0] += 1
                pool.wait_ge(sums_rdy, done[0])
                g_.tensor_scalar(out, sums, 1.0 / n, eps, ALU.mult, ALU.add).then_inc(mean_rdy, 1)
                means[0] += 1
                pool.wait_ge(mean_rdy, means[0])
                g_.tensor_tensor(out, out, minus_half[:, 0:out.shape[1]], ALU.pow).then_inc(rstd_rdy, 1)

            g_.memset(idx_all, 0).then_inc(place_zero, 1)
            pool.wait_ge(place_zero, 1)
            pool.dma_start(place_dram.rearrange("(p i) o -> p (i o)", p=P), idx_all).then_inc(zero_st, 16)
            g_.memset(minus_half, -0.5)
            g_.memset(uT[:, :, 0:PAD], 0.0)
            g_.memset(yzero, 0.0)
            g_.memset(win[0][:, 0:PAD], 0.0)
            g_.memset(win[1][:, 0:PAD], 0.0)
            D_().then_inc(pad_zero, 1)
            def rsqrt_tiles(eps):
                for t in range(NT):
                    rsqrt_mean(rstd[:, t:t + 1], sumsq[:, t:t + 1], D, eps)

            rsqrt_tiles(EPS1)
            pool.wait_ge(proj_ev, 12)
            pool.dma_start(y_dram[E * P:, :].rearrange("(i p) n -> p i n", p=P),
                           yzero.unsqueeze(1).to_broadcast([P, NITEM - E, D])).then_inc(yzero_st, 16)
            pool.wait_ge(cst_ld, 16)
            iw = C["invw"].rearrange("p (g n) -> p g n", g=4)
            for g, w in enumerate(WINDOWS):
                src, step, at = uT[:, g, :], 1, 0
                while step < w:
                    g_.tensor_tensor(win[at][:, PAD:], src[:, PAD:], src[:, PAD - step:PAD + S - step], ALU.add)
                    D_()
                    src, step, at = win[at], 2 * step, 1 - at
                mean = win[at]
                g_.tensor_scalar(mean[:, PAD:], src[:, PAD:], 1.0 / w, None, ALU.mult)
                D_()
                g_.tensor_tensor(mean[:, PAD:2 * PAD], src[:, PAD:2 * PAD], iw[:, g, :], ALU.mult)
                D_()
                g_.tensor_tensor(uT[:, g, PAD:], mean[:, PAD:], uT[:, g, PAD:], ALU.subtract).then_inc(pooled, 1)
                D_()
            for t in range(NT):
                rsqrt_mean(var[:, t * 8:(t + 1) * 8], var[:, t * 8:(t + 1) * 8], DH, EPS1)
            rsqrt_tiles(EPS1)
            pool.wait_ge(zero_st, 16)
            pool.wait_ge(place_rdy, 1)
            for a in range(16):
                pool.indirect_dma_start(out=place_dram[:, :], out_offset=bass.IndirectOffsetOnAxis(ap=place_u[:, a:a + 1], axis=0),
                                        in_=tok_i[:, a // 4:a // 4 + 1], in_offset=None).then_inc(place_st, 16)
            pool.wait_ge(place_st, 16 * 16)
            pool.dma_start(idx_all, place_dram.rearrange("(p i) o -> p (i o)", p=P)).then_inc(idx_ld, 16)
            pool.wait_ge(idx_ld, 16)
            pool.wait_ge(rows_st, 16)
            pool.wait_ge(gT_ev, 1)
            pool.wait_ge(bd_done, 8)

            def gather(i):
                g_.tensor_copy(idx_cur, idx_all[:, ds(i, 1)])
                D_()
                pool.indirect_dma_start(out=xg, out_offset=None, in_=xn_dram[:, :],
                                        in_offset=bass.IndirectOffsetOnAxis(ap=idx_cur.bitcast(U32), axis=0)
                                        ).then_inc(xg_ld, 16)

            last = pool.value_load(last_item[0:1, 0:1], min_val=E - 1, max_val=NITEM - 2)
            gather(0)
            with pool.Fori(1, last + 2) as i:
                pool.wait_ge(xgT_done, i)
                pool.wait_ge(xg_ld, 16 * i)
                gather(i)
            pool.wait_ge(y_all, 1)
            for a in range(16):
                pool.indirect_dma_start(out=ygat[:, a, :], out_offset=None, in_=y_dram[:, :],
                                        in_offset=bass.IndirectOffsetOnAxis(ap=slot_u[:, a:a + 1], axis=0)
                                        ).then_inc(yg_ld[a // 4], 16)
            for eps in (EPS1, EPS1, EPS2):
                rsqrt_tiles(eps)
            rsqrt_mean(mu, mu, DH, EPS2)
            done[0] += 1
            pool.wait_ge(sums_rdy, done[0])
            g_.tensor_scalar(mu, mu, 1.0 / DH, EPS2, ALU.mult, ALU.add)
            D_()
            g_.tensor_tensor(mu, mu, minus_half, ALU.pow)
            D_()
            ka = pr2[:, :, C_KA:C_KA + 512].rearrange("p t (a f) -> p t a f", a=HEADS)
            g_.tensor_tensor(ka, ka, mu.rearrange("p (t a) -> p t a", t=NT).unsqueeze(3).to_broadcast([P, NT, HEADS, DH]), ALU.mult)
            D_()
            for t in range(NT):
                ins = g_.tensor_tensor(ka[:, t], ka[:, t], M["ak"].unsqueeze(1).to_broadcast([P, HEADS, DH]), ALU.mult)
            ins.then_inc(rstd_rdy, 1)
            for j, n in enumerate((Q_LORA, KV_LORA)):
                rsqrt_mean(lat_sum[:, j * NT:(j + 1) * NT], lat_sum[:, j * NT:(j + 1) * NT], n, EPS2)
            silus = [(0, 1, 2), (3,), (4, 5), (6, 7)]
            for t in range(NT):
                rsqrt_mean(mu[:, 0:8], mu[:, 0:8], DQ_B, EPS2)
                for g in silus[t]:
                    pool.wait_ge(gate_sg, g + 1)
                    g_.tensor_tensor(out_gate(g), out_gate(g), out_sig[:, g, :], ALU.mult).then_inc(silu_rdy, 1)
                done[0] += 1
                pool.wait_ge(sums_rdy, done[0])
                r, k_sum = krow.rearrange("p (a n) -> p a n", a=HEADS), mu[:, 8:16]
                g_.tensor_scalar(k_sum, k_sum, 1.0 / DQ_B, EPS2, ALU.mult, ALU.add)
                D_()
                g_.tensor_tensor(k_sum, k_sum, minus_half[:, 0:8], ALU.pow)
                D_()
                g_.tensor_tensor(r, r, k_sum.unsqueeze(2).to_broadcast([P, HEADS, DQ_B]), ALU.mult)
                D_()
                g_.tensor_tensor(r, r, M["bk"].unsqueeze(1).to_broadcast([P, HEADS, DQ_B]), ALU.mult).then_inc(rstd_rdy, 1)


INPUTS = ("x", "p", "positions", "w_in", "w_out", "pool_w", "norm_moe_w", "router_w", "expert_w_gate_up",
          "expert_b_gate_up", "expert_w_down", "expert_b_down", "ple_gate_w", "ple_proj_w", "final_norm_w",
          "w_in_2", "w_uq_2", "w_ukv_2", "w_out_2", "small", "constants")


def kernel(**inputs):
    import concourse.bacc as bacc
    from concourse.bass_utils import run_bass_kernel_spmd

    a = {k: np.asarray(v) for k, v in inputs.items()}

    def cols(v):
        return v.reshape(-1, P).T

    def rows(v):
        return np.broadcast_to(v.reshape(1, -1), (P, v.size))

    small = {"g_mix": cols(a["norm_mix_w"]), "gn_w": cols(a["ret_gn_w"]), "pool_scale": cols(a["pool_scale"]),
             "g_ple": cols(a["norm_ple_w"]), "gain2": cols(a["norm_gain_2"]), "bq_lat": cols(a["b_q_latent_norm_2"]),
             "bkv_lat": cols(a["b_kv_latent_norm_2"]), "router_b": rows(a["router_b"]), "aq": rows(a["a_q_norm_2"]),
             "ak": rows(a["a_k_norm_2"]), "bq": rows(a["b_q_norm_2"]), "bk": rows(a["b_k_norm_2"])}
    one = {k: a[k][0] for k in ("x", "p", "w_in", "w_out", "pool_w", "router_w", "expert_w_gate_up", "expert_b_gate_up",
                                "expert_w_down", "expert_b_down", "ple_gate_w", "ple_proj_w", "w_in_2", "w_uq_2",
                                "w_ukv_2", "w_out_2")}
    one["p"] = one["p"].reshape(S, PLE)
    one["positions"] = a["positions"].reshape(NT, P).T
    one["norm_moe_w"] = a["norm_moe_w"].reshape(D)
    one["final_norm_w"] = a["final_norm_w"]
    one["small"] = np.concatenate([small[k] for k in SMALL.at], axis=1)
    one["constants"] = shape_constants()

    nc = bacc.Bacc("TRN2", target_bir_lowering=False, num_devices=1)
    arrays, args = {}, {}
    for name in INPUTS:
        v = np.ascontiguousarray(one[name])
        arrays["in_" + name] = v
        args[name] = nc.dram_tensor("in_" + name, v.shape, mybir.dt.from_np(v.dtype), kind="ExternalInput").ap()
    args["out"] = nc.dram_tensor("out_rows", (S, D), F32, kind="ExternalOutput").ap()
    build_program(nc, args)
    r = run_bass_kernel_spmd(nc, [arrays], core_ids=[0])
    return r.results[0]["out_rows"].reshape(1, S, D)
```
